# Optimizing a Trainium2 kernel written in Bass

```python
import jax, jax.numpy as jnp
from jax import lax
import numpy as np
import math

D_MODEL = 1024
BATCH = 1
SEQ = 512
DEPTH = 1

D_MIX = D_MODEL
D_LRU = D_MIX // 2
D_CONV = D_MIX - D_LRU
LRU_HEADS = 8
LRU_HEAD_DIM = D_LRU // LRU_HEADS
LRU_CONV_WIDTH = 4
LRU_C = 8.0
LRU_A_MIN = 0.9
LRU_A_MAX = 0.999
CONV_GROUPS = 8
CONV_GROUP_DIM = D_CONV // CONV_GROUPS
CONF_KERNEL = 31
PEER_HEADS = 8
PEER_N_KEYS = 128
PEER_N_EXPERTS = PEER_N_KEYS ** 2
PEER_D_QUERY = 256
PEER_HALF = PEER_D_QUERY // 2
PEER_TOPK = 16
PEER_BLOCK = 128
EPS = 1e-6


def rms_norm(x, g):
    xf = x.astype(jnp.float32)
    y = xf * lax.rsqrt(jnp.mean(xf * xf, axis=-1, keepdims=True) + EPS)
    return (y * g.astype(jnp.float32)).astype(x.dtype)

def group_layer_norm(x, g, b):
    B_, S_, C = x.shape
    xg = x.astype(jnp.float32).reshape(B_, S_, CONV_GROUPS, CONV_GROUP_DIM)
    mu = jnp.mean(xg, axis=-1, keepdims=True)
    var = jnp.mean(jnp.square(xg - mu), axis=-1, keepdims=True)
    y = ((xg - mu) * lax.rsqrt(var + EPS)).reshape(B_, S_, C)
    return (y * g.astype(jnp.float32) + b.astype(jnp.float32)).astype(x.dtype)

def depthwise_conv(x, w, b, pad):
    C = x.shape[-1]
    y = lax.conv_general_dilated(
        x, w[:, None, :].astype(x.dtype), window_strides=(1,), padding=[pad],
        dimension_numbers=("NWC", "WIO", "NWC"), feature_group_count=C)
    return y + b.astype(x.dtype)

def block_diag_linear(x, w, b):
    B_, S_, _ = x.shape
    xh = x.reshape(B_, S_, LRU_HEADS, LRU_HEAD_DIM)
    y = jnp.einsum("bshi,hij->bshj", xh, w.astype(jnp.float32))
    return y.reshape(B_, S_, D_LRU) + b.astype(jnp.float32)

def _linear_recurrence(left, right):
    a_l, b_l = left
    a_r, b_r = right
    return a_l * a_r, a_r * b_l + b_r

def rg_lru(x, w_r, b_r, w_i, b_i, lam, reverse):
    xf = x.astype(jnp.float32)
    r = jax.nn.sigmoid(block_diag_linear(xf, w_r, b_r))
    i = jax.nn.sigmoid(block_diag_linear(xf, w_i, b_i))
    log_a = LRU_C * r * jax.nn.log_sigmoid(lam.astype(jnp.float32))
    a = jnp.exp(log_a)
    u = jnp.sqrt(-jnp.expm1(2.0 * log_a)) * (i * xf)
    _, h = lax.associative_scan(_linear_recurrence, (a, u), reverse=reverse, axis=1)
    return h

def hybrid_mixer(n, w_in, lru_conv_w, lru_conv_b, lru_w_rg, lru_b_rg, lru_w_ig, lru_b_ig,
                 lru_lambda, conf_conv_w, conf_conv_b, conf_norm_g, conf_norm_b,
                 beta_lru, beta_conv, w_out):
    z = jnp.einsum("bsd,de->bse", n, w_in.astype(n.dtype))
    x_lru, g_lru, a_glu, b_glu = jnp.split(
        z, [D_LRU, 2 * D_LRU, 2 * D_LRU + D_CONV], axis=-1)

    lpad = LRU_CONV_WIDTH // 2
    xc = depthwise_conv(x_lru, lru_conv_w, lru_conv_b, (lpad, LRU_CONV_WIDTH - 1 - lpad))
    h_fwd = rg_lru(xc, lru_w_rg[0], lru_b_rg[0], lru_w_ig[0], lru_b_ig[0], lru_lambda[0], False)
    h_bwd = rg_lru(xc, lru_w_rg[1], lru_b_rg[1], lru_w_ig[1], lru_b_ig[1], lru_lambda[1], True)
    y_lru = ((h_fwd + h_bwd) * jax.nn.gelu(g_lru.astype(jnp.float32))).astype(n.dtype)

    glu = a_glu * jax.nn.sigmoid(b_glu)
    c = depthwise_conv(glu, conf_conv_w, conf_conv_b, (CONF_KERNEL // 2, CONF_KERNEL // 2))
    y_conv = jax.nn.silu(group_layer_norm(c, conf_norm_g, conf_norm_b))

    y = jnp.concatenate([rms_norm(y_lru, beta_lru), rms_norm(y_conv, beta_conv)], axis=-1)
    return jnp.einsum("bse,ed->bsd", y, w_out.astype(y.dtype))

def peer_ffn(n, w_q, sub_keys, expert_u, expert_v):
    B_, S_, D = n.shape
    n_blocks = (B_ * S_) // PEER_BLOCK
    xb = n.reshape(n_blocks, PEER_BLOCK, D)

    def retrieve(xt):
        q = jnp.einsum("td,de->te", xt, w_q.astype(xt.dtype))
        q = q.reshape(PEER_BLOCK, PEER_HEADS, 2, PEER_HALF).astype(jnp.float32)
        s = jnp.einsum("thpc,hpkc->thpk", q, sub_keys.astype(jnp.float32))
        s1, i1 = lax.top_k(s[:, :, 0], PEER_TOPK)
        s2, i2 = lax.top_k(s[:, :, 1], PEER_TOPK)
        cand_s = (s1[..., :, None] + s2[..., None, :]).reshape(PEER_BLOCK, PEER_HEADS, PEER_TOPK * PEER_TOPK)
        cand_i = (i1[..., :, None] * PEER_N_KEYS + i2[..., None, :]).reshape(PEER_BLOCK, PEER_HEADS, PEER_TOPK * PEER_TOPK)
        top_s, pos = lax.top_k(cand_s, PEER_TOPK)
        idx = jnp.take_along_axis(cand_i, pos, axis=-1)
        gate = jax.nn.softmax(top_s, axis=-1)
        u = expert_u[idx]
        v = expert_v[idx]
        act = jax.nn.gelu(jnp.einsum("thkd,td->thk", u, xt))
        return jnp.einsum("thk,thkd->td", (gate * act).astype(v.dtype), v)

    out = lax.map(retrieve, xb)
    return out.reshape(B_, S_, D).astype(n.dtype)

def first_inputs(seed: int = 0) -> dict:
    key = jax.random.key(seed)
    ks = jax.random.split(key, 24)
    L = DEPTH
    nrm = lambda k, shape, scale: jax.random.normal(k, shape, jnp.float32) * scale
    gain = lambda k, shape: 1.0 + 0.02 * jax.random.normal(k, shape, jnp.float32)
    a0 = jax.random.uniform(ks[9], (L, 2, D_LRU), jnp.float32, LRU_A_MIN, LRU_A_MAX)
    p = a0 ** (1.0 / LRU_C)
    lru_lambda = jnp.log(p) - jnp.log1p(-p)
    return {
        "x": nrm(ks[0], (BATCH, SEQ, D_MODEL), 1.0),
        "mix_norm_g": gain(ks[1], (L, D_MODEL)),
        "w_in": nrm(ks[2], (L, D_MODEL, 2 * D_LRU + 2 * D_CONV), D_MODEL ** -0.5),
        "lru_conv_w": nrm(ks[3], (L, LRU_CONV_WIDTH, D_LRU), LRU_CONV_WIDTH ** -0.5),
        "lru_conv_b": nrm(ks[4], (L, D_LRU), 0.02),
        "lru_w_rg": nrm(ks[5], (L, 2, LRU_HEADS, LRU_HEAD_DIM, LRU_HEAD_DIM), LRU_HEAD_DIM ** -0.5),
        "lru_b_rg": nrm(ks[6], (L, 2, D_LRU), 0.02),
        "lru_w_ig": nrm(ks[7], (L, 2, LRU_HEADS, LRU_HEAD_DIM, LRU_HEAD_DIM), LRU_HEAD_DIM ** -0.5),
        "lru_b_ig": nrm(ks[8], (L, 2, D_LRU), 0.02),
        "lru_lambda": lru_lambda,
        "conf_conv_w": nrm(ks[10], (L, CONF_KERNEL, D_CONV), CONF_KERNEL ** -0.5),
        "conf_conv_b": nrm(ks[11], (L, D_CONV), 0.02),
        "conf_norm_g": gain(ks[12], (L, D_CONV)),
        "conf_norm_b": nrm(ks[13], (L, D_CONV), 0.02),
        "beta_lru": gain(ks[14], (L, D_LRU)),
        "beta_conv": gain(ks[15], (L, D_CONV)),
        "w_out": nrm(ks[16], (L, D_MIX, D_MODEL), D_MIX ** -0.5),
        "ffn_norm_g": gain(ks[17], (L, D_MODEL)),
        "peer_w_q": nrm(ks[18], (L, D_MODEL, PEER_HEADS * PEER_D_QUERY), D_MODEL ** -0.5),
        "peer_sub_keys": nrm(ks[19], (L, PEER_HEADS, 2, PEER_N_KEYS, PEER_HALF), PEER_HALF ** -0.5),
        "peer_u": nrm(ks[20], (L, PEER_N_EXPERTS, D_MODEL), D_MODEL ** -0.5),
        "peer_v": nrm(ks[21], (L, PEER_N_EXPERTS, D_MODEL), PEER_HEADS ** -0.5),
        "final_norm_g": gain(ks[22], (D_MODEL,)),
    }

def first_block(x, mix_norm_g, w_in, lru_conv_w, lru_conv_b, lru_w_rg, lru_b_rg, lru_w_ig,
              lru_b_ig, lru_lambda, conf_conv_w, conf_conv_b, conf_norm_g, conf_norm_b,
              beta_lru, beta_conv, w_out, ffn_norm_g, peer_w_q, peer_sub_keys, peer_u,
              peer_v, final_norm_g):
    h = x
    for l in range(DEPTH):
        h = h + hybrid_mixer(
            rms_norm(h, mix_norm_g[l]), w_in[l], lru_conv_w[l], lru_conv_b[l],
            lru_w_rg[l], lru_b_rg[l], lru_w_ig[l], lru_b_ig[l], lru_lambda[l],
            conf_conv_w[l], conf_conv_b[l], conf_norm_g[l], conf_norm_b[l],
            beta_lru[l], beta_conv[l], w_out[l])
        h = h + peer_ffn(rms_norm(h, ffn_norm_g[l]), peer_w_q[l], peer_sub_keys[l],
                         peer_u[l], peer_v[l])
    return rms_norm(h, final_norm_g)


DEPTH_2 = 2

N_A_LAYERS = DEPTH_2 // 2
N_B_LAYERS = DEPTH_2 - N_A_LAYERS
MEM_TOKENS = 256
D_FF = 2816
HEAD_DIM = 64
MEM_HEADS = 4
MEM_WIDTH = MEM_HEADS * HEAD_DIM
MLSTM_HEADS = 4
MLSTM_HEAD_DIM = 192
MLSTM_WIDTH = MLSTM_HEADS * MLSTM_HEAD_DIM
MLSTM_CHUNK = 128
CONV_WIDTH = 4
DILATED_GROUPS = ((128, 1), (512, 4), (2048, 16))
HEADS_PER_GROUP = 4
N_DIL_HEADS = HEADS_PER_GROUP * len(DILATED_GROUPS)
DIL_WIDTH = N_DIL_HEADS * HEAD_DIM
A_IN_WIDTH = 4 * MLSTM_WIDTH + 2 * MLSTM_HEADS + MEM_WIDTH
B_IN_WIDTH = DIL_WIDTH + MEM_WIDTH
NUM_BUCKETS = 32
MAX_DISTANCE = 2048
RMS_EPS = 1e-6
NEG_INF = -1e30
ATTN_SCALE = HEAD_DIM ** -0.5


def rms_norm_2(x, gain):
    xf = x.astype(jnp.float32)
    y = xf * lax.rsqrt(jnp.mean(xf * xf, axis=-1, keepdims=True) + RMS_EPS)
    return (y * gain.astype(jnp.float32)).astype(x.dtype)

def swiglu(h, w_gate, w_up, w_down):
    return (jax.nn.silu(h @ w_gate) * (h @ w_up)) @ w_down

def causal_conv(x, w):
    C = x.shape[-1]
    return lax.conv_general_dilated(x, w[:, None, :].astype(x.dtype), window_strides=(1,),
                                    padding=[(w.shape[0] - 1, 0)],
                                    dimension_numbers=('NWC', 'WIO', 'NWC'),
                                    feature_group_count=C)

def t5_causal_bucket(dist):
    max_exact = NUM_BUCKETS // 2
    d_f = jnp.maximum(dist, 1).astype(jnp.float32)
    large = max_exact + (jnp.log(d_f / max_exact) / math.log(MAX_DISTANCE / max_exact)
                         * (NUM_BUCKETS - max_exact)).astype(jnp.int32)
    large = jnp.minimum(large, NUM_BUCKETS - 1)
    return jnp.where(dist < max_exact, dist, large)

def mlstm_chunkwise(q, k, v, i_pre, f_pre):
    B, S, H, DK = q.shape
    DV = v.shape[-1]
    L = MLSTM_CHUNK
    NC = S // L
    f32 = jnp.float32

    def chunks(t):
        t = t.astype(f32).reshape(B, NC, L, H, *t.shape[3:])
        return jnp.moveaxis(t, 3, 2)

    qc = chunks(q)
    kc = chunks(k) * (DK ** -0.5)
    vc = chunks(v)
    ic = chunks(i_pre)
    logf = jax.nn.log_sigmoid(chunks(f_pre))
    b = jnp.cumsum(logf, axis=-1)
    b_last = b[..., -1]
    a = b_last[..., None] - b + ic

    def step(carry, xs):
        C, n, m = carry
        k_j, v_j, a_j, bl_j = xs
        m_new = jnp.maximum(bl_j + m, jnp.max(a_j, axis=-1))
        w = jnp.exp(a_j - m_new[..., None])
        decay = jnp.exp(bl_j + m - m_new)
        C_new = decay[..., None, None] * C + jnp.einsum('bhl,bhlk,bhlv->bhkv', w, k_j, v_j)
        n_new = decay[..., None] * n + jnp.einsum('bhl,bhlk->bhk', w, k_j)
        return (C_new, n_new, m_new), (C, n, m)

    init = (jnp.zeros((B, H, DK, DV), f32), jnp.zeros((B, H, DK), f32), jnp.zeros((B, H), f32))
    xs = (jnp.moveaxis(kc, 1, 0), jnp.moveaxis(vc, 1, 0), jnp.moveaxis(a, 1, 0), jnp.moveaxis(b_last, 1, 0))
    _, (C0, n0, m0) = lax.scan(step, init, xs)
    C0 = jnp.moveaxis(C0, 0, 1)
    n0 = jnp.moveaxis(n0, 0, 1)
    m0 = jnp.moveaxis(m0, 0, 1)

    causal = jnp.tril(jnp.ones((L, L), dtype=bool))
    Dlog = jnp.where(causal, b[..., :, None] - b[..., None, :] + ic[..., None, :], NEG_INF)
    g = b + m0[..., None]
    m_t = jnp.maximum(g, jnp.max(Dlog, axis=-1))
    W = jnp.exp(Dlog - m_t[..., None]) * jnp.einsum('bchtk,bchsk->bchts', qc, kc)
    inter = jnp.exp(g - m_t)
    num = jnp.einsum('bchts,bchsv->bchtv', W, vc) + inter[..., None] * jnp.einsum('bchtk,bchkv->bchtv', qc, C0)
    den = jnp.sum(W, axis=-1) + inter * jnp.einsum('bchtk,bchk->bcht', qc, n0)
    h = num / jnp.maximum(jnp.abs(den), jnp.exp(-m_t))[..., None]
    return jnp.moveaxis(h, 2, 3).reshape(B, S, H, DV)

def dilated_group_attention(q, k, v, bias_table, window, dilation):
    B, S, H, E = q.shape
    blk = window // dilation
    span = window
    Lp = -(-S // span) * span
    nb = Lp // span
    pad = ((0, 0), (0, Lp - S), (0, 0), (0, 0))

    def to_blocks(t):
        t = jnp.pad(t.astype(jnp.float32), pad).reshape(B, Lp // dilation, dilation, H, E)
        return jnp.transpose(t, (0, 2, 1, 3, 4)).reshape(B, dilation, nb, blk, H, E)

    qb = to_blocks(q)
    kb = to_blocks(k)
    vb = to_blocks(v)
    prev = lambda t: jnp.pad(t, ((0, 0), (0, 0), (1, 0), (0, 0), (0, 0), (0, 0)))[:, :, :-1]
    kk = jnp.concatenate([prev(kb), kb], axis=3)
    vv = jnp.concatenate([prev(vb), vb], axis=3)

    qi = jnp.arange(blk)[:, None]
    kj = jnp.arange(2 * blk)[None, :]
    m_off = qi + blk - kj
    band = (m_off >= 0) & (m_off <= blk)
    bucket = t5_causal_bucket(jnp.clip(m_off, 0, blk) * dilation)
    bias = jnp.transpose(bias_table.astype(jnp.float32)[bucket], (2, 0, 1))
    n_idx = jnp.arange(nb)[:, None, None]
    allowed = band[None] & ~((n_idx == 0) & (kj[None] < blk))

    s = jnp.einsum('brnqhe,brnkhe->brnhqk', qb, kk) * ATTN_SCALE + bias
    s = jnp.where(allowed[:, None], s, NEG_INF)
    mx = jnp.max(s, axis=-1, keepdims=True)
    p = jnp.exp(s - mx)
    den = jnp.sum(p, axis=-1)
    out = jnp.einsum('brnhqk,brnkhe->brnqhe', p, vv) / jnp.moveaxis(den, 3, 4)[..., None]
    lse = mx[..., 0] + jnp.log(den)

    out = jnp.transpose(out.reshape(B, dilation, Lp // dilation, H, E), (0, 2, 1, 3, 4)).reshape(B, Lp, H, E)[:, :S]
    lse = jnp.moveaxis(lse, 3, 4).reshape(B, dilation, Lp // dilation, H)
    lse = jnp.transpose(lse, (0, 2, 1, 3)).reshape(B, Lp, H)[:, :S]
    return out, lse

def memory_cross_attention(q_mem, mem_n, w_mem_kv, q_gain, k_gain):
    B, S, _ = q_mem.shape
    M = mem_n.shape[1]
    q = rms_norm_2(q_mem.reshape(B, S, MEM_HEADS, HEAD_DIM), q_gain)
    kv = mem_n @ w_mem_kv
    k = rms_norm_2(kv[..., :MEM_WIDTH].reshape(B, M, MEM_HEADS, HEAD_DIM), k_gain)
    v = kv[..., MEM_WIDTH:].reshape(B, M, MEM_HEADS, HEAD_DIM)
    s = jnp.einsum('bshe,bmhe->bhsm', q.astype(jnp.float32), k.astype(jnp.float32)) * ATTN_SCALE
    p = jax.nn.softmax(s, axis=-1)
    out = jnp.einsum('bhsm,bmhe->bshe', p, v.astype(jnp.float32))
    return out.reshape(B, S, MEM_WIDTH).astype(q_mem.dtype)

def mlstm_mixer(h, mem_n, w_in, conv_w, gate_bias, h_gain, w_out, w_mem_kv, mq_gain, mk_gain):
    B, S, _ = h.shape
    W = MLSTM_WIDTH
    p = h @ w_in
    qk = jax.nn.silu(causal_conv(p[..., :2 * W], conv_w))
    v = p[..., 2 * W:3 * W]
    o = p[..., 3 * W:4 * W]
    gates = p[..., 4 * W:4 * W + 2 * MLSTM_HEADS].astype(jnp.float32) + gate_bias.astype(jnp.float32)
    q_mem = p[..., 4 * W + 2 * MLSTM_HEADS:]
    heads = lambda t: t.reshape(B, S, MLSTM_HEADS, MLSTM_HEAD_DIM)
    cell = mlstm_chunkwise(heads(qk[..., :W]), heads(qk[..., W:]), heads(v),
                           gates[..., :MLSTM_HEADS], gates[..., MLSTM_HEADS:])
    cell = rms_norm_2(cell, h_gain).reshape(B, S, W)
    h_a = (jax.nn.sigmoid(o.astype(jnp.float32)) * cell).astype(h.dtype)
    h_m = memory_cross_attention(q_mem, mem_n, w_mem_kv, mq_gain, mk_gain)
    return jnp.concatenate([h_a, h_m], axis=-1) @ w_out

def dilated_mixer(h, mem_n, k_sh, v_sh, w_q, q_gain, w_out, rel_bias, w_mem_kv, mq_gain, mk_gain):
    B, S, _ = h.shape
    p = h @ w_q
    q_d = rms_norm_2(p[..., :DIL_WIDTH].reshape(B, S, len(DILATED_GROUPS), HEADS_PER_GROUP, HEAD_DIM), q_gain)
    outs, lses = [], []
    for g, (window, dilation) in enumerate(DILATED_GROUPS):
        table = rel_bias[:, g * HEADS_PER_GROUP:(g + 1) * HEADS_PER_GROUP]
        o_g, l_g = dilated_group_attention(q_d[:, :, g], k_sh[:, :, g], v_sh[:, :, g], table, window, dilation)
        outs.append(o_g)
        lses.append(l_g)
    outs = jnp.stack(outs, axis=2)
    alpha = jax.nn.softmax(jnp.stack(lses, axis=2), axis=2)
    h_d = (outs * alpha[..., None]).reshape(B, S, DIL_WIDTH).astype(h.dtype)
    h_m = memory_cross_attention(p[..., DIL_WIDTH:], mem_n, w_mem_kv, mq_gain, mk_gain)
    return jnp.concatenate([h_d, h_m], axis=-1) @ w_out

def second_inputs(seed: int = 0) -> dict:
    key = jax.random.key(seed)
    ks = iter(jax.random.split(key, 40))
    nrm = lambda shape, scale: jax.random.normal(next(ks), shape, jnp.float32) * scale
    gain = lambda shape: 1.0 + nrm(shape, 0.02)
    D, F = D_MODEL, D_FF
    return {
        'x': nrm((BATCH, SEQ, D), 1.0),
        'mem': nrm((BATCH, MEM_TOKENS, D), 1.0),
        'ffn1_norm': gain((DEPTH_2, D)),
        'ffn1_w_gate': nrm((DEPTH_2, D, F), D ** -0.5),
        'ffn1_w_up': nrm((DEPTH_2, D, F), D ** -0.5),
        'ffn1_w_down': nrm((DEPTH_2, F, D), F ** -0.5),
        'ffn2_norm': gain((DEPTH_2, D)),
        'ffn2_w_gate': nrm((DEPTH_2, D, F), D ** -0.5),
        'ffn2_w_up': nrm((DEPTH_2, D, F), D ** -0.5),
        'ffn2_w_down': nrm((DEPTH_2, F, D), F ** -0.5),
        'mix_norm': gain((DEPTH_2, D)),
        'mem_norm': gain((DEPTH_2, D)),
        'w_mem_kv': nrm((DEPTH_2, D, 2 * MEM_WIDTH), D ** -0.5),
        'mem_q_norm': gain((DEPTH_2, HEAD_DIM)),
        'mem_k_norm': gain((DEPTH_2, HEAD_DIM)),
        'a_w_in': nrm((N_A_LAYERS, D, A_IN_WIDTH), D ** -0.5),
        'a_conv': nrm((N_A_LAYERS, CONV_WIDTH, 2 * MLSTM_WIDTH), CONV_WIDTH ** -0.5),
        'a_gate_bias': jnp.concatenate([nrm((N_A_LAYERS, MLSTM_HEADS), 0.1),
                                        3.0 + nrm((N_A_LAYERS, MLSTM_HEADS), 0.5)], axis=-1),
        'a_h_norm': gain((N_A_LAYERS, MLSTM_HEADS, MLSTM_HEAD_DIM)),
        'a_w_out': nrm((N_A_LAYERS, MLSTM_WIDTH + MEM_WIDTH, D), (MLSTM_WIDTH + MEM_WIDTH) ** -0.5),
        'b_w_q': nrm((N_B_LAYERS, D, B_IN_WIDTH), D ** -0.5),
        'b_q_norm': gain((N_B_LAYERS, HEAD_DIM)),
        'b_w_out': nrm((N_B_LAYERS, DIL_WIDTH + MEM_WIDTH, D), (DIL_WIDTH + MEM_WIDTH) ** -0.5),
        'kv_norm': gain((D,)),
        'w_kv': nrm((D, 2 * DIL_WIDTH), D ** -0.5),
        'kv_k_norm': gain((HEAD_DIM,)),
        'rel_bias': nrm((NUM_BUCKETS, N_DIL_HEADS), 0.3),
    }

def second_block(x, mem, ffn1_norm, ffn1_w_gate, ffn1_w_up, ffn1_w_down,
              ffn2_norm, ffn2_w_gate, ffn2_w_up, ffn2_w_down,
              mix_norm, mem_norm, w_mem_kv, mem_q_norm, mem_k_norm,
              a_w_in, a_conv, a_gate_bias, a_h_norm, a_w_out,
              b_w_q, b_q_norm, b_w_out, kv_norm, w_kv, kv_k_norm, rel_bias):
    B, S, _ = x.shape
    n_groups = len(DILATED_GROUPS)
    k_sh = None
    v_sh = None
    for layer in range(DEPTH_2):
        x = x + 0.5 * swiglu(rms_norm_2(x, ffn1_norm[layer]), ffn1_w_gate[layer], ffn1_w_up[layer], ffn1_w_down[layer])
        h = rms_norm_2(x, mix_norm[layer])
        mem_n = rms_norm_2(mem, mem_norm[layer])
        if layer < N_A_LAYERS:
            ia = layer
            mix = mlstm_mixer(h, mem_n, a_w_in[ia], a_conv[ia], a_gate_bias[ia], a_h_norm[ia], a_w_out[ia],
                              w_mem_kv[layer], mem_q_norm[layer], mem_k_norm[layer])
        else:
            ib = layer - N_A_LAYERS
            mix = dilated_mixer(h, mem_n, k_sh, v_sh, b_w_q[ib], b_q_norm[ib], b_w_out[ib], rel_bias,
                                w_mem_kv[layer], mem_q_norm[layer], mem_k_norm[layer])
        x = x + mix
        x = x + 0.5 * swiglu(rms_norm_2(x, ffn2_norm[layer]), ffn2_w_gate[layer], ffn2_w_up[layer], ffn2_w_down[layer])
        if layer == N_A_LAYERS - 1:
            kv = rms_norm_2(x, kv_norm) @ w_kv
            k_sh = rms_norm_2(kv[..., :DIL_WIDTH].reshape(B, S, N_DIL_HEADS, HEAD_DIM), kv_k_norm)
            k_sh = k_sh.reshape(B, S, n_groups, HEADS_PER_GROUP, HEAD_DIM)
            v_sh = kv[..., DIL_WIDTH:].reshape(B, S, n_groups, HEADS_PER_GROUP, HEAD_DIM)
    return x


def setup_inputs(seed=0):
    out = dict(first_inputs(seed))
    for name, value in second_inputs(seed + 1).items():
        if name != "x":
            out[name + "_2"] = value
    return out


def reference(
    x, mix_norm_g, w_in, lru_conv_w, lru_conv_b, lru_w_rg, lru_b_rg, lru_w_ig, lru_b_ig,
    lru_lambda, conf_conv_w, conf_conv_b, conf_norm_g, conf_norm_b, beta_lru, beta_conv, w_out,
    ffn_norm_g, peer_w_q, peer_sub_keys, peer_u, peer_v, final_norm_g, mem_2, ffn1_norm_2,
    ffn1_w_gate_2, ffn1_w_up_2, ffn1_w_down_2, ffn2_norm_2, ffn2_w_gate_2, ffn2_w_up_2,
    ffn2_w_down_2, mix_norm_2, mem_norm_2, w_mem_kv_2, mem_q_norm_2, mem_k_norm_2, a_w_in_2,
    a_conv_2, a_gate_bias_2, a_h_norm_2, a_w_out_2, b_w_q_2, b_q_norm_2, b_w_out_2, kv_norm_2,
    w_kv_2, kv_k_norm_2, rel_bias_2,
):
    x = first_block(
        x, mix_norm_g, w_in, lru_conv_w, lru_conv_b, lru_w_rg, lru_b_rg, lru_w_ig, lru_b_ig,
        lru_lambda, conf_conv_w, conf_conv_b, conf_norm_g, conf_norm_b, beta_lru, beta_conv,
        w_out, ffn_norm_g, peer_w_q, peer_sub_keys, peer_u, peer_v, final_norm_g,
    )
    return second_block(
        x, mem_2, ffn1_norm_2, ffn1_w_gate_2, ffn1_w_up_2, ffn1_w_down_2, ffn2_norm_2,
        ffn2_w_gate_2, ffn2_w_up_2, ffn2_w_down_2, mix_norm_2, mem_norm_2, w_mem_kv_2,
        mem_q_norm_2, mem_k_norm_2, a_w_in_2, a_conv_2, a_gate_bias_2, a_h_norm_2, a_w_out_2,
        b_w_q_2, b_q_norm_2, b_w_out_2, kv_norm_2, w_kv_2, kv_k_norm_2, rel_bias_2,
    )


_drawn_inputs = setup_inputs


def setup_inputs(seed=0):
    import zlib

    import numpy as np

    out = dict(_drawn_inputs(seed))
    spreads = {}
    factors = {'lru_b_rg': 6.167,
     'lru_b_ig': 5.49,
     'beta_lru': 3.066,
     'beta_conv': 2.846,
     'ffn1_norm_2': 4.884,
     'ffn2_norm_2': 5.554,
     'mix_norm_2': 4.38,
     'mem_norm_2': 8.0,
     'mem_q_norm_2': 8.0,
     'mem_k_norm_2': 8.0,
     'a_h_norm_2': 5.69,
     'b_q_norm_2': 8.0,
     'kv_norm_2': 8.0,
     'kv_k_norm_2': 8.0,
     'rel_bias_2': 3.005}
    for name, (base, spread) in spreads.items():
        noise = np.random.default_rng([zlib.crc32(name.encode()), seed]).standard_normal(out[name].shape)
        drawn = base * np.exp(spread * noise) if base else spread * noise
        out[name] = __import__('jax').numpy.asarray(drawn.astype(out[name].dtype))
    for name, factor in factors.items():
        out[name] = (out[name] * factor).astype(out[name].dtype)
    return out
```

```python
from contextlib import ExitStack

import concourse.bass as bass
import numpy as np
from concourse import mybir

FP = mybir.dt.float32
U32 = mybir.dt.uint32
ALU = mybir.AluOpType
ACT = mybir.ActivationFunctionType
AX = mybir.AxisListType.X

P = 128
T = 512
D = 1024
DC = D // P
TT = T // P
EPS = 1e-6
NEG = -1e30

LRU_C4 = 4
LRU_TAPS, LRU_LEFT = 4, 2
CONF_TAPS, CONF_LEFT = 31, 15
HEADS, KEYS, TOPK = 8, 128, 16
HP = 2 * HEADS
EXPERT_GROUP = 8
EXPERT_GROUPS = KEYS // EXPERT_GROUP

FF = 2816
FC = FF // P
MEM_T, MEM_HEADS, HD = 256, 4, 64
ATT_SCALE = HD ** -0.5
ML_HEADS, ML_HD = 4, 192
ML_W = ML_HEADS * ML_HD
ML_CHUNKS = ML_W // P
ML_TAPS = 4
DIL_HEADS, DIL_PER_GROUP = 12, 4
DIL_W = DIL_HEADS * HD
DILATIONS = ((128, 1), (512, 4), (2048, 16))
BUCKETS, MAX_DISTANCE = 32, 2048
ML_PIECES = [[(0, 0, 128), (1, 0, 64)], [(1, 64, 64), (2, 0, 128)],
             [(3, 0, 128), (4, 0, 64)], [(4, 64, 64), (5, 0, 128)]]

SLOTS = 4
PANEL = DC * P
WORK = 38400

VEC = {}


def _vec_columns():
    at = 0
    for name, n in (("mix_g", 8), ("ffn_g", 8), ("final_g", 8), ("ffn1_g", 16), ("ffn2_g", 16),
                    ("mix2_g", 16), ("mem_g", 16), ("kv_g", 8), ("lru_w", 16), ("lru_b", 4),
                    ("b_rg", 8), ("b_ig", 8), ("lam", 8), ("conf_w", 124), ("conf_b", 4),
                    ("conf_g", 4), ("conf_nb", 4), ("beta_lru", 4), ("beta_conv", 4),
                    ("a_conv", 48), ("a_h", 6), ("mem_q", 2), ("mem_k", 2), ("b_q", 1),
                    ("kv_k", 1), ("gate_i", 1), ("gate_f", 1)):
        VEC[name] = at
        at += n
    return at


VEC_COLUMNS = _vec_columns()

IDENT, ONES, BLOCK, COUNT = 0, P, 2 * P, 3 * P
CONST_COLUMNS = 4 * P
TOEP = T + P


class Machine:

    def __init__(self, nc, ctx):
        self.nc, self.ctx = nc, ctx
        sb = lambda name, shape, dt=FP: ctx.enter_context(nc.sbuf_tensor(name, shape, dt))
        self.x = sb("residual", [P, DC, T])
        self.n = sb("normed", [P, DC, T])
        self.ring = sb("weight_ring", [P, SLOTS, PANEL])
        self.const = sb("constants", [P, CONST_COLUMNS])
        self.vec = sb("vectors", [P, VEC_COLUMNS])
        self.work = sb("work", [P, WORK])
        self.bank = [ctx.enter_context(nc.psum_tensor(f"bank{b}", [P, T], FP)) for b in range(8)]
        self.reached = {}
        self.sems = {}
        self.loaded = [self.sem(f"panel_loaded{s}") for s in range(SLOTS)]
        self.used = self.sem("panels_used")
        self.bank_free = [self.sem(f"bank_free{b}") for b in range(SLOTS)]
        self.panels = 0
        self.fills = 0
        self.eps = EPS
        self.vector_order = Order(self.sem("vector_order"))
        self.scalar_order = Order(self.sem("scalar_order"))

    def sem(self, name):
        if name not in self.sems:
            self.sems[name] = self.ctx.enter_context(self.nc.semaphore(name))
            self.reached[name] = 0
        return self.sems[name]

    def v(self, name, column=0):
        at = VEC[name] + column
        return self.vec[:, at:at + 1]

    def cut(self, at, *dims):
        n = int(np.prod(dims))
        assert at + n <= WORK, (at, dims)
        flat = self.work[:, at:at + n]
        if len(dims) == 1:
            return flat
        if len(dims) == 2:
            return flat.rearrange("p (a b) -> p a b", a=dims[0])
        return flat.rearrange("p (a b c) -> p a b c", a=dims[0], b=dims[1])


class Count:

    def __init__(self, m, name, total):
        self.sem, self.base = m.sem(name), m.reached[name] if name in m.reached else 0
        m.reached[name] = self.base + total


class Order:

    def __init__(self, sem):
        self.sem, self.n = sem, 0

    def step(self, eng, ins):
        ins.then_inc(self.sem, 1)
        self.n += 1
        eng.wait_ge(self.sem, self.n)


def weight_panels(m, sp, dram, n):
    first = m.panels
    with sp.Fori(0, n // SLOTS) as i:
        for s in range(SLOTS):
            sp.wait_ge(m.used, i * SLOTS + (first + s + 1))
            sp.dma_start(m.ring[:, s, :], dram[bass.ds(i * SLOTS + s, 1)].rearrange("o p n -> p (o n)"))\
              .then_inc(m.loaded[s], 16)


def panel_products(m, pe, n, rhs, width=T):
    panel0, fill0 = m.panels // SLOTS, m.fills // SLOTS
    with pe.Fori(0, n // SLOTS) as i:
        for s in range(SLOTS):
            pe.wait_ge(m.loaded[s], i * 16 + 16 * (panel0 + 1))
            pe.wait_ge(m.bank_free[s], i + (fill0 + 1))
            for c in range(DC):
                last = m.nc.tensor.matmul(m.bank[s][:, 0:width], m.ring[:, s, c * P:(c + 1) * P],
                                          rhs(c), start=(c == 0), stop=(c == DC - 1))
            last.then_inc(m.used, 1)


def start(m, io):
    nc = m.nc
    loaded = m.sem("start_loaded")
    with nc.Block() as block:
        @block.sync
        def _(sp):
            sp.dma_start(m.const[:, :], io["constants"]).then_inc(loaded, 16)
            sp.dma_start(m.vec[:, :], io["vectors"]).then_inc(loaded, 16)
            sp.dma_start(m.x[:, :, :], io["x"]).then_inc(loaded, 16)
            sp.wait_ge(loaded, 48)

        @block.gpsimd
        def _(pool):
            pool.sem_inc(m.used, SLOTS)
            for b in range(SLOTS):
                pool.sem_inc(m.bank_free[b], 1)


def rms(m, src, dst, gain, chunks, width, at, square_src=None):
    nc = m.nc
    sq = m.cut(at, 4, width)
    root = m.cut(at + 4 * width, width)
    inv = m.cut(at + 5 * width, width)
    squared = Count(m, "norm_squared", chunks)
    summed = Count(m, "norm_summed", chunks)
    rooted = Count(m, "norm_rooted", 1)
    total = m.bank[7]
    with nc.Block() as block:
        @block.scalar
        def _(act):
            for c in range(chunks):
                if c >= 4:
                    act.wait_ge(summed.sem, summed.base + c - 3)
                nc.scalar.activation(sq[:, c % 4, :], src(c), ACT.Square).then_inc(squared.sem, 1)
            act.wait_ge(summed.sem, summed.base + chunks)
            nc.scalar.activation(root, total[:, 0:width], ACT.Sqrt, bias=m.eps,
                                 scale=1.0 / (chunks * P)).then_inc(rooted.sem, 1)

        @block.tensor
        def _(pe):
            for c in range(chunks):
                pe.wait_ge(squared.sem, squared.base + c + 1)
                nc.tensor.matmul(total[:, 0:width], m.const[:, ONES:ONES + P], sq[:, c % 4, :],
                                 start=(c == 0), stop=(c == chunks - 1)).then_inc(summed.sem, 1)

        @block.vector
        def _(dve):
            dve.wait_ge(rooted.sem, rooted.base + 1)
            m.vector_order.step(dve, nc.vector.reciprocal(inv, root))
            for c in range(chunks):
                nc.vector.scalar_tensor_tensor(out=dst(c), in0=src(c), scalar=gain(c), in1=inv,
                                               op0=ALU.mult, op1=ALU.mult)


def norm_x(m, name, column=0, dst=None):
    to = dst or (lambda c: m.n[:, c, :])
    rms(m, lambda c: m.x[:, c, :], to, lambda c: m.v(name, column + c), DC, T, 0)


def linear_add(m, dram):
    nc = m.nc
    first, fill0 = m.panels, m.fills // SLOTS
    with nc.Block() as block:
        @block.sync
        def _(sp):
            weight_panels(m, sp, dram, DC)

        @block.tensor
        def _(pe):
            panel_products(m, pe, DC, lambda c: m.n[:, c, :])

        @block.vector
        def _(dve):
            for c in range(DC):
                dve.wait_ge(m.used, first + SLOTS + c + 1)
                nc.vector.tensor_tensor(m.x[:, c, :], m.x[:, c, :], m.bank[c % 4][:, :], ALU.add)\
                  .then_inc(m.bank_free[c % 4], 1)
    m.panels += DC
    m.fills += DC


def hybrid_mixer(m, io):
    nc = m.nc
    C4 = LRU_C4
    at = 0

    def take(*dims):
        nonlocal at
        view = m.cut(at, *dims)
        at += int(np.prod(dims))
        return view

    XPAD = T + 4
    GPAD = T + 32
    x_pad = take(C4, XPAD)
    g_gelu = take(C4, T)
    a_glu = take(C4, T)
    glu_pad = take(C4, GPAD)
    gate_w = take(4 * C4, P)
    xc = take(C4, T)
    tanh = take(2 * C4, T)
    gate_i = take(2 * C4, T)
    root = take(2 * C4, T)
    inv = take(2 * C4, T)
    conv = take(C4, T)
    lam = take(8, 8)
    DIAGS = 16
    diag = take(DIAGS, P)
    b_sig = conv

    side = m.sem("mix_side_loaded")
    first = m.panels
    in_evac = m.sem("mix_in_evacuated")
    lam_exp = m.sem("mix_lambda_exp")
    lam_done = m.sem("mix_lambda_done")
    xc_ready = m.sem("mix_xc_ready")
    glu_ready = m.sem("mix_glu_ready")
    gate_done = m.sem("mix_gate_products")
    gate_evac = m.sem("mix_gates_evacuated")
    tanh_done = m.sem("mix_tanh_done")
    root_done = m.sem("mix_root_done")
    inv_done = m.sem("mix_inv_done")
    diag_ready = m.sem("mix_diag_ready")
    diag_used = m.sem("mix_diag_used")
    conv_done = m.sem("mix_conv_evacuated")
    V = m.v
    with nc.Block() as block:
        @block.sync
        def _(sp):
            sp.dma_start(gate_w, io["lru_gates"]).then_inc(side, 16)
            weight_panels(m, sp, io["w_in"], 4 * C4)
            sp.wait_ge(side, 16)

        @block.gpsimd
        def _(pool):
            for k in range(C4 * CONF_TAPS):
                if k >= DIAGS:
                    pool.wait_ge(diag_used, k - DIAGS + 1)
                nc.gpsimd.tensor_scalar(diag[:, k % DIAGS, :], m.const[:, IDENT:IDENT + P],
                                        V("conf_w", k), None, ALU.mult).then_inc(diag_ready, 1)

        @block.tensor
        def _(pe):
            panel_products(m, pe, 4 * C4, lambda c: m.n[:, c, :])
            pe.wait_ge(side, 16)
            pe.wait_ge(xc_ready, C4)
            for j in range(4 * C4):
                gate, way, c = j // (2 * C4), j // C4 % 2, j % C4
                if j >= 4:
                    pe.wait_ge(gate_evac, j - 3)
                else:
                    pe.wait_ge(in_evac, 4 * C4)
                nc.tensor.matmul(m.bank[j % 4][:, :], gate_w[:, (way * 2 + gate) * C4 + c, :], xc[:, c, :],
                                 start=True, stop=True).then_inc(gate_done, 1)
            pe.wait_ge(glu_ready, C4)
            for k in range(C4 * CONF_TAPS):
                c, tap = divmod(k, CONF_TAPS)
                pe.wait_ge(diag_ready, k + 1)
                nc.tensor.matmul(m.bank[4 + c][:, :], diag[:, k % DIAGS, :], glu_pad[:, c, tap:tap + T],
                                 start=(tap == 0), stop=(tap == CONF_TAPS - 1)).then_inc(diag_used, 1)

        @block.scalar
        def _(act):
            order = m.scalar_order
            order.step(act, nc.scalar.activation(lam[:, 0, :], m.vec[:, VEC["lam"]:VEC["lam"] + 8], ACT.Abs))
            nc.scalar.activation(lam[:, 1, :], lam[:, 0, :], ACT.Exp, scale=-1.0).then_inc(lam_exp, 1)
            kinds = [(x_pad, ACT.Copy), (g_gelu, ACT.Gelu_apprx_tanh), (a_glu, ACT.Copy), (b_sig, ACT.Sigmoid)]
            for j in range(4 * C4):
                dst, func = kinds[j // C4]
                out = dst[:, j % C4, LRU_LEFT:LRU_LEFT + T] if j < C4 else dst[:, j % C4, :]
                act.wait_ge(m.used, first + SLOTS + j + 1)
                order.step(act, nc.scalar.activation(out, m.bank[j % 4][:, :], func))
                act.sem_inc(m.bank_free[j % 4], 1)
                act.sem_inc(in_evac, 1)
            for j in range(4 * C4):
                gate, way, c = j // (2 * C4), j // C4 % 2, j % C4
                act.wait_ge(gate_done, j + 1)
                dst = tanh if gate == 0 else gate_i
                bias = V("b_rg" if gate == 0 else "b_ig", way * C4 + c)
                nc.scalar.activation(dst[:, way * C4 + c, :], m.bank[j % 4][:, :], ACT.Sigmoid, bias=bias)\
                  .then_inc(gate_evac, 1)
            act.wait_ge(lam_done, 1)
            act.wait_ge(gate_evac, 4 * C4)
            for w in range(2 * C4):
                nc.scalar.activation(tanh[:, w, :], tanh[:, w, :], ACT.Tanh, scale=lam[:, 7, w:w + 1])\
                  .then_inc(tanh_done, 1)
            act.wait_ge(tanh_done, 2 * C4)
            for w in range(2 * C4):
                nc.scalar.activation(root[:, w, :], tanh[:, w, :], ACT.Sqrt, scale=4.0).then_inc(root_done, 1)
            act.wait_ge(glu_ready, C4)
            for c in range(C4):
                act.wait_ge(diag_used, (c + 1) * CONF_TAPS)
                nc.scalar.activation(conv[:, c, :], m.bank[4 + c][:, :], ACT.Identity, bias=V("conf_b", c))\
                  .then_inc(conv_done, 1)

        @block.vector
        def _(dve):
            order = m.vector_order
            vec = nc.vector
            vec.memset(x_pad[:, :, 0:LRU_LEFT], 0.0)
            vec.memset(x_pad[:, :, LRU_LEFT + T:XPAD], 0.0)
            vec.memset(glu_pad[:, :, 0:CONF_LEFT], 0.0)
            order.step(dve, vec.memset(glu_pad[:, :, CONF_LEFT + T:GPAD], 0.0))
            dve.wait_ge(lam_exp, 1)
            e, z, z2, p, neg = (lam[:, i, :] for i in (1, 2, 3, 4, 5))
            order.step(dve, vec.tensor_scalar(z, e, 2.0, None, ALU.add))
            order.step(dve, vec.reciprocal(z, z))
            order.step(dve, vec.tensor_tensor(z, z, e, ALU.mult))
            order.step(dve, vec.tensor_tensor(z2, z, z, ALU.mult))
            order.step(dve, vec.tensor_scalar(p, z2, 1.0 / 17, None, ALU.mult))
            for k in (15, 13, 11, 9, 7, 5, 3):
                order.step(dve, vec.scalar_tensor_tensor(out=p, in0=p, scalar=1.0 / k, in1=z2, op0=ALU.add, op1=ALU.mult))
            order.step(dve, vec.scalar_tensor_tensor(out=p, in0=p, scalar=1.0, in1=z, op0=ALU.add, op1=ALU.mult))
            order.step(dve, vec.tensor_scalar(neg, m.vec[:, VEC["lam"]:VEC["lam"] + 8], -1.0, 0.0, ALU.mult, ALU.max))
            order.step(dve, vec.scalar_tensor_tensor(out=p, in0=p, scalar=2.0, in1=neg, op0=ALU.mult, op1=ALU.add))
            vec.tensor_scalar(lam[:, 7, :], p, 4.0, None, ALU.mult).then_inc(lam_done, 1)
            dve.wait_ge(in_evac, C4)
            for tap in range(LRU_TAPS):
                for c in range(C4):
                    src, w = x_pad[:, c, tap:tap + T], V("lru_w", tap * C4 + c)
                    if tap == 0:
                        ins = vec.tensor_scalar(xc[:, c, :], src, w, V("lru_b", c), ALU.mult, ALU.add)
                    else:
                        ins = vec.scalar_tensor_tensor(out=xc[:, c, :], in0=src, scalar=w, in1=xc[:, c, :],
                                                       op0=ALU.mult, op1=ALU.add)
                    if tap == LRU_TAPS - 1:
                        ins.then_inc(xc_ready, 1)
                    elif c == C4 - 1:
                        order.step(dve, ins)
            for c in range(C4):
                dve.wait_ge(in_evac, 3 * C4 + c + 1)
                vec.tensor_tensor(glu_pad[:, c, CONF_LEFT:CONF_LEFT + T], a_glu[:, c, :], b_sig[:, c, :],
                                  ALU.mult).then_inc(glu_ready, 1)
            dve.wait_ge(xc_ready, C4)
            for w in range(2 * C4):
                dve.wait_ge(tanh_done, w + 1)
                order.step(dve, vec.tensor_scalar(inv[:, w, :], tanh[:, w, :], 1.0, None, ALU.add))
                order.step(dve, vec.reciprocal(inv[:, w, :], inv[:, w, :]))
                vec.tensor_tensor(gate_i[:, w, :], gate_i[:, w, :], xc[:, w % C4, :], ALU.mult)
                dve.wait_ge(root_done, w + 1)
                vec.tensor_scalar(tanh[:, w, :], inv[:, w, :], 2.0, -1.0, ALU.mult, ALU.add)
                order.step(dve, vec.tensor_tensor(root[:, w, :], root[:, w, :], inv[:, w, :], ALU.mult))
                order.step(dve, vec.tensor_tensor(root[:, w, :], root[:, w, :], gate_i[:, w, :], ALU.mult))
                if w < C4:
                    ins = vec.tensor_tensor_scan(inv[:, w, :], tanh[:, w, :], root[:, w, :], 0.0, ALU.mult, ALU.add)
                else:
                    ins = vec.tensor_tensor_scan(inv[:, w, ::-1], tanh[:, w, ::-1], root[:, w, ::-1], 0.0,
                                                 ALU.mult, ALU.add)
            order.step(dve, ins)
            for c in range(C4):
                ins = vec.tensor_tensor(inv[:, c, :], inv[:, c, :], inv[:, C4 + c, :], ALU.add)
            order.step(dve, ins)
            for c in range(C4):
                vec.tensor_tensor(inv[:, c, :], inv[:, c, :], g_gelu[:, c, :], ALU.mult)
    m.panels += 4 * C4
    m.fills += 4 * C4

    sq, std = tanh, gate_i
    averaged = m.sem("gln_averaged")
    centred = m.sem("gln_centred")
    squared = m.sem("gln_squared")
    summed = m.sem("gln_summed")
    rooted = m.sem("gln_rooted")
    scaled = m.sem("gln_scaled")
    with nc.Block() as block:
        @block.tensor
        def _(pe):
            for c in range(C4):
                nc.tensor.matmul(m.bank[c][:, :], m.const[:, BLOCK:BLOCK + P], conv[:, c, :],
                                 start=True, stop=True).then_inc(averaged, 1)
            for c in range(C4):
                pe.wait_ge(squared, c + 1)
                nc.tensor.matmul(m.bank[4 + c][:, :], m.const[:, BLOCK:BLOCK + P], sq[:, c, :],
                                 start=True, stop=True).then_inc(summed, 1)

        @block.vector
        def _(dve):
            for c in range(C4):
                dve.wait_ge(averaged, c + 1)
                nc.vector.scalar_tensor_tensor(out=conv[:, c, :], in0=m.bank[c][:, :], scalar=-1.0 / HD,
                                               in1=conv[:, c, :], op0=ALU.mult, op1=ALU.add).then_inc(centred, 1)
            for c in range(C4):
                dve.wait_ge(rooted, c + 1)
                m.vector_order.step(dve, nc.vector.reciprocal(std[:, c, :], std[:, c, :]))
                nc.vector.tensor_tensor(std[:, c, :], std[:, c, :], conv[:, c, :], ALU.mult).then_inc(scaled, 1)

        @block.scalar
        def _(act):
            for c in range(C4):
                act.wait_ge(centred, c + 1)
                nc.scalar.activation(sq[:, c, :], conv[:, c, :], ACT.Square).then_inc(squared, 1)
            for c in range(C4):
                act.wait_ge(summed, c + 1)
                nc.scalar.activation(std[:, c, :], m.bank[4 + c][:, :], ACT.Sqrt, bias=m.eps, scale=1.0 / HD)\
                  .then_inc(rooted, 1)
            for c in range(C4):
                act.wait_ge(scaled, c + 1)
                nc.scalar.activation(conv[:, c, :], std[:, c, :], ACT.Silu, bias=V("conf_nb", c),
                                     scale=V("conf_g", c))
    rms(m, lambda c: inv[:, c, :], lambda c: m.n[:, c, :], lambda c: V("beta_lru", c), C4, T, 0)
    rms(m, lambda c: conv[:, c, :], lambda c: m.n[:, C4 + c, :], lambda c: V("beta_conv", c), C4, T, 0)
    linear_add(m, io["w_out"])


ROUTE_GT = WORK - 3 * T


def route(m, io):
    nc = m.nc
    at = 0

    def take(*dims):
        nonlocal at
        view = m.cut(at, *dims)
        at += int(np.prod(dims))
        return view

    q = take(HP, T)
    keys = take(HP, KEYS)
    s = take(HP, KEYS)
    s2 = take(HP, KEYS)
    cand = take(HEADS, TOPK * TOPK)
    cand2 = take(HEADS, TOPK * TOPK)
    hot = take(HEADS * TOPK, TOPK)
    top = take(HP, TOPK)
    idx = take(HP, TOPK).bitcast(U32)
    idxf = take(HP, TOPK)
    ts = take(HEADS, TOPK)
    pos = take(HEADS, TOPK).bitcast(U32)
    part = take(2, HEADS * TOPK).bitcast(U32)
    partf = take(2, HEADS * TOPK)
    ex = take(HEADS, TOPK)
    tot = take(HEADS)
    found = take(TT, 3 * HEADS * TOPK)
    assert at <= ROUTE_GT
    gt = m.cut(ROUTE_GT, 3, T)
    first = m.panels
    side = m.sem("route_keys_loaded")
    q_ready = m.sem("route_q_ready")
    s_done = m.sem("route_scores_done")
    s_evac = m.sem("route_scores_evacuated")
    s_used = m.sem("route_scores_used")
    diff = m.sem("route_gate_diff")
    expd = m.sem("route_gate_exp")
    tile_done = m.sem("route_tile_done")
    turned = m.sem("route_turned")
    NEVER = -3.0e38
    with nc.Block() as block:
        @block.sync
        def _(sp):
            sp.dma_start(keys, io["keys"]).then_inc(side, 16)
            weight_panels(m, sp, io["w_q"], HP)
            sp.wait_ge(side, 16)

        @block.tensor
        def _(pe):
            panel_products(m, pe, HP, lambda c: m.n[:, c, :])
            pe.wait_ge(side, 16)
            pe.wait_ge(q_ready, HP)
            for t in range(TT):
                for j in range(HP):
                    if t and j % 4 == 0:
                        pe.wait_ge(s_evac, 4 * (t - 1) + j // 4 + 1)
                    ins = nc.tensor.matmul(m.bank[4 + j // 4][:, (j % 4) * P:(j % 4 + 1) * P],
                                           q[:, j, t * P:(t + 1) * P], keys[:, j, :], start=(j % 4 == 0),
                                           stop=(j % 4 == 3), skip_group_check=True)
                    if j % 4 == 3:
                        ins.then_inc(s_done, 1)
            for t in range(TT):
                pe.wait_ge(tile_done, t + 1)
                for w in range(3):
                    ins = nc.tensor.transpose(m.bank[w][:, t * P:(t + 1) * P],
                                              found[:, t, w * P:(w + 1) * P], m.const[:, IDENT:IDENT + P])
            ins.then_inc(turned, 1)

        @block.scalar
        def _(act):
            for j in range(HP):
                act.wait_ge(m.used, first + SLOTS + j + 1)
                m.scalar_order.step(act, nc.scalar.activation(q[:, j, :], m.bank[j % 4][:, :], ACT.Copy))
                act.sem_inc(m.bank_free[j % 4], 1)
                act.sem_inc(q_ready, 1)
            for t in range(TT):
                for b in range(4):
                    act.wait_ge(s_done, 4 * t + b + 1)
                    if t:
                        act.wait_ge(s_used, t)
                    nc.scalar.activation(s[:, 4 * b:4 * b + 4, :].rearrange("p a b -> p (a b)"),
                                         m.bank[4 + b][:, :], ACT.Copy).then_inc(s_evac, 1)
                act.wait_ge(diff, t + 1)
                nc.scalar.activation(ex, ex, ACT.Exp).then_inc(expd, 1)
            act.wait_ge(turned, 1)
            for w in range(3):
                nc.scalar.activation(gt[:, w, :], m.bank[w][:, :], ACT.Copy)

        @block.vector
        def _(dve):
            order, vec = m.vector_order, nc.vector
            count16 = m.const[:, COUNT:COUNT + TOPK]
            for t in range(TT):
                dve.wait_ge(s_evac, t * 4 + 4)
                for j in range(HP):
                    ins = vec.max(top[:, j, 0:8], s[:, j, :])
                order.step(dve, ins)
                for j in range(HP):
                    vec.max_index(idx[:, j, 0:8], top[:, j, 0:8], s[:, j, :])
                    ins = vec.match_replace(s2[:, j, :], top[:, j, 0:8], s[:, j, :], NEVER)
                order.step(dve, ins)
                dve.sem_inc(s_used, 1)
                for j in range(HP):
                    ins = vec.max(top[:, j, 8:16], s2[:, j, :])
                order.step(dve, ins)
                for j in range(HP):
                    ins = vec.max_index(idx[:, j, 8:16], top[:, j, 8:16], s2[:, j, :])
                halves = top.rearrange("p (h w) k -> p h w k", w=2)
                order.step(dve, vec.tensor_tensor(
                    cand.rearrange("p h (a b) -> p h a b", a=TOPK),
                    halves[:, :, 0, :].unsqueeze(3).to_broadcast([P, HEADS, TOPK, TOPK]),
                    halves[:, :, 1, :].unsqueeze(2).to_broadcast([P, HEADS, TOPK, TOPK]), ALU.add))
                vec.tensor_copy(idxf, idx)
                for h in range(HEADS):
                    ins = vec.max(ts[:, h, 0:8], cand[:, h, :])
                order.step(dve, ins)
                for h in range(HEADS):
                    vec.max_index(pos[:, h, 0:8], ts[:, h, 0:8], cand[:, h, :])
                    ins = vec.match_replace(cand2[:, h, :], ts[:, h, 0:8], cand[:, h, :], NEVER)
                order.step(dve, ins)
                for h in range(HEADS):
                    ins = vec.max(ts[:, h, 8:16], cand2[:, h, :])
                order.step(dve, ins)
                for h in range(HEADS):
                    vec.max_index(pos[:, h, 8:16], ts[:, h, 8:16], cand2[:, h, :])
                order.step(dve, vec.tensor_tensor(ex, ts, ts[:, :, 0:1].to_broadcast([P, HEADS, TOPK]), ALU.subtract))
                dve.sem_inc(diff, 1)
                flat = pos.rearrange("p h k -> p (h k)")
                vec.tensor_scalar(part[:, 0, :], flat, 4, None, ALU.logical_shift_right)
                order.step(dve, vec.tensor_scalar(part[:, 1, :], flat, TOPK - 1, None, ALU.bitwise_and))
                order.step(dve, vec.tensor_copy(partf, part))
                index = idxf.rearrange("p (h w) k -> p h w k", w=2)
                hots = hot.rearrange("p (h k) a -> p h k a", h=HEADS)
                base = found[:, t, :]
                for w in range(2):
                    order.step(dve, vec.tensor_tensor(
                        hot, partf[:, w, :].unsqueeze(2).to_broadcast([P, HEADS * TOPK, TOPK]),
                        count16.unsqueeze(1).to_broadcast([P, HEADS * TOPK, TOPK]), ALU.is_equal))
                    order.step(dve, vec.tensor_tensor(
                        hots, hots, index[:, :, w, :].unsqueeze(2).to_broadcast([P, HEADS, TOPK, TOPK]), ALU.mult))
                    order.step(dve, vec.tensor_reduce(base[:, w * P:(w + 1) * P], hot, AX, ALU.add))
                dve.wait_ge(expd, t + 1)
                order.step(dve, vec.tensor_reduce(tot, ex, AX, ALU.add))
                order.step(dve, vec.reciprocal(tot, tot))
                vec.tensor_tensor(base[:, 2 * P:3 * P].rearrange("p (h k) -> p h k", h=HEADS), ex,
                                  tot.unsqueeze(2).to_broadcast([P, HEADS, TOPK]), ALU.mult).then_inc(tile_done, 1)
    m.panels += HP
    m.fills += HP


def spread_gates(m, io):
    nc = m.nc
    gt = m.cut(ROUTE_GT, 3, T)
    stage = [m.cut(h * KEYS * P, KEYS, P) for h in range(2)]
    BATCH = 4
    rows2 = m.cut(2 * KEYS * P, 2, BATCH * P)
    rows1 = m.cut(2 * KEYS * P + 2 * BATCH * P, 2, BATCH * P)
    gates = io["gates"].rearrange("a b t -> b a t")
    rows_ready = m.sem("spread_rows_ready")
    done = m.sem("spread_products")
    evac = m.sem("spread_evacuated")
    stored = [m.sem(f"spread_stored{h}") for h in range(2)]
    PER_TILE = P // BATCH
    count = m.const[:, COUNT:COUNT + P]
    with nc.Block() as block:
        @block.vector
        def _(dve):
            dve.sem_inc(done, 2)
            with dve.Fori(0, TT * PER_TILE // 2) as i:
                for h in range(2):
                    dve.wait_ge(done, i * 2 + h + 1)
                    for u in range(BATCH):
                        t = i * (2 * BATCH) + (h * BATCH + u)
                        nc.vector.tensor_scalar(rows2[:, h, u * P:(u + 1) * P], count,
                                                gt[:, 1, bass.ds(t, 1)], None, ALU.is_equal)
                        ins = nc.vector.tensor_scalar(rows1[:, h, u * P:(u + 1) * P], count,
                                                      gt[:, 0, bass.ds(t, 1)], gt[:, 2, bass.ds(t, 1)],
                                                      ALU.is_equal, ALU.mult)
                    ins.then_inc(rows_ready, 1)

        @block.tensor
        def _(pe):
            pe.sem_inc(evac, 2)
            with pe.Fori(0, TT * PER_TILE // 2) as i:
                for h in range(2):
                    pe.wait_ge(rows_ready, i * 2 + h + 1)
                    pe.wait_ge(evac, i * 2 + h + 1)
                    for u in range(BATCH):
                        ins = nc.tensor.matmul(m.bank[h][:, u * P:(u + 1) * P], rows2[:, h, u * P:(u + 1) * P],
                                               rows1[:, h, u * P:(u + 1) * P], start=(u == 0),
                                               stop=(u == BATCH - 1), skip_group_check=True)
                    ins.then_inc(done, 1)

        @block.scalar
        def _(act):
            for tile in range(TT):
                if tile >= 2:
                    act.wait_ge(stored[tile % 2], 16 * (tile // 2))
                with act.Fori(0, PER_TILE // 2) as i:
                    for h in range(2):
                        act.wait_ge(done, i * 2 + (tile * PER_TILE + h + 3))
                        out = stage[tile % 2][:, :, bass.ds(i * (2 * BATCH) + h * BATCH, BATCH)]
                        nc.scalar.activation(out.rearrange("p a t -> p t a"),
                                             m.bank[h][:, :].rearrange("p (t a) -> p t a", t=BATCH), ACT.Copy)\
                          .then_inc(evac, 1)

        @block.sync
        def _(sp):
            for tile in range(TT):
                sp.wait_ge(evac, 2 + (tile + 1) * PER_TILE)
                sp.dma_start(gates[:, :, tile * P:(tile + 1) * P], stage[tile % 2]).then_inc(stored[tile % 2], 16)
            for h in range(2):
                sp.wait_ge(stored[h], 16 * (TT // 2))


def experts(m, io):
    nc = m.nc
    E = EXPERT_GROUP
    gates = m.cut(0, 2 * E, T)
    gated = m.cut(2 * E * T, E, T)
    act_buf = m.cut(3 * E * T, SLOTS, T)
    first, fill0 = m.panels, m.fills // SLOTS
    panel0 = m.panels // SLOTS
    gate_loaded = [m.sem(f"expert_gate_loaded{h}") for h in range(2)]
    activated = m.sem("expert_activated")
    group_used = m.sem("expert_group_gated")
    with nc.Block() as block:
        @block.sync
        def _(sp):
            with sp.Fori(0, EXPERT_GROUPS) as g:
                for half, dram in ((0, io["expert_u"]), (1, io["expert_v"])):
                    for j in range(E):
                        s = j % SLOTS
                        sp.wait_ge(m.used, g * (2 * E) + (first + half * E + j + 1))
                        sp.dma_start(m.ring[:, s, :], dram[bass.ds(g * E + j, 1)].rearrange("o p n -> p (o n)"))\
                          .then_inc(m.loaded[s], 16)

        @block.gpsimd
        def _(pool):
            pool.sem_inc(group_used, 2)
            with pool.Fori(0, EXPERT_GROUPS // 2) as g:
                for h in range(2):
                    pool.wait_ge(group_used, g * 2 + h + 1)
                    pool.dma_start(gates[:, h * E:(h + 1) * E, :],
                                   io["gates"][bass.ds((g * 2 + h) * E, E)].rearrange("a p t -> p a t"))\
                        .then_inc(gate_loaded[h], 16)

        @block.tensor
        def _(pe):
            with pe.Fori(0, EXPERT_GROUPS) as g:
                for j in range(2 * E):
                    s = j % SLOTS
                    turn = j // SLOTS
                    pe.wait_ge(m.loaded[s], g * (16 * 2 * E // SLOTS) + 16 * (panel0 + turn + 1))
                    pe.wait_ge(m.bank_free[s], g * (2 * E // SLOTS) + (fill0 + turn + 1))
                    if j == E:
                        for b in range(SLOTS):
                            pe.wait_ge(m.bank_free[b], g * (2 * E // SLOTS) + (fill0 + 3))
                    for c in range(DC):
                        rhs = m.n[:, c, :] if j < E else gated[:, c, :]
                        last = nc.tensor.matmul(m.bank[s][:, :], m.ring[:, s, c * P:(c + 1) * P], rhs,
                                                start=(c == 0), stop=(c == DC - 1))
                    last.then_inc(m.used, 1)

        @block.scalar
        def _(act):
            with act.Fori(0, EXPERT_GROUPS) as g:
                for j in range(E):
                    s = j % SLOTS
                    turn = j // SLOTS
                    act.wait_ge(m.used, g * (2 * E) + (first + SLOTS + j + 1))
                    act.wait_ge(m.bank_free[s], g * (2 * E // SLOTS) + (fill0 + turn + 1))
                    nc.scalar.activation(act_buf[:, s, :], m.bank[s][:, :], ACT.Gelu_apprx_tanh)\
                      .then_inc(activated, 1)

        @block.vector
        def _(dve):
            with dve.Fori(0, EXPERT_GROUPS // 2) as g:
                for h in range(2):
                    dve.wait_ge(gate_loaded[h], g * 16 + 16)
                    dve.wait_ge(m.used, g * (4 * E) + (first + SLOTS + 2 * E * h))
                    for j in range(E):
                        dve.wait_ge(activated, g * (2 * E) + (h * E + j + 1))
                        nc.vector.tensor_tensor(gated[:, j, :], act_buf[:, j % SLOTS, :], gates[:, h * E + j, :],
                                                ALU.mult).then_inc(m.bank_free[j % SLOTS], 1)
                    for c in range(DC):
                        dve.wait_ge(m.used, g * (4 * E) + (first + SLOTS + 2 * E * h + E + c + 1))
                        ins = nc.vector.tensor_tensor(m.x[:, c, :], m.x[:, c, :], m.bank[c % SLOTS][:, :], ALU.add)
                        ins.then_inc(m.bank_free[c % SLOTS], 1)
                    dve.wait_ge(m.bank_free[SLOTS - 1], g * 8 + (fill0 + 1 + 4 * (h + 1)))
                    dve.sem_inc(group_used, 1)
    m.panels += 2 * E * EXPERT_GROUPS
    m.fills += 2 * E * EXPERT_GROUPS


def swiglu(m, gate_w, up_w, down_w):
    nc = m.nc
    hidden = m.cut(0, FC, T)
    sg = m.cut(FC * T, 2, T)
    first, fill0 = m.panels, m.fills // SLOTS
    panel0 = m.panels // SLOTS
    down_first, down_fill0 = first + 2 * FC, fill0 + 2 * FC // SLOTS
    down_panel0 = down_first // SLOTS
    WIDTHS = (8, 8, FC - 16)
    with nc.Block() as block:
        @block.sync
        def _(sp):
            with sp.Fori(0, FC // 2) as i:
                for s in range(SLOTS):
                    dram = (gate_w, up_w)[s % 2]
                    sp.wait_ge(m.used, i * SLOTS + (first + s + 1))
                    sp.dma_start(m.ring[:, s, :], dram[bass.ds(i * 2 + s // 2, 1)].rearrange("o p n -> p (o n)"))\
                      .then_inc(m.loaded[s], 16)
            with sp.Fori(0, 2) as i:
                for k in range(12):
                    s, (c, part) = k % SLOTS, divmod(k, 3)
                    sp.wait_ge(m.used, i * 12 + (down_first + k + 1))
                    sp.dma_start(m.ring[:, s, 0:WIDTHS[part] * P],
                                 down_w[bass.ds(i * 4 + c, 1), :, part * PANEL:part * PANEL + WIDTHS[part] * P]
                                 .rearrange("o p n -> p (o n)")).then_inc(m.loaded[s], 16)

        @block.tensor
        def _(pe):
            panel_products(m, pe, 2 * FC, lambda c: m.n[:, c, :])
            for b in (1, 3):
                pe.wait_ge(m.bank_free[b], fill0 + FC // 2 + 1)
            with pe.Fori(0, 2) as i:
                for k in range(12):
                    s, (b, part) = k % SLOTS, divmod(k, 3)
                    pe.wait_ge(m.loaded[s], i * 48 + 16 * (down_panel0 + k // SLOTS + 1))
                    if part == 0:
                        pe.wait_ge(m.bank_free[b], i + (down_fill0 + 1))
                    for c in range(WIDTHS[part]):
                        f = part * 8 + c
                        last = nc.tensor.matmul(m.bank[b][:, :], m.ring[:, s, c * P:(c + 1) * P],
                                                hidden[:, f, :], start=(f == 0), stop=(f == FC - 1))
                    last.then_inc(m.used, 1)

        @block.scalar
        def _(act):
            with act.Fori(0, FC // 2) as i:
                for v in range(2):
                    act.wait_ge(m.used, i * SLOTS + (first + SLOTS + 2 * v + 1))
                    act.wait_ge(m.bank_free[2 * v + 1], i + (fill0 + 1))
                    nc.scalar.activation(sg[:, v, :], m.bank[2 * v][:, :], ACT.Silu)\
                      .then_inc(m.bank_free[2 * v], 1)

        @block.vector
        def _(dve):
            with dve.Fori(0, FC // 2) as i:
                for v in range(2):
                    dve.wait_ge(m.bank_free[2 * v], i + (fill0 + 2))
                    dve.wait_ge(m.used, i * SLOTS + (first + SLOTS + 2 * v + 2))
                    nc.vector.tensor_tensor(hidden[:, bass.ds(i * 2 + v, 1), :].rearrange("p o t -> p (o t)"),
                                            sg[:, v, :], m.bank[2 * v + 1][:, :], ALU.mult)\
                      .then_inc(m.bank_free[2 * v + 1], 1)
            with dve.Fori(0, 2) as i:
                for b in range(4):
                    dve.wait_ge(m.used, i * 12 + (down_first + SLOTS + 3 * b + 3))
                    x = m.x[:, bass.ds(i * 4 + b, 1), :].rearrange("p o t -> p (o t)")
                    nc.vector.scalar_tensor_tensor(out=x, in0=m.bank[b][:, :], scalar=0.5, in1=x,
                                                   op0=ALU.mult, op1=ALU.add).then_inc(m.bank_free[b], 1)
    m.panels = down_first + 3 * DC
    m.fills += 2 * FC + DC


MEM_KEYS_AT = WORK - 2 * MEM_T
MEM_VALUES_AT = WORK - 4 * MEM_T


def head_rms(m, src, dst, gain, chunks, width, at):
    nc = m.nc
    sq = m.cut(at, 4, width)
    root = m.cut(at + 4 * width, 4, width)
    squared = Count(m, "head_squared", chunks)
    summed = Count(m, "head_summed", chunks)
    rooted = Count(m, "head_rooted", chunks)
    scaled = Count(m, "head_scaled", chunks)
    with nc.Block() as block:
        @block.scalar
        def _(act):
            def roots(c):
                act.wait_ge(summed.sem, summed.base + c + 1)
                nc.scalar.activation(root[:, c % 4, :], m.bank[4 + c % 4][:, 0:width], ACT.Sqrt, bias=m.eps,
                                     scale=1.0 / HD).then_inc(rooted.sem, 1)
            for c in range(chunks):
                if c >= 4:
                    act.wait_ge(scaled.sem, scaled.base + c - 3)
                nc.scalar.activation(sq[:, c % 4, :], src(c), ACT.Square).then_inc(squared.sem, 1)
                if c >= 1:
                    roots(c - 1)
            roots(chunks - 1)

        @block.tensor
        def _(pe):
            for c in range(chunks):
                pe.wait_ge(squared.sem, squared.base + c + 1)
                if c >= 4:
                    pe.wait_ge(rooted.sem, rooted.base + c - 3)
                nc.tensor.matmul(m.bank[4 + c % 4][:, 0:width], m.const[:, BLOCK:BLOCK + P], sq[:, c % 4, :],
                                 start=True, stop=True).then_inc(summed.sem, 1)

        @block.vector
        def _(dve):
            for c in range(chunks):
                dve.wait_ge(rooted.sem, rooted.base + c + 1)
                m.vector_order.step(dve, nc.vector.reciprocal(root[:, c % 4, :], root[:, c % 4, :]))
                nc.vector.scalar_tensor_tensor(out=dst(c), in0=src(c), scalar=gain(c), in1=root[:, c % 4, :],
                                               op0=ALU.mult, op1=ALU.mult).then_inc(scaled.sem, 1)


def memory_keys_values(m, io, layer):
    nc = m.nc
    mem = m.cut(0, DC, MEM_T)
    normed = m.cut(DC * MEM_T, DC, MEM_T)
    w = m.cut(2 * DC * MEM_T, DC, 2 * MEM_HEADS * HD)
    scratch = 2 * DC * MEM_T + DC * 2 * MEM_HEADS * HD
    keys = m.cut(MEM_KEYS_AT, 2, MEM_T)
    values = m.cut(MEM_VALUES_AT, 2, MEM_T)
    mem_loaded = Count(m, "memory_loaded", 32)
    done = Count(m, "memory_products", 4)
    with nc.Block() as block:
        @block.sync
        def _(sp):
            sp.dma_start(mem, io["mem"]).then_inc(mem_loaded.sem, 16)
            sp.dma_start(w, io["w_mem_kv"][layer]).then_inc(mem_loaded.sem, 16)
            sp.wait_ge(mem_loaded.sem, mem_loaded.base + 32)
    rms(m, lambda c: mem[:, c, :], lambda c: normed[:, c, :], lambda c: m.v("mem_g", layer * DC + c),
        DC, MEM_T, scratch)
    with nc.Block() as block:
        @block.tensor
        def _(pe):
            for j in range(4):
                for c in range(DC):
                    if j < 2:
                        lhs, rhs = w[:, c, j * P:(j + 1) * P], normed[:, c, :]
                    else:
                        lhs, rhs = normed[:, c, (j - 2) * P:(j - 1) * P], w[:, c, 2 * P:4 * P]
                    ins = nc.tensor.matmul(m.bank[4 + j][:, 0:MEM_T], lhs, rhs, start=(c == 0), stop=(c == DC - 1))
                ins.then_inc(done.sem, 1)

        @block.scalar
        def _(act):
            for j in range(4):
                act.wait_ge(done.sem, done.base + j + 1)
                dst = keys[:, j, :] if j < 2 else values[:, j - 2, :]
                nc.scalar.activation(dst, m.bank[4 + j][:, 0:MEM_T], ACT.Copy)
    head_rms(m, lambda c: keys[:, c, :], lambda c: keys[:, c, :], lambda c: m.v("mem_k", layer), 2, MEM_T, scratch)


class Head:

    def __init__(self, q, k, value, span, bias, group, chunk, off):
        self.q, self.k, self.value, self.span = q, k, value, span
        self.bias, self.group, self.chunk, self.off = bias, group, chunk, off


def memory_heads(m, q, first_group, first_chunk):
    keys = m.cut(MEM_KEYS_AT, 2, MEM_T)
    values = m.cut(MEM_VALUES_AT, 2, MEM_T)
    heads = []
    for h in range(MEM_HEADS):
        c, off = h // 2, HD * (h % 2)
        heads.append(Head(q=lambda t, c=c, off=off: q[off:off + HD, c, t * P:(t + 1) * P],
                          k=lambda a, b, c=c, off=off: keys[off:off + HD, c, a * P:b * P],
                          value=lambda s, h=h: values[:, s, h * HD:(h + 1) * HD],
                          span=lambda t: (0, MEM_T // P), bias=None, group=first_group + h,
                          chunk=first_chunk + c, off=off))
    return heads


def attention(m, heads, groups, at):
    nc = m.nc
    H = len(heads)
    s = m.cut(at, H, T)
    at += H * T
    pt = m.cut(at, 4, T)
    at += 4 * T
    top = m.cut(at, H)
    negtop = m.cut(at + H, groups)
    den = m.cut(at + 2 * H, H)
    inv = m.cut(at + 3 * H, groups)
    N = TT * H
    s_done = Count(m, "att_scores_done", N)
    s_read = Count(m, "att_scores_read", N)
    top_ready = Count(m, "att_top_ready", TT)
    exp_done = Count(m, "att_exp_done", TT)
    p_ready = Count(m, "att_weights_ready", N)
    turned = Count(m, "att_weights_turned", N)
    pt_ready = Count(m, "att_turned_read", N)
    v_done = Count(m, "att_values_done", N // 2)
    v_read = Count(m, "att_values_read", N // 2)
    members = [[h for h in range(H) if heads[h].group == g] for g in range(groups)]
    shared = [g for g in range(groups) if len(members[g]) > 1]
    for g in shared:
        assert members[g] == [g + len(shared) * i for i in range(len(members[g]))]
    with nc.Block() as block:
        @block.tensor
        def _(pe):
            def product(t, h):
                head, g = heads[h], t * H + h
                lo, hi = head.span(t)
                pair = g // 2
                out = m.bank[6 + pair % 2][head.off:head.off + HD, 0:P]
                pe.wait_ge(pt_ready.sem, pt_ready.base + g + 1)
                if head.off == 0 and pair >= 2:
                    pe.wait_ge(v_read.sem, v_read.base + pair - 1)
                for j in range(lo, hi):
                    ins = nc.tensor.matmul(out, head.value(j), pt[:, g % 4, (j - lo) * P:(j - lo + 1) * P],
                                           start=(j == lo), stop=(j == hi - 1))
                if head.off:
                    ins.then_inc(v_done.sem, 1)

            for t in range(TT):
                for h in range(H):
                    head, g = heads[h], t * H + h
                    lo, hi = head.span(t)
                    if g >= 4:
                        pe.wait_ge(s_read.sem, s_read.base + g - 3)
                    nc.tensor.matmul(m.bank[g % 4][:, 0:(hi - lo) * P], head.q(t), head.k(lo, hi),
                                     start=True, stop=True).then_inc(s_done.sem, 1)
                for h in range(H):
                    head, g = heads[h], t * H + h
                    lo, hi = head.span(t)
                    pe.wait_ge(p_ready.sem, p_ready.base + g + 1)
                    if g >= 2:
                        pe.wait_ge(pt_ready.sem, pt_ready.base + g - 1)
                    for j in range(hi - lo):
                        ins = nc.tensor.transpose(m.bank[4 + g % 2][:, j * P:(j + 1) * P],
                                                  s[:, h, j * P:(j + 1) * P], m.const[:, IDENT:IDENT + P])
                    ins.then_inc(turned.sem, 1)
                    if h:
                        product(t, h - 1)
                product(t, H - 1)

        @block.vector
        def _(dve):
            order = m.vector_order
            for t in range(TT):
                for h in range(H):
                    head, g = heads[h], t * H + h
                    lo, hi = head.span(t)
                    dst, src = s[:, h, 0:(hi - lo) * P], m.bank[g % 4][:, 0:(hi - lo) * P]
                    dve.wait_ge(s_done.sem, s_done.base + g + 1)
                    if t:
                        dve.wait_ge(turned.sem, turned.base + g - H + 1)
                    if head.bias is None:
                        ins = nc.vector.tensor_scalar(dst, src, ATT_SCALE, None, ALU.mult)
                    else:
                        ins = nc.vector.scalar_tensor_tensor(out=dst, in0=src, scalar=ATT_SCALE, in1=head.bias(t),
                                                             op0=ALU.mult, op1=ALU.add)
                    ins.then_inc(s_read.sem, 1)
                dve.wait_ge(s_read.sem, s_read.base + (t + 1) * H)
                for h in range(H):
                    lo, hi = heads[h].span(t)
                    ins = nc.vector.reduce_max(top[:, h:h + 1], s[:, h, 0:(hi - lo) * P], AX)
                order.step(dve, ins)
                G, S = len(shared), len(members[0])
                if G:
                    for i in range(1, S):
                        order.step(dve, nc.vector.tensor_tensor(top[:, 0:G], top[:, 0:G], top[:, i * G:(i + 1) * G], ALU.max))
                    nc.vector.tensor_scalar(negtop[:, 0:G], top[:, 0:G], -1.0, None, ALU.mult)
                order.step(dve, nc.vector.tensor_scalar(negtop[:, G:groups], top[:, H - groups + G:H], -1.0, None, ALU.mult))
                dve.sem_inc(top_ready.sem, 1)
                dve.wait_ge(exp_done.sem, exp_done.base + t + 1)
                if G:
                    for i in range(1, S):
                        order.step(dve, nc.vector.tensor_tensor(den[:, 0:G], den[:, 0:G], den[:, i * G:(i + 1) * G], ALU.add))
                    nc.vector.reciprocal(inv[:, 0:G], den[:, 0:G])
                order.step(dve, nc.vector.reciprocal(inv[:, G:groups], den[:, H - groups + G:H]))
                for h in range(H):
                    lo, hi = heads[h].span(t)
                    w = s[:, h, 0:(hi - lo) * P]
                    nc.vector.tensor_scalar(w, w, inv[:, heads[h].group:heads[h].group + 1], None, ALU.mult)\
                      .then_inc(p_ready.sem, 1)

        @block.scalar
        def _(act):
            def values(act, t, h):
                pair = (t * H + h) // 2
                act.wait_ge(v_done.sem, v_done.base + pair + 1)
                nc.scalar.activation(m.n[:, heads[h].chunk, t * P:(t + 1) * P], m.bank[6 + pair % 2][:, 0:P], ACT.Copy)\
                  .then_inc(v_read.sem, 1)

            for t in range(TT):
                act.wait_ge(top_ready.sem, top_ready.base + t + 1)
                for h in range(H):
                    lo, hi = heads[h].span(t)
                    w = s[:, h, 0:(hi - lo) * P]
                    ins = nc.scalar.activation(w, w, ACT.Exp, bias=negtop[:, heads[h].group:heads[h].group + 1],
                                               accum_out=den[:, h:h + 1])
                ins.then_inc(exp_done.sem, 1)
                for h in range(H):
                    head, g = heads[h], t * H + h
                    lo, hi = head.span(t)
                    act.wait_ge(turned.sem, turned.base + g + 1)
                    nc.scalar.activation(pt[:, g % 4, 0:(hi - lo) * P], m.bank[4 + g % 2][:, 0:(hi - lo) * P], ACT.Copy)\
                      .then_inc(pt_ready.sem, 1)
                    if h % 2 and h > 1:
                        values(act, t, h - 2)
                values(act, t, H - 1)



SECOND_SEL, SECOND_MASK = 0, ML_HEADS * P
SECOND_HOT = SECOND_MASK + P
SECOND_COLUMNS = SECOND_HOT + TOEP


def mlstm_layer(m, io):
    nc = m.nc
    at = 0

    def take(*dims):
        nonlocal at
        view = m.cut(at, *dims)
        at += int(np.prod(dims))
        return view

    PAD = T + 4
    QK = 2 * ML_CHUNKS
    pq = take(QK, PAD)
    out_gate = take(ML_CHUNKS, T)
    qm = take(2, T)
    values = take(TT, ML_W)
    qk = take(QK, T)
    wv = take(DC, ML_W + 2 * ML_HEADS)
    rows = take(8, T)
    second = take(SECOND_HOT)
    neg_m = take(T)
    diag = take(TT, P)
    w = take(TT, T)
    dn = take(T)
    ccol = take(TT, ML_HEADS)
    cell = m.cut(0, ML_CHUNKS, T)
    assert at <= MEM_VALUES_AT
    first = m.panels
    side = m.sem("ml_side_loaded")
    evac = m.sem("ml_evacuated")
    padded = m.sem("ml_padded")
    convolved = m.sem("ml_convolved")
    v_done = m.sem("ml_values_done")
    v_read = m.sem("ml_values_read")
    lnf = m.sem("ml_ln_ready")
    sums = m.sem("ml_sums_ready")
    R = ML_HEADS
    i_row, f_row, l_row, one_row, b_row, c_row, m_row, g_row = (rows[0:R, j, :] for j in range(8))
    with nc.Block() as block:
        @block.sync
        def _(sp):
            sp.dma_start(wv, io["a_w_v"]).then_inc(side, 16)
            sp.dma_start(second, io["second"][:, 0:SECOND_HOT]).then_inc(side, 16)
            weight_panels(m, sp, io["a_w_in"], 20)
            sp.wait_ge(side, 32)

        @block.tensor
        def _(pe):
            panel_products(m, pe, 20, lambda c: m.n[:, c, :])
            pe.wait_ge(side, 32)
            HALF = ML_W // 2
            for j in range(10):
                if j >= 4:
                    pe.wait_ge(v_read, j - 3)
                bank = m.bank[4 + j % 4]
                for c in range(DC):
                    if j < 8:
                        t, h = divmod(j, 2)
                        out, lhs, rhs = bank[:, 0:HALF], m.n[:, c, t * P:(t + 1) * P], wv[:, c, h * HALF:(h + 1) * HALF]
                    else:
                        g0 = ML_W + (j - 8) * R
                        out, lhs, rhs = bank[0:R, :], wv[:, c, g0:g0 + R], m.n[:, c, :]
                    ins = nc.tensor.matmul(out, lhs, rhs, start=(c == 0), stop=(c == DC - 1))
                ins.then_inc(v_done, 1)

        @block.scalar
        def _(act):
            order = m.scalar_order
            for j in range(20):
                if j < QK:
                    out, func = pq[:, j, 3:3 + T], ACT.Copy
                elif j < QK + ML_CHUNKS:
                    out, func = out_gate[:, j - QK, :], ACT.Sigmoid
                else:
                    out, func = qm[:, j - QK - ML_CHUNKS, :], ACT.Copy
                act.wait_ge(m.used, first + SLOTS + j + 1)
                order.step(act, nc.scalar.activation(out, m.bank[j % 4][:, :], func))
                act.sem_inc(m.bank_free[j % 4], 1)
                act.sem_inc(evac, 1)
            for j in range(10):
                act.wait_ge(v_done, j + 1)
                bank = m.bank[4 + j % 4]
                if j < 8:
                    t, h = divmod(j, 2)
                    nc.scalar.activation(values[:, t, h * (ML_W // 2):(h + 1) * (ML_W // 2)], bank[:, 0:ML_W // 2],
                                         ACT.Copy).then_inc(v_read, 1)
                else:
                    at_v = VEC["gate_i" if j == 8 else "gate_f"]
                    nc.scalar.activation(i_row if j == 8 else f_row, bank[0:R, :], ACT.Identity,
                                         bias=m.vec[0:R, at_v:at_v + 1]).then_inc(v_read, 1)
            act.wait_ge(v_read, 10)
            order.step(act, nc.scalar.activation(l_row, f_row, ACT.Abs))
            order.step(act, nc.scalar.activation(l_row, l_row, ACT.Exp, scale=-1.0))
            nc.scalar.activation(l_row, l_row, ACT.Ln, bias=1.0).then_inc(lnf, 1)
            act.wait_ge(sums, 1)
            nc.scalar.activation(g_row, g_row, ACT.Exp, scale=-1.0)
            for j in range(QK):
                act.wait_ge(convolved, j // 4 + 1)
                nc.scalar.activation(qk[:, j, :], qk[:, j, :], ACT.Silu)

        @block.vector
        def _(dve):
            order, vec = m.vector_order, nc.vector
            vec.memset(one_row, 1.0)
            order.step(dve, vec.memset(pq[:, :, 0:3], 0.0))
            for b in range(QK // 4):
                dve.wait_ge(evac, 4 * b + 4)
                for tap in range(ML_TAPS):
                    for j in range(4 * b, 4 * b + 4):
                        src, tapw = pq[:, j, tap:tap + T], m.v("a_conv", tap * QK + j)
                        if tap == 0:
                            ins = vec.tensor_scalar(qk[:, j, :], src, tapw, None, ALU.mult)
                        else:
                            ins = vec.scalar_tensor_tensor(out=qk[:, j, :], in0=src, scalar=tapw, in1=qk[:, j, :],
                                                           op0=ALU.mult, op1=ALU.add)
                    if tap < ML_TAPS - 1:
                        order.step(dve, ins)
                ins.then_inc(convolved, 1)
            dve.wait_ge(lnf, 1)
            order.step(dve, vec.tensor_scalar(f_row, f_row, 0.0, None, ALU.min))
            order.step(dve, vec.tensor_tensor(l_row, f_row, l_row, ALU.subtract))
            order.step(dve, vec.tensor_tensor_scan(b_row, one_row, l_row, 0.0, ALU.mult, ALU.add))
            order.step(dve, vec.tensor_tensor(c_row, i_row, b_row, ALU.subtract))
            order.step(dve, vec.tensor_tensor_scan(m_row, one_row, c_row, 0.0, ALU.mult, ALU.max))
            vec.tensor_tensor(g_row, b_row, m_row, ALU.add).then_inc(sums, 1)
    m.panels += 20
    m.fills += 20

    spread = m.sem("ml_rows_spread")
    cols = m.sem("ml_columns_ready")
    scores = m.sem("ml_scores_done")
    negated = m.sem("ml_negated")
    exps = m.sem("ml_exp_done")
    weights = m.sem("ml_weights_ready")
    summed = m.sem("ml_cell_sums")
    absd = m.sem("ml_abs_ready")
    celled = m.sem("ml_cell_ready")
    sel = lambda h: second[0:R, h * P:(h + 1) * P]
    mask = second[:, SECOND_MASK:SECOND_MASK + P]
    COLS, GUARD, DEN = m.bank[7], m.bank[5], m.bank[4]
    NUM = (m.bank[6], m.bank[7])
    with nc.Block() as block:
        @block.tensor
        def _(pe):
            for sb in range(TT):
                ins = nc.tensor.transpose(COLS[:, sb * R:(sb + 1) * R], c_row[:, sb * P:(sb + 1) * P],
                                          m.const[0:R, IDENT:IDENT + R])
            ins.then_inc(cols, 1)
            for h in range(ML_HEADS):
                if h:
                    pe.wait_ge(celled, h)
                nc.tensor.matmul(NUM[0][:, :], sel(h), m_row, start=True, stop=True).then_inc(spread, 1)
                nc.tensor.matmul(GUARD[:, :], sel(h), g_row, start=True, stop=True)
                for sb in range(TT):
                    for i, (c, p0, n) in enumerate(ML_PIECES[h]):
                        ins = nc.tensor.matmul(m.bank[sb][:, 0:T - sb * P],
                                               qk[p0:p0 + n, ML_CHUNKS + c, sb * P:(sb + 1) * P],
                                               qk[p0:p0 + n, c, sb * P:T], start=(i == 0), stop=(i == 1))
                    ins.then_inc(scores, 1)
                pe.wait_ge(negated, h + 1)
                pe.wait_ge(cols, 2)
                for sb in range(TT):
                    pe.wait_ge(weights, h * TT + sb + 1)
                    for i, (c, p0, n) in enumerate(ML_PIECES[h]):
                        f0 = c * P + p0
                        nc.tensor.matmul(NUM[i][p0:p0 + n, sb * P:T], values[:, sb, f0:f0 + n], w[:, sb, 0:T - sb * P],
                                         start=(sb == 0), stop=(sb == TT - 1))
                    ins = nc.tensor.matmul(DEN[:, sb * P:T], m.const[:, ONES:ONES + P], w[:, sb, 0:T - sb * P],
                                           start=(sb == 0), stop=(sb == TT - 1))
                ins.then_inc(summed, 1)

        @block.scalar
        def _(act):
            act.wait_ge(cols, 1)
            m.scalar_order.step(act, nc.scalar.activation(ccol.rearrange("p s h -> p (s h)"), COLS[:, 0:TT * R], ACT.Copy))
            act.sem_inc(cols, 1)
            for h in range(ML_HEADS):
                act.wait_ge(negated, h + 1)
                for sb in range(TT):
                    bias = ccol[:, sb, h:h + 1]
                    ins = nc.scalar.activation(w[:, sb, 0:P], diag[:, sb, :], ACT.Exp, bias=bias)
                    if sb < TT - 1:
                        ins = nc.scalar.activation(w[:, sb, P:T - sb * P], neg_m[:, (sb + 1) * P:T], ACT.Exp, bias=bias)
                    ins.then_inc(exps, 1)
                act.wait_ge(summed, h + 1)
                nc.scalar.activation(dn, DEN[:, :], ACT.Abs).then_inc(absd, 1)

        @block.vector
        def _(dve):
            order, vec = m.vector_order, nc.vector
            for h in range(ML_HEADS):
                dve.wait_ge(spread, h + 1)
                order.step(dve, vec.tensor_scalar(neg_m, NUM[0][:, :], -1.0, None, ALU.mult))
                vec.tensor_tensor(diag, neg_m.rearrange("p (s t) -> p s t", s=TT),
                                  mask.unsqueeze(1).to_broadcast([P, TT, P]), ALU.add).then_inc(negated, 1)
                for sb in range(TT):
                    n = T - sb * P
                    dve.wait_ge(exps, h * TT + sb + 1)
                    dve.wait_ge(scores, h * TT + sb + 1)
                    vec.scalar_tensor_tensor(out=w[:, sb, 0:n], in0=m.bank[sb][:, 0:n], scalar=ML_HD ** -0.5,
                                             in1=w[:, sb, 0:n], op0=ALU.mult, op1=ALU.mult).then_inc(weights, 1)
                dve.wait_ge(absd, h + 1)
                order.step(dve, vec.tensor_tensor(dn, dn, GUARD[:, :], ALU.max))
                order.step(dve, vec.reciprocal(dn, dn))
                for i, (c, p0, n) in enumerate(ML_PIECES[h]):
                    ins = vec.tensor_tensor(cell[p0:p0 + n, c, :], NUM[i][p0:p0 + n, :], dn[p0:p0 + n, :], ALU.mult)
                ins.then_inc(celled, 1)

    sq = m.cut(ML_CHUNKS * T, ML_CHUNKS, T)
    assert 2 * ML_CHUNKS * T <= QK * PAD
    squared = m.sem("ml_squared")
    total = m.sem("ml_norm_sums")
    rooted = m.sem("ml_norm_rooted")
    root = m.cut(QK * PAD + (ML_CHUNKS + 2) * T + TT * ML_W, TT, T)
    with nc.Block() as block:
        @block.scalar
        def _(act):
            for c in range(ML_CHUNKS):
                nc.scalar.activation(sq[:, c, :], cell[:, c, :], ACT.Square).then_inc(squared, 1)
            for h in range(ML_HEADS):
                act.wait_ge(total, h + 1)
                nc.scalar.activation(root[:, h, :], m.bank[h][:, :], ACT.Sqrt, bias=m.eps, scale=1.0 / ML_HD)\
                  .then_inc(rooted, 1)

        @block.tensor
        def _(pe):
            for h in range(ML_HEADS):
                pe.wait_ge(squared, max(c for c, _, _ in ML_PIECES[h]) + 1)
                for i, (c, p0, n) in enumerate(ML_PIECES[h]):
                    ins = nc.tensor.matmul(m.bank[h][:, :], m.const[p0:p0 + n, ONES:ONES + P], sq[p0:p0 + n, c, :],
                                           start=(i == 0), stop=(i == 1))
                ins.then_inc(total, 1)

        @block.vector
        def _(dve):
            order, vec = m.vector_order, nc.vector
            for h in range(ML_HEADS):
                dve.wait_ge(rooted, h + 1)
                order.step(dve, vec.reciprocal(root[:, h, :], root[:, h, :]))
                for c, p0, n in ML_PIECES[h]:
                    g0 = VEC["a_h"] + c
                    ins = vec.scalar_tensor_tensor(out=cell[p0:p0 + n, c, :], in0=cell[p0:p0 + n, c, :],
                                                   scalar=m.vec[p0:p0 + n, g0:g0 + 1], in1=root[p0:p0 + n, h, :],
                                                   op0=ALU.mult, op1=ALU.mult)
            order.step(dve, ins)
            for c in range(ML_CHUNKS):
                vec.tensor_tensor(m.n[:, c, :], cell[:, c, :], out_gate[:, c, :], ALU.mult)

    head_rms(m, lambda c: qm[:, c, :], lambda c: qm[:, c, :], lambda c: m.v("mem_q", 0), 2, T, 0)
    at = QK * PAD + (ML_CHUNKS + 2) * T
    attention(m, memory_heads(m, qm, 0, ML_CHUNKS), MEM_HEADS, at)
    linear_add(m, io["a_w_out"])


KEYS_AT = 12288
VALUES_AT = KEYS_AT + DIL_W // P * T


def shared_keys_values(m, io):
    nc = m.nc
    K6 = DIL_W // P
    w = m.cut(0, DC, 2 * DIL_W)
    keys = m.cut(KEYS_AT, K6, T)
    values = m.cut(VALUES_AT, TT, DIL_W)
    loaded = m.sem("kv_weights_loaded")
    done = m.sem("kv_products")
    read = m.sem("kv_read")
    HALF = DIL_W // 2
    with nc.Block() as block:
        @block.sync
        def _(sp):
            sp.dma_start(w, io["w_kv"]).then_inc(loaded, 16)

        @block.tensor
        def _(pe):
            pe.wait_ge(loaded, 16)
            for j in range(K6 + 2 * TT):
                if j >= 4:
                    pe.wait_ge(read, j - 3)
                for c in range(DC):
                    if j < K6:
                        out, lhs, rhs = m.bank[4 + j % 4][:, :], w[:, c, j * P:(j + 1) * P], m.n[:, c, :]
                    else:
                        t, h = divmod(j - K6, 2)
                        v0 = DIL_W + h * HALF
                        out, lhs, rhs = m.bank[4 + j % 4][:, 0:HALF], m.n[:, c, t * P:(t + 1) * P], w[:, c, v0:v0 + HALF]
                    ins = nc.tensor.matmul(out, lhs, rhs, start=(c == 0), stop=(c == DC - 1))
                ins.then_inc(done, 1)

        @block.scalar
        def _(act):
            for j in range(K6 + 2 * TT):
                act.wait_ge(done, j + 1)
                if j < K6:
                    ins = nc.scalar.activation(keys[:, j, :], m.bank[4 + j % 4][:, :], ACT.Copy)
                else:
                    t, h = divmod(j - K6, 2)
                    ins = nc.scalar.activation(values[:, t, h * HALF:(h + 1) * HALF], m.bank[4 + j % 4][:, 0:HALF], ACT.Copy)
                ins.then_inc(read, 1)
    head_rms(m, lambda c: keys[:, c, :], lambda c: keys[:, c, :], lambda c: m.v("kv_k"), K6, T, 0)


def dilated_layer(m, io):
    nc = m.nc
    K6 = DIL_W // P
    keys = m.cut(KEYS_AT, K6, T)
    values = m.cut(VALUES_AT, TT, DIL_W)
    at = VALUES_AT + TT * DIL_W
    q = m.cut(at, DC, T)
    bias = m.cut(at + DC * T, DIL_HEADS, T)
    hot = m.cut(at + (DC + DIL_HEADS) * T, TOEP)
    table = m.cut(at + (DC + DIL_HEADS) * T + TOEP, DIL_HEADS)
    line = m.cut(at + (DC + DIL_HEADS) * T + TOEP + DIL_HEADS, TOEP)
    assert at + (DC + DIL_HEADS) * T + 2 * TOEP + DIL_HEADS <= MEM_VALUES_AT
    K = BUCKETS + len(DILATIONS)
    first = m.panels
    side = m.sem("dil_side_loaded")
    line_done = m.sem("dil_line_products")
    line_read = m.sem("dil_line_read")
    line_stored = m.sem("dil_line_stored")
    spread = m.sem("dil_bias_spread")
    scratch = io["bias_lines"]
    with nc.Block() as block:
        @block.sync
        def _(sp):
            sp.dma_start(hot[0:K, :], io["second"][0:K, SECOND_HOT:SECOND_COLUMNS]).then_inc(side, 16)
            sp.dma_start(table[0:K, :], io["rel_bias"]).then_inc(side, 16)
            weight_panels(m, sp, io["b_w_q"], DC)

        @block.tensor
        def _(pe):
            pe.wait_ge(side, 32)
            for j in range(2):
                nc.tensor.matmul(m.bank[4 + j][0:DIL_HEADS, 0:TOEP // 2], table[0:K, :],
                                 hot[0:K, j * TOEP // 2:(j + 1) * TOEP // 2], start=True, stop=True)\
                  .then_inc(line_done, 1)
            panel_products(m, pe, DC, lambda c: m.n[:, c, :])

        @block.scalar
        def _(act):
            for j in range(2):
                act.wait_ge(line_done, j + 1)
                nc.scalar.activation(line[0:DIL_HEADS, j * TOEP // 2:(j + 1) * TOEP // 2],
                                     m.bank[4 + j][0:DIL_HEADS, 0:TOEP // 2], ACT.Copy).then_inc(line_read, 1)
            for j in range(DC):
                act.wait_ge(m.used, first + SLOTS + j + 1)
                nc.scalar.activation(q[:, j, :], m.bank[j % 4][:, :], ACT.Copy).then_inc(m.bank_free[j % 4], 1)

        @block.gpsimd
        def _(pool):
            pool.wait_ge(line_read, 2)
            pool.dma_start(scratch, line[0:DIL_HEADS, :].unsqueeze(1).to_broadcast([DIL_HEADS, P, TOEP]))\
                .then_inc(line_stored, 16)
            pool.wait_ge(line_stored, 16)
            for h in range(DIL_HEADS):
                pool.dma_start(bias[:, h, :], bass.AP(scratch.tensor, h * P * TOEP + P - 1, [[TOEP - 1, P], [1, T]]))\
                    .then_inc(spread, 16)
            pool.wait_ge(spread, 16 * DIL_HEADS)
    m.panels += DC
    m.fills += DC
    gain = lambda c: m.v("b_q") if c < K6 else m.v("mem_q", 1)
    head_rms(m, lambda c: q[:, c, :], lambda c: q[:, c, :], gain, DC, T, 0)
    heads = []
    for h in range(DIL_HEADS):
        c, off, g = h // 2, HD * (h % 2), h // DIL_PER_GROUP
        span = (lambda t: (max(t - 1, 0), t + 1)) if g == 0 else (lambda t: (0, t + 1))
        heads.append(Head(
            q=lambda t, c=c, off=off: q[off:off + HD, c, t * P:(t + 1) * P],
            k=lambda a, b, c=c, off=off: keys[off:off + HD, c, a * P:b * P],
            value=lambda s, h=h: values[:, s, h * HD:(h + 1) * HD], span=span,
            bias=lambda t, h=h, span=span: bias[:, h, (TT - 1 - t + span(t)[0]) * P:T],
            group=h % DIL_PER_GROUP, chunk=c, off=off))
    heads += memory_heads(m, q[:, K6:DC, :], DIL_PER_GROUP, K6)
    attention(m, heads, DIL_PER_GROUP + MEM_HEADS, 0)
    linear_add(m, io["b_w_out"])


def store(m, io):
    stored = m.sem("result_stored")
    with m.nc.Block() as block:
        @block.sync
        def _(sp):
            sp.dma_start(io["out"], m.x[:, :, :]).then_inc(stored, 16)
            sp.wait_ge(stored, 16)


def first_block(m, io):
    norm_x(m, "mix_g")
    hybrid_mixer(m, io)
    norm_x(m, "ffn_g")
    route(m, io)
    spread_gates(m, io)
    experts(m, io)
    norm_x(m, "final_g", dst=lambda c: m.x[:, c, :])


def feed_forward(m, io, which, layer):
    norm_x(m, f"ffn{which}_g", layer * DC)
    swiglu(m, io[f"ffn{which}_gate"][layer * FC:(layer + 1) * FC], io[f"ffn{which}_up"][layer * FC:(layer + 1) * FC],
           io[f"ffn{which}_down"][layer * DC:(layer + 1) * DC])


def second_block(m, io):
    feed_forward(m, io, 1, 0)
    memory_keys_values(m, io, 0)
    norm_x(m, "mix2_g", 0)
    mlstm_layer(m, io)
    feed_forward(m, io, 2, 0)
    norm_x(m, "kv_g")
    shared_keys_values(m, io)
    feed_forward(m, io, 1, 1)
    memory_keys_values(m, io, 1)
    norm_x(m, "mix2_g", DC)
    dilated_layer(m, io)
    feed_forward(m, io, 2, 1)


def program(nc, io):
    with ExitStack() as ctx:
        m = Machine(nc, ctx)
        start(m, io)
        first_block(m, io)
        second_block(m, io)
        store(m, io)



def panels(w):
    k, n = w.shape
    return w.reshape(k // P, P, n // P, P).transpose(2, 1, 0, 3).reshape(n // P, P, k)


def by_chunk(w):
    k, n = w.shape
    return w.reshape(k // P, P, n).transpose(1, 0, 2)


def columns(v):
    return np.asarray(v, np.float32).reshape(-1, P).T


def constants():
    c = np.zeros((P, CONST_COLUMNS), np.float32)
    c[:, IDENT:IDENT + P] = np.eye(P)
    c[:, ONES:ONES + P] = 1
    for b in range(P // HD):
        c[b * HD:(b + 1) * HD, BLOCK + b * HD:BLOCK + (b + 1) * HD] = 1
    c[:, COUNT:COUNT + P] = np.arange(P)
    return c


def second_constants():
    c = np.zeros((P, SECOND_COLUMNS), np.float32)
    for h in range(ML_HEADS):
        c[h, SECOND_SEL + h * P:SECOND_SEL + (h + 1) * P] = 1
    s, t = np.arange(P)[:, None], np.arange(P)[None, :]
    c[:, SECOND_MASK:SECOND_MASK + P] = np.where(t >= s, 0, NEG)
    exact = BUCKETS // 2
    for y in range(TOEP):
        d = T - 1 - y
        if d < 0:
            c[BUCKETS:BUCKETS + len(DILATIONS), SECOND_HOT + y] = NEG
            continue
        f = np.float32(max(d, 1))
        large = exact + int(np.log(f / np.float32(exact)) / np.float32(np.log(MAX_DISTANCE / exact)) * np.float32(BUCKETS - exact))
        c[d if d < exact else min(large, BUCKETS - 1), SECOND_HOT + y] = 1
        for g, (window, dilation) in enumerate(DILATIONS):
            if d % dilation or d > window:
                c[BUCKETS + g, SECOND_HOT + y] = NEG
    return c


def layouts(a):
    f = {k: np.asarray(v) for k, v in a.items()}
    io = {"constants": constants(), "second": second_constants()}
    vec = np.zeros((P, VEC_COLUMNS), np.float32)

    def put(name, cols):
        vec[:cols.shape[0], VEC[name]:VEC[name] + cols.shape[1]] = cols

    for name, key in (("mix_g", "mix_norm_g"), ("ffn_g", "ffn_norm_g"), ("final_g", "final_norm_g"),
                      ("ffn1_g", "ffn1_norm_2"), ("ffn2_g", "ffn2_norm_2"), ("mix2_g", "mix_norm_2"),
                      ("mem_g", "mem_norm_2"), ("kv_g", "kv_norm_2"), ("lru_w", "lru_conv_w"),
                      ("lru_b", "lru_conv_b"), ("b_rg", "lru_b_rg"), ("b_ig", "lru_b_ig"),
                      ("lam", "lru_lambda"), ("conf_b", "conf_conv_b"), ("conf_g", "conf_norm_g"),
                      ("conf_nb", "conf_norm_b"), ("beta_lru", "beta_lru"), ("beta_conv", "beta_conv"),
                      ("a_conv", "a_conv_2"), ("a_h", "a_h_norm_2")):
        put(name, columns(f[key]))
    put("conf_w", f["conf_conv_w"][0].reshape(CONF_TAPS, LRU_C4, P).transpose(2, 1, 0).reshape(P, -1))
    for name, key in (("mem_q", "mem_q_norm_2"), ("mem_k", "mem_k_norm_2"), ("b_q", "b_q_norm_2"),
                      ("kv_k", "kv_k_norm_2")):
        g = f[key].reshape(-1, HD)
        put(name, np.concatenate([g, g], axis=1).T)
    put("gate_i", f["a_gate_bias_2"][0, :ML_HEADS].reshape(-1, 1))
    put("gate_f", f["a_gate_bias_2"][0, ML_HEADS:].reshape(-1, 1))
    io["vectors"] = vec
    io["x"] = f["x"][0].T.reshape(DC, P, T).transpose(1, 0, 2)
    io["w_in"] = panels(f["w_in"][0])
    io["w_out"] = panels(f["w_out"][0])
    gates = np.zeros((P, 4 * LRU_C4, P), np.float32)
    for way in range(2):
        for gate, key in enumerate(("lru_w_rg", "lru_w_ig")):
            for h in range(8):
                o = h % 2 * HD
                gates[o:o + HD, (way * 2 + gate) * LRU_C4 + h // 2, o:o + HD] = f[key][0, way, h]
    io["lru_gates"] = gates
    io["w_q"] = panels(f["peer_w_q"][0])
    io["keys"] = f["peer_sub_keys"][0].reshape(HP, KEYS, P).transpose(2, 0, 1)
    io["expert_u"] = f["peer_u"][0].reshape(KEYS, P, DC, P).transpose(0, 3, 2, 1).reshape(KEYS, P, D)
    io["expert_v"] = f["peer_v"][0].reshape(EXPERT_GROUPS, EXPERT_GROUP, P, DC, P).transpose(0, 3, 2, 1, 4)\
        .reshape(KEYS, P, D)
    for which in (1, 2):
        for name in ("gate", "up", "down"):
            w = f[f"ffn{which}_w_{name}_2"]
            io[f"ffn{which}_{name}"] = np.concatenate([panels(w[0]), panels(w[1])])
    io["mem"] = f["mem_2"][0].T.reshape(DC, P, MEM_T).transpose(1, 0, 2)
    io["w_mem_kv"] = np.stack([by_chunk(w) for w in f["w_mem_kv_2"]])
    w = f["a_w_in_2"][0]
    v0, o0, g0 = 2 * ML_W, 3 * ML_W, 4 * ML_W
    m0 = g0 + 2 * ML_HEADS
    io["a_w_in"] = panels(np.concatenate([w[:, :v0], w[:, o0:g0], w[:, m0:]], axis=1))
    io["a_w_v"] = by_chunk(np.concatenate([w[:, v0:o0], w[:, g0:m0]], axis=1))
    io["a_w_out"] = panels(f["a_w_out_2"][0])
    io["w_kv"] = by_chunk(f["w_kv_2"])
    io["b_w_q"] = panels(f["b_w_q_2"][0])
    io["b_w_out"] = panels(f["b_w_out_2"][0])
    pick = np.zeros((len(DILATIONS), DIL_HEADS), np.float32)
    for h in range(DIL_HEADS):
        pick[h // DIL_PER_GROUP, h] = 1
    io["rel_bias"] = np.concatenate([f["rel_bias_2"], pick])
    return {k: np.ascontiguousarray(v) for k, v in io.items()}


def build(nc, shapes):
    io = {}
    for name, (shape, dtype) in shapes.items():
        io[name] = nc.dram_tensor(f"in_{name}", shape, mybir.dt.from_np(dtype), kind="ExternalInput").ap()
    io["out"] = nc.dram_tensor("out", (P, DC, T), FP, kind="ExternalOutput").ap()
    io["gates"] = nc.dram_tensor("expert_gates", (KEYS, P, T), FP).ap()
    io["bias_lines"] = nc.dram_tensor("dilated_bias_lines", (DIL_HEADS, P, TOEP), FP).ap()
    program(nc, io)


def kernel(**inputs):
    import concourse.bacc as bacc
    from concourse.bass_utils import run_bass_kernel_spmd

    nc = bacc.Bacc("TRN2", target_bir_lowering=False, num_devices=1)
    arrays = layouts(inputs)
    build(nc, {k: (v.shape, v.dtype) for k, v in arrays.items()})
    r = run_bass_kernel_spmd(nc, [{f"in_{k}": v for k, v in arrays.items()}], core_ids=[0])
    out = r.results[0]["out"]
    return out.transpose(1, 0, 2).reshape(D, T).T.reshape(1, T, D)
```

```python
from contextlib import ExitStack

import concourse.bass as bass
import numpy as np
from concourse import mybir

FP = mybir.dt.float32
FR = mybir.dt.float32r
U32 = mybir.dt.uint32
ALU = mybir.AluOpType
ACT = mybir.ActivationFunctionType
AX = mybir.AxisListType.X

P = 128
T = 512
D = 1024
DC = D // P
TT = T // P
EPS = 1e-6
NEG = -1e30

LRU_C4 = 4
LRU_TAPS, LRU_LEFT = 4, 2
CONF_TAPS, CONF_LEFT = 31, 15
HEADS, KEYS, TOPK = 8, 128, 16
HP = 2 * HEADS
EXPERT_GROUP = 8
EXPERT_GROUPS = KEYS // EXPERT_GROUP

FF = 2816
FC = FF // P
MEM_T, MEM_HEADS, HD = 256, 4, 64
LAYERS = 2
ATT_SCALE = HD ** -0.5
ML_HEADS, ML_HD = 4, 192
ML_W = ML_HEADS * ML_HD
ML_CHUNKS = ML_W // P
ML_TAPS = 4
DIL_HEADS, DIL_PER_GROUP = 12, 4
DIL_W = DIL_HEADS * HD
DILATIONS = ((128, 1), (512, 4), (2048, 16))
BUCKETS, MAX_DISTANCE = 32, 2048
ML_PIECES = [[(0, 0, 128), (1, 0, 64)], [(1, 64, 64), (2, 0, 128)],
             [(3, 0, 128), (4, 0, 64)], [(4, 64, 64), (5, 0, 128)]]

SLOTS = 4
PANEL = DC * P
PARTS = 2

VEC = {}


def _vec_columns():
    at = 0
    for name, n in (("mix_g", 8), ("ffn_g", 8), ("final_g", 8), ("ffn1_g", 16), ("ffn2_g", 16),
                    ("mix2_g", 16), ("mem_g", 16), ("kv_g", 8), ("lru_w", 16), ("lru_b", 4),
                    ("b_rg", 8), ("b_ig", 8), ("lam", 8), ("conf_w", 124), ("conf_b", 4),
                    ("conf_g", 4), ("conf_nb", 4), ("beta_lru", 4), ("beta_conv", 4),
                    ("a_conv", 48), ("a_h", 6), ("mem_q", 2), ("mem_k", 2), ("b_q", 1),
                    ("kv_k", 1), ("gate_i", 1), ("gate_f", 1)):
        VEC[name] = at
        at += n
    return at


VEC_COLUMNS = _vec_columns()

IDENT, ONES, BLOCK, COUNT = 0, P, 2 * P, 3 * P
CONST_COLUMNS = 4 * P
TOEP = T + P


class Machine:

    def __init__(self, nc, ctx):
        self.nc, self.ctx = nc, ctx
        self.x = self.tensor("residual", DC, T)
        self.n_hi = self.tensor("normed_high", DC, T, dt=FR)
        self.n_lo = self.tensor("normed_low", DC, T, dt=FR)
        self.ring = self.tensor("weight_ring", SLOTS, PANEL)
        self.w_hi = self.tensor("weight_high", PARTS, PANEL, dt=FR)
        self.w_lo = self.tensor("weight_low", PARTS, PANEL, dt=FR)
        self.sum = self.tensor("residual_squares", T)
        self.square = self.tensor("square", 2, T)
        self.const = self.tensor("constants", CONST_COLUMNS)
        self.vec = self.tensor("vectors", VEC_COLUMNS)
        self.bank = [ctx.enter_context(nc.psum_tensor(f"bank{b}", [P, T], FP)) for b in range(8)]
        self.reached = {}
        self.sems = {}
        self.loaded = [self.sem(f"panel_loaded{s}") for s in range(SLOTS)]
        self.high = self.sem("panels_high")
        self.low = self.sem("panels_low")
        self.used = self.sem("panels_used")
        self.bank_free = [self.sem(f"bank_free{b}") for b in range(SLOTS)]
        self.panels = 0
        self.fills = 0
        self.spaces = 0
        self.eps = EPS
        self.hidden = self.sem("hidden_ready")
        self.vector_order = Order(self.sem("vector_order"))
        self.scalar_order = Order(self.sem("scalar_order"))

    def tensor(self, name, *dims, dt=FP, ctx=None):
        return (ctx or self.ctx).enter_context(self.nc.sbuf_tensor(name, [P, *dims], dt))

    def sem(self, name):
        if name not in self.sems:
            self.sems[name] = self.ctx.enter_context(self.nc.semaphore(name))
            self.reached[name] = 0
        return self.sems[name]

    def v(self, name, column=0):
        at = VEC[name] + column
        return self.vec[:, at:at + 1]


class Space:

    def __init__(self, m, ctx, name, floats):
        self.m, self.floats, self.at = m, floats, 0
        m.spaces += 1
        self.region = m.tensor(f"{name}_space{m.spaces}", floats, ctx=ctx)

    def cut(self, at, *dims):
        n = int(np.prod(dims))
        assert at + n <= self.floats, (at, dims)
        flat = self.region[:, at:at + n]
        if len(dims) == 1:
            return flat
        if len(dims) == 2:
            return flat.rearrange("p (a b) -> p a b", a=dims[0])
        return flat.rearrange("p (a b c) -> p a b c", a=dims[0], b=dims[1])

    def take(self, *dims):
        view = self.cut(self.at, *dims)
        self.at += int(np.prod(dims))
        return view


class Scratch:

    def __init__(self, space, at):
        self.space, self.at = space, at

    def cut(self, at, *dims):
        return self.space.cut(self.at + at, *dims)


class Count:

    def __init__(self, m, name, total):
        self.sem, self.base = m.sem(name), m.reached[name] if name in m.reached else 0
        m.reached[name] = self.base + total


class Order:

    def __init__(self, sem):
        self.sem, self.n = sem, 0

    def step(self, eng, ins):
        ins.then_inc(self.sem, 1)
        self.n += 1
        eng.wait_ge(self.sem, self.n)



def low_count(p):
    return p + 1 + SLOTS


def used_count(p):
    return p + 1 + PARTS


def panel(dram, j, width=None, column=0):
    return dram[bass.ds(j, 1), :, column:column + (width or PANEL)].rearrange("o p n -> p (o n)")


def load_panel(m, sp, p, s, source, width=PANEL):
    sp.wait_ge(m.low, low_count(p - SLOTS))
    sp.dma_start(m.ring[:, s, 0:width], source).then_inc(m.loaded[s], 16)


def split_high(m, act, p, s, width=PANEL):
    turn, k = p
    act.wait_ge(m.loaded[s], turn * 16 + 16)
    act.wait_ge(m.used, turn * SLOTS + used_count(k - PARTS))
    m.nc.scalar.activation(m.w_hi[:, s % PARTS, 0:width], m.ring[:, s, 0:width], ACT.Copy).then_inc(m.high, 1)


def split_next(m, act, turn, s, width=PANEL):
    if s + 1 < SLOTS:
        split_high(m, act, (turn, s + 1), s + 1, width)
    else:
        split_high(m, act, (turn + 1, 0), 0, width)


def split_low(m, pool, n, widths=(PANEL,)):
    first = m.panels
    body = len(widths) * SLOTS if len(widths) > 1 else SLOTS
    with pool.Fori(0, n // body) as i:
        for k in range(body):
            s, width = k % SLOTS, widths[k % len(widths)]
            pool.wait_ge(m.high, i * body + (first + k + 1))
            m.nc.gpsimd.tensor_tensor(m.w_lo[:, s % PARTS, 0:width], m.ring[:, s, 0:width],
                                      m.w_hi[:, s % PARTS, 0:width].bitcast(FP), ALU.subtract).then_inc(m.low, 1)


def part_products(m, out, s, chunks, hi, lo, first, last):
    for c in range(chunks):
        w_hi = m.w_hi[:, s % PARTS, c * P:(c + 1) * P]
        w_lo = m.w_lo[:, s % PARTS, c * P:(c + 1) * P]
        m.nc.tensor.matmul(out, w_hi, hi(c), start=(first and c == 0), stop=False)
        m.nc.tensor.matmul(out, w_hi, lo(c), start=False, stop=False)
        ins = m.nc.tensor.matmul(out, w_lo, hi(c), start=False, stop=(last and c == chunks - 1))
    return ins


def n_hi(m):
    return lambda c: m.n_hi[:, c, :]


def n_lo(m):
    return lambda c: m.n_lo[:, c, :]


def weight_panels(m, sp, dram, n, ahead):
    if n > SLOTS:
        with sp.Fori(1, n // SLOTS) as i:
            for s in range(SLOTS):
                load_panel(m, sp, i * SLOTS + (m.panels + s), s, panel(dram, i * SLOTS + s))
    for s, (source, width) in enumerate(ahead):
        load_panel(m, sp, m.panels + n + s, s, source, width)


def panel_products(m, pe, n):
    first, fill0 = m.panels, m.fills // SLOTS
    with pe.Fori(0, n // SLOTS) as i:
        for s in range(SLOTS):
            pe.wait_ge(m.low, i * SLOTS + low_count(first + s))
            pe.wait_ge(m.bank_free[s], i + (fill0 + 1))
            part_products(m, m.bank[s][:, :], s, DC, n_hi(m), n_lo(m), True, True).then_inc(m.used, 1)


def add_squares(m, dve, c):
    x = m.x[:, c, :]
    sq = m.sum if c == 0 else m.square[:, c % 2, :]
    m.vector_order.step(dve, m.nc.vector.tensor_tensor(sq[:, :] if c == 0 else sq, x, x, ALU.mult))
    if c:
        m.vector_order.step(dve, m.nc.vector.tensor_tensor(m.sum[:, :], m.sum[:, :], sq, ALU.add))


def start(m, io, ahead):
    nc = m.nc
    loaded = m.sem("start_loaded")
    x_loaded = [m.sem(f"start_residual_loaded{k}") for k in range(4)]
    with nc.Block() as block:
        @block.sync
        def _(sp):
            sp.dma_start(m.const[:, :], io["constants"]).then_inc(loaded, 16)
            sp.dma_start(m.vec[:, :], io["vectors"]).then_inc(loaded, 16)
            for k in range(4):
                sp.dma_start(m.x[:, 2 * k:2 * k + 2, :], io["x"][:, 2 * k:2 * k + 2, :]).then_inc(x_loaded[k], 16)
            sp.sem_inc(m.low, SLOTS)
            for s, (source, width) in enumerate(ahead):
                load_panel(m, sp, s, s, source, width)
            sp.wait_ge(loaded, 32)

        @block.vector
        def _(dve):
            for c in range(DC):
                if c % 2 == 0:
                    dve.wait_ge(x_loaded[c // 2], 16)
                add_squares(m, dve, c)

        @block.tensor
        def _(pe):
            pe.sem_inc(m.used, PARTS)
            pe.sem_inc(m.hidden, 2)
            for b in range(SLOTS):
                pe.sem_inc(m.bank_free[b], 1)

        @block.scalar
        def _(act):
            split_high(m, act, (0, 0), 0)


def rms(m, src, dst, gain, chunks, width, scratch=None, residual=False):
    nc = m.nc
    sums = 1 if residual else chunks
    squared = Count(m, "norm_squared", 0 if residual else chunks)
    summed = Count(m, "norm_summed", sums)
    rooted = Count(m, "norm_rooted", 1)
    scaled = Count(m, "norm_scaled", chunks)
    high = Count(m, "norm_high", chunks)
    total = m.bank[7]
    with ExitStack() as ctx:
        space = scratch or Space(m, ctx, "norm", 10 * width)
        sq, out = space.cut(0, 4, width), space.cut(0, 8, width)
        root, inv = space.cut(8 * width, width), space.cut(9 * width, width)
        with nc.Block() as block:
            @block.scalar
            def _(act):
                for c in range(0 if residual else chunks):
                    if c >= 4:
                        act.wait_ge(summed.sem, summed.base + c - 3)
                    nc.scalar.activation(sq[:, c % 4, :], src(c), ACT.Square).then_inc(squared.sem, 1)
                act.wait_ge(summed.sem, summed.base + sums)
                nc.scalar.activation(root, total[:, 0:width], ACT.Sqrt, bias=m.eps,
                                     scale=1.0 / (chunks * P)).then_inc(rooted.sem, 1)
                if not callable(dst):
                    input_high(m, act, chunks, lambda c: out[:, c, :], dst, scaled, high)
                elif residual:
                    for c in range(chunks):
                        act.wait_ge(scaled.sem, scaled.base + c + 1)
                        nc.scalar.activation(out[:, c, :], src(c), ACT.Square).then_inc(high.sem, 1)

            @block.tensor
            def _(pe):
                if residual:
                    nc.tensor.matmul(total[:, 0:width], m.const[:, ONES:ONES + P], m.sum[:, :],
                                     start=True, stop=True).then_inc(summed.sem, 1)
                for c in range(0 if residual else chunks):
                    pe.wait_ge(squared.sem, squared.base + c + 1)
                    nc.tensor.matmul(total[:, 0:width], m.const[:, ONES:ONES + P], sq[:, c % 4, :],
                                     start=(c == 0), stop=(c == chunks - 1)).then_inc(summed.sem, 1)

            @block.gpsimd
            def _(pool):
                if not callable(dst):
                    input_low(m, pool, nc.gpsimd, range(0, chunks, 2), lambda c: out[:, c, :], dst, high)

            @block.vector
            def _(dve):
                dve.wait_ge(rooted.sem, rooted.base + 1)
                m.vector_order.step(dve, nc.vector.reciprocal(inv, root))
                for c in range(chunks):
                    nc.vector.scalar_tensor_tensor(out=dst(c) if callable(dst) else out[:, c, :], in0=src(c),
                                                   scalar=gain(c), in1=inv, op0=ALU.mult, op1=ALU.mult)\
                      .then_inc(scaled.sem, 1)
                if not callable(dst):
                    input_low(m, dve, nc.vector, range(1, chunks, 2), lambda c: out[:, c, :], dst, high)
                elif residual:
                    dve.wait_ge(high.sem, high.base + 2)
                    m.vector_order.step(dve, nc.vector.tensor_tensor(m.sum[:, :], out[:, 0, :], out[:, 1, :], ALU.add))
                    for c in range(2, chunks):
                        dve.wait_ge(high.sem, high.base + c + 1)
                        m.vector_order.step(dve, nc.vector.tensor_tensor(m.sum[:, :], m.sum[:, :], out[:, c, :], ALU.add))
    if callable(dst) and not residual:
        m.reached["norm_high"] -= chunks


def input_high(m, act, chunks, value, dst, scaled, high):
    for c in range(chunks):
        act.wait_ge(scaled.sem, scaled.base + c + 1)
        m.nc.scalar.activation(m.n_hi[:, dst + c, :], value(c), ACT.Copy).then_inc(high.sem, 1)


def input_low(m, eng, ops, chunks, value, dst, high):
    for c in chunks:
        eng.wait_ge(high.sem, high.base + c + 1)
        ops.tensor_tensor(m.n_lo[:, dst + c, :], value(c), m.n_hi[:, dst + c, :].bitcast(FP), ALU.subtract)


def norm_x(m, name, column=0, dst=0):
    rms(m, lambda c: m.x[:, c, :], dst, lambda c: m.v(name, column + c), DC, T, residual=True)


def linear_add(m, dram, ahead):
    nc = m.nc
    first, turn0 = m.panels, m.panels // SLOTS
    with nc.Block() as block:
        @block.sync
        def _(sp):
            weight_panels(m, sp, dram, DC, ahead)

        @block.gpsimd
        def _(pool):
            split_low(m, pool, DC)

        @block.scalar
        def _(act):
            for c in range(DC):
                split_next(m, act, turn0 + c // SLOTS, c % SLOTS)

        @block.tensor
        def _(pe):
            panel_products(m, pe, DC)

        @block.vector
        def _(dve):
            for c in range(DC):
                dve.wait_ge(m.used, used_count(first + c))
                m.vector_order.step(dve, nc.vector.tensor_tensor(m.x[:, c, :], m.x[:, c, :], m.bank[c % 4][:, :], ALU.add))
                dve.sem_inc(m.bank_free[c % 4], 1)
                add_squares(m, dve, c)
    m.panels += DC
    m.fills += DC


def hybrid_mixer(m, io, ahead):
    with ExitStack() as ctx:
        space = Space(m, ctx, "hybrid", 29904)
        lru, conv = hybrid_branches(m, io, space, panels_ahead(io["w_out"]))
        rms(m, lambda c: lru[:, c, :], 0, lambda c: m.v("beta_lru", c), LRU_C4, T, space)
        rms(m, lambda c: conv[:, c, :], LRU_C4, lambda c: m.v("beta_conv", c), LRU_C4, T, space)
    linear_add(m, io["w_out"], ahead)


def hybrid_branches(m, io, space, ahead):
    nc = m.nc
    C4 = LRU_C4
    take = space.take
    XPAD = T + 4
    GPAD = T + 32
    x_pad = take(C4, XPAD)
    g_gelu = take(C4, T)
    glu_pad = take(C4, GPAD)
    gate_w = take(4 * C4, P)
    xc = take(C4, T)
    tanh = take(2 * C4, T)
    gate_i = take(2 * C4, T)
    root = take(2 * C4, T)
    inv = take(2 * C4, T)
    conv = take(C4, T)
    lam = take(8, 8)
    DIAGS = 8
    diag = take(DIAGS, P)
    b_sig = conv

    side = m.sem("mix_side_loaded")
    first = m.panels
    in_evac = m.sem("mix_in_evacuated")
    lam_exp = m.sem("mix_lambda_exp")
    lam_done = m.sem("mix_lambda_done")
    xc_ready = m.sem("mix_xc_ready")
    glu_ready = m.sem("mix_glu_ready")
    gate_done = m.sem("mix_gate_products")
    gate_evac = m.sem("mix_gates_evacuated")
    tanh_done = m.sem("mix_tanh_done")
    root_done = m.sem("mix_root_done")
    diag_ready = m.sem("mix_diag_ready")
    diag_used = m.sem("mix_diag_used")
    conv_done = m.sem("mix_conv_evacuated")
    V = m.v
    with nc.Block() as block:
        @block.sync
        def _(sp):
            sp.dma_start(gate_w, io["lru_gates"]).then_inc(side, 16)
            weight_panels(m, sp, io["w_in"], 4 * C4, ahead)
            sp.wait_ge(side, 16)

        @block.gpsimd
        def _(pool):
            split_low(m, pool, 4 * C4)
            for k in range((C4 - 1) * CONF_TAPS):
                if k >= DIAGS:
                    pool.wait_ge(diag_used, k - DIAGS + 1)
                nc.gpsimd.tensor_scalar(diag[:, k % DIAGS, :], m.const[:, IDENT:IDENT + P],
                                        V("conf_w", k), None, ALU.mult).then_inc(diag_ready, 1)

        @block.tensor
        def _(pe):
            panel_products(m, pe, 4 * C4)
            pe.wait_ge(side, 16)
            pe.wait_ge(xc_ready, C4)
            for j in range(4 * C4):
                gate, way, c = j // (2 * C4), j // C4 % 2, j % C4
                if j >= 4:
                    pe.wait_ge(gate_evac, j - 3)
                else:
                    pe.wait_ge(in_evac, 4 * C4)
                nc.tensor.matmul(m.bank[j % 4][:, :], gate_w[:, (way * 2 + gate) * C4 + c, :], xc[:, c, :],
                                 start=True, stop=True).then_inc(gate_done, 1)
            pe.wait_ge(glu_ready, C4)
            for k in range((C4 - 1) * CONF_TAPS):
                c, tap = divmod(k, CONF_TAPS)
                pe.wait_ge(diag_ready, k + 1)
                nc.tensor.matmul(m.bank[4 + c][:, :], diag[:, k % DIAGS, :], glu_pad[:, c, tap:tap + T],
                                 start=(tap == 0), stop=(tap == CONF_TAPS - 1)).then_inc(diag_used, 1)

        @block.scalar
        def _(act):
            order = m.scalar_order
            order.step(act, nc.scalar.activation(lam[:, 0, :], m.vec[:, VEC["lam"]:VEC["lam"] + 8], ACT.Abs))
            nc.scalar.activation(lam[:, 1, :], lam[:, 0, :], ACT.Exp, scale=-1.0).then_inc(lam_exp, 1)
            kinds = [(x_pad, ACT.Copy, LRU_LEFT), (g_gelu, ACT.Gelu_apprx_tanh, 0), (glu_pad, ACT.Copy, CONF_LEFT),
                     (b_sig, ACT.Sigmoid, 0)]
            for j in range(4 * C4):
                dst, func, left = kinds[j // C4]
                out = dst[:, j % C4, left:left + T]
                split_next(m, act, first // SLOTS + j // SLOTS, j % SLOTS)
                act.wait_ge(m.used, used_count(first + j))
                order.step(act, nc.scalar.activation(out, m.bank[j % 4][:, :], func))
                act.sem_inc(m.bank_free[j % 4], 1)
                act.sem_inc(in_evac, 1)
            for j in range(4 * C4):
                gate, way, c = j // (2 * C4), j // C4 % 2, j % C4
                act.wait_ge(gate_done, j + 1)
                dst = tanh if gate == 0 else gate_i
                bias = V("b_rg" if gate == 0 else "b_ig", way * C4 + c)
                nc.scalar.activation(dst[:, way * C4 + c, :], m.bank[j % 4][:, :], ACT.Sigmoid, bias=bias)\
                  .then_inc(gate_evac, 1)
            act.wait_ge(lam_done, 1)
            act.wait_ge(gate_evac, 4 * C4)
            for w in range(2 * C4):
                nc.scalar.activation(tanh[:, w, :], tanh[:, w, :], ACT.Tanh, scale=lam[:, 7, w:w + 1])\
                  .then_inc(tanh_done, 1)
            act.wait_ge(tanh_done, 2 * C4)
            for w in range(2 * C4):
                nc.scalar.activation(root[:, w, :], tanh[:, w, :], ACT.Sqrt, scale=4.0).then_inc(root_done, 1)
            act.wait_ge(glu_ready, C4)
            for c in range(C4 - 1):
                act.wait_ge(diag_used, (c + 1) * CONF_TAPS)
                nc.scalar.activation(conv[:, c, :], m.bank[4 + c][:, :], ACT.Identity, bias=V("conf_b", c))\
                  .then_inc(conv_done, 1)

        @block.vector
        def _(dve):
            order = m.vector_order
            vec = nc.vector
            vec.memset(x_pad[:, :, 0:LRU_LEFT], 0.0)
            vec.memset(x_pad[:, :, LRU_LEFT + T:XPAD], 0.0)
            vec.memset(glu_pad[:, :, 0:CONF_LEFT], 0.0)
            order.step(dve, vec.memset(glu_pad[:, :, CONF_LEFT + T:GPAD], 0.0))
            dve.wait_ge(lam_exp, 1)
            e, z, z2, p, neg = (lam[:, i, :] for i in (1, 2, 3, 4, 5))
            order.step(dve, vec.tensor_scalar(z, e, 2.0, None, ALU.add))
            order.step(dve, vec.reciprocal(z, z))
            order.step(dve, vec.tensor_tensor(z, z, e, ALU.mult))
            order.step(dve, vec.tensor_tensor(z2, z, z, ALU.mult))
            order.step(dve, vec.tensor_scalar(p, z2, 1.0 / 17, None, ALU.mult))
            for k in (15, 13, 11, 9, 7, 5, 3):
                order.step(dve, vec.scalar_tensor_tensor(out=p, in0=p, scalar=1.0 / k, in1=z2, op0=ALU.add, op1=ALU.mult))
            order.step(dve, vec.scalar_tensor_tensor(out=p, in0=p, scalar=1.0, in1=z, op0=ALU.add, op1=ALU.mult))
            order.step(dve, vec.tensor_scalar(neg, m.vec[:, VEC["lam"]:VEC["lam"] + 8], -1.0, 0.0, ALU.mult, ALU.max))
            order.step(dve, vec.scalar_tensor_tensor(out=p, in0=p, scalar=2.0, in1=neg, op0=ALU.mult, op1=ALU.add))
            vec.tensor_scalar(lam[:, 7, :], p, 4.0, None, ALU.mult).then_inc(lam_done, 1)
            dve.wait_ge(in_evac, C4)
            for tap in range(LRU_TAPS):
                for c in range(C4):
                    src, w = x_pad[:, c, tap:tap + T], V("lru_w", tap * C4 + c)
                    if tap == 0:
                        ins = vec.tensor_scalar(xc[:, c, :], src, w, V("lru_b", c), ALU.mult, ALU.add)
                    else:
                        ins = vec.scalar_tensor_tensor(out=xc[:, c, :], in0=src, scalar=w, in1=xc[:, c, :],
                                                       op0=ALU.mult, op1=ALU.add)
                    if tap == LRU_TAPS - 1:
                        ins.then_inc(xc_ready, 1)
                    elif c == C4 - 1:
                        order.step(dve, ins)
            for c in range(C4):
                dve.wait_ge(in_evac, 3 * C4 + c + 1)
                glu = glu_pad[:, c, CONF_LEFT:CONF_LEFT + T]
                vec.tensor_tensor(glu, glu, b_sig[:, c, :], ALU.mult).then_inc(glu_ready, 1)
            dve.wait_ge(xc_ready, C4)
            for w in range(2 * C4):
                dve.wait_ge(tanh_done, w + 1)
                order.step(dve, vec.tensor_scalar(inv[:, w, :], tanh[:, w, :], 1.0, None, ALU.add))
                order.step(dve, vec.reciprocal(inv[:, w, :], inv[:, w, :]))
                vec.tensor_tensor(gate_i[:, w, :], gate_i[:, w, :], xc[:, w % C4, :], ALU.mult)
                dve.wait_ge(root_done, w + 1)
                vec.tensor_scalar(tanh[:, w, :], inv[:, w, :], 2.0, -1.0, ALU.mult, ALU.add)
                order.step(dve, vec.tensor_tensor(root[:, w, :], root[:, w, :], inv[:, w, :], ALU.mult))
                order.step(dve, vec.tensor_tensor(root[:, w, :], root[:, w, :], gate_i[:, w, :], ALU.mult))
                if w < C4:
                    ins = vec.tensor_tensor_scan(inv[:, w, :], tanh[:, w, :], root[:, w, :], 0.0, ALU.mult, ALU.add)
                else:
                    ins = vec.tensor_tensor_scan(inv[:, w, ::-1], tanh[:, w, ::-1], root[:, w, ::-1], 0.0,
                                                 ALU.mult, ALU.add)
            order.step(dve, ins)
            for c in range(C4):
                ins = vec.tensor_tensor(inv[:, c, :], inv[:, c, :], inv[:, C4 + c, :], ALU.add)
            order.step(dve, ins)
            for c in range(C4):
                vec.tensor_tensor(inv[:, c, :], inv[:, c, :], g_gelu[:, c, :], ALU.mult)
            dve.wait_ge(glu_ready, C4)
            c = C4 - 1
            for tap in range(CONF_TAPS):
                src, w = glu_pad[:, c, tap:tap + T], V("conf_w", c * CONF_TAPS + tap)
                if tap == 0:
                    ins = vec.tensor_scalar(conv[:, c, :], src, w, V("conf_b", c), ALU.mult, ALU.add)
                else:
                    ins = vec.scalar_tensor_tensor(out=conv[:, c, :], in0=src, scalar=w, in1=conv[:, c, :],
                                                   op0=ALU.mult, op1=ALU.add)
                order.step(dve, ins)
    m.panels += 4 * C4
    m.fills += 4 * C4

    sq, std = tanh, gate_i
    averaged = m.sem("gln_averaged")
    centred = m.sem("gln_centred")
    squared = m.sem("gln_squared")
    summed = m.sem("gln_summed")
    rooted = m.sem("gln_rooted")
    scaled = m.sem("gln_scaled")
    with nc.Block() as block:
        @block.tensor
        def _(pe):
            for c in range(C4):
                nc.tensor.matmul(m.bank[c][:, :], m.const[:, BLOCK:BLOCK + P], conv[:, c, :],
                                 start=True, stop=True).then_inc(averaged, 1)
            for c in range(C4):
                pe.wait_ge(squared, c + 1)
                nc.tensor.matmul(m.bank[4 + c][:, :], m.const[:, BLOCK:BLOCK + P], sq[:, c, :],
                                 start=True, stop=True).then_inc(summed, 1)

        @block.vector
        def _(dve):
            for c in range(C4):
                dve.wait_ge(averaged, c + 1)
                nc.vector.scalar_tensor_tensor(out=conv[:, c, :], in0=m.bank[c][:, :], scalar=-1.0 / HD,
                                               in1=conv[:, c, :], op0=ALU.mult, op1=ALU.add).then_inc(centred, 1)
            for c in range(C4):
                dve.wait_ge(rooted, c + 1)
                m.vector_order.step(dve, nc.vector.reciprocal(std[:, c, :], std[:, c, :]))
                nc.vector.tensor_tensor(std[:, c, :], std[:, c, :], conv[:, c, :], ALU.mult).then_inc(scaled, 1)

        @block.scalar
        def _(act):
            for c in range(C4):
                act.wait_ge(centred, c + 1)
                nc.scalar.activation(sq[:, c, :], conv[:, c, :], ACT.Square).then_inc(squared, 1)
            for c in range(C4):
                act.wait_ge(summed, c + 1)
                nc.scalar.activation(std[:, c, :], m.bank[4 + c][:, :], ACT.Sqrt, bias=m.eps, scale=1.0 / HD)\
                  .then_inc(rooted, 1)
            for c in range(C4):
                act.wait_ge(scaled, c + 1)
                nc.scalar.activation(conv[:, c, :], std[:, c, :], ACT.Silu, bias=V("conf_nb", c),
                                     scale=V("conf_g", c))
    return inv, conv


ROUTE_GROUPS = 5
SPREAD_GROUPS = 4
LATE_GROUPS = 1
PARKED = ROUTE_GROUPS + SPREAD_GROUPS + LATE_GROUPS
SPREAD_T = 64


def panels_ahead(dram, at=0, widths=(PANEL,) * SLOTS):
    return [(panel(dram, at + s, w), w) for s, w in enumerate(widths)]


def activate(m, act, buffers, turn, s, u_turn, activated, stored):
    split_next(m, act, turn, s)
    act.wait_ge(m.used, turn * SLOTS + used_count(s))
    act.wait_ge(stored[s], turn * 16 + 16 * (1 - u_turn))
    m.nc.scalar.activation(buffers[:, s, :], m.bank[s][:, :], ACT.Gelu_apprx_tanh).then_inc(activated, 1)
    act.wait_ge(activated, turn * SLOTS + (s + 1 - u_turn * SLOTS))
    act.sem_inc(m.bank_free[s], 1)


def route(m, io, found):
    nc = m.nc
    first = m.panels
    u_first = first + HP
    U = ROUTE_GROUPS * EXPERT_GROUP
    side = m.sem("route_keys_loaded")
    q_ready = m.sem("route_q_ready")
    s_done = m.sem("route_scores_done")
    s_evac = m.sem("route_scores_evacuated")
    activated = m.sem("parked_activated")
    stored = [m.sem(f"parked_stored{s}") for s in range(SLOTS)]
    NEVER = -3.0e38
    with ExitStack() as ctx:
        space = Space(m, ctx, "route", 28000)
        take = space.take
        q = take(HP, T)
        keys = take(HP, KEYS)
        s = take(TT * HP, KEYS)
        s2 = take(HP, KEYS)
        cand = take(HEADS, TOPK * TOPK)
        cand2 = keys.rearrange("p (h a) k -> p h (a k)", a=2)
        hot = s2.rearrange("p (h a) (b k) -> p (h a b) k", a=1, k=TOPK)
        top = take(HP, TOPK)
        idx = take(HP, TOPK).bitcast(U32)
        idxf = take(HP, TOPK)
        ts = take(HEADS, TOPK)
        pos = take(HEADS, TOPK).bitcast(U32)
        part = take(2, HEADS * TOPK).bitcast(U32)
        partf = take(2, HEADS * TOPK)
        buffers = take(SLOTS, T)
        with nc.Block() as block:
            @block.sync
            def _(sp):
                sp.dma_start(keys, io["keys"]).then_inc(side, 16)
                weight_panels(m, sp, io["w_q"], HP, panels_ahead(io["experts"]))
                with sp.Fori(0, U // SLOTS) as i:
                    for k in range(SLOTS):
                        load_panel(m, sp, i * SLOTS + (u_first + SLOTS + k), k, panel(io["experts"], i * SLOTS + SLOTS + k))
                        sp.wait_ge(activated, i * SLOTS + k + 1)
                        sp.dma_start(panel(io["parked"], i * SLOTS + k, T), buffers[:, k, :]).then_inc(stored[k], 16)
                sp.wait_ge(side, 16)

            @block.gpsimd
            def _(pool):
                for k in range(SLOTS):
                    pool.sem_inc(stored[k], 16)
                split_low(m, pool, HP + U)

            @block.tensor
            def _(pe):
                panel_products(m, pe, HP)
                pe.wait_ge(side, 16)
                pe.wait_ge(q_ready, HP)
                for k in range(4 * TT):
                    t, b = divmod(k, 4)
                    if t:
                        pe.wait_ge(s_evac, k - 3)
                    for j in range(4 * b, 4 * b + 4):
                        ins = nc.tensor.matmul(m.bank[4 + b][:, (j % 4) * P:(j % 4 + 1) * P],
                                               q[:, j, t * P:(t + 1) * P], keys[:, j, :], start=(j % 4 == 0),
                                               stop=(j % 4 == 3), skip_group_check=True)
                    ins.then_inc(s_done, 1)
                m.panels, m.fills = m.panels + HP, m.fills + HP
                panel_products(m, pe, U)
                m.panels, m.fills = m.panels - HP, m.fills - HP

            @block.scalar
            def _(act):
                for j in range(HP):
                    split_next(m, act, first // SLOTS + j // SLOTS, j % SLOTS)
                    act.wait_ge(m.used, used_count(first + j))
                    m.scalar_order.step(act, nc.scalar.activation(q[:, j, :], m.bank[j % 4][:, :], ACT.Copy))
                    act.sem_inc(m.bank_free[j % 4], 1)
                    act.sem_inc(q_ready, 1)
                for k in range(4 * TT):
                    act.wait_ge(s_done, k + 1)
                    nc.scalar.activation(s[:, 4 * k:4 * k + 4, :].rearrange("p a b -> p (a b)"),
                                         m.bank[4 + k % 4][:, :], ACT.Copy).then_inc(s_evac, 1)
                with act.Fori(0, U // SLOTS) as i:
                    for k in range(SLOTS):
                        activate(m, act, buffers, i + u_first // SLOTS, k, u_first // SLOTS, activated, stored)

            @block.vector
            def _(dve):
                order, vec = m.vector_order, nc.vector
                count16 = m.const[:, COUNT:COUNT + TOPK]
                for t in range(TT):
                    dve.wait_ge(s_evac, 4 * TT if t == 0 else 4 * t + 4)
                    st = s[:, t * HP:(t + 1) * HP, :]
                    for j in range(HP):
                        ins = vec.max(top[:, j, 0:8], st[:, j, :])
                    order.step(dve, ins)
                    for j in range(HP):
                        vec.max_index(idx[:, j, 0:8], top[:, j, 0:8], st[:, j, :])
                        ins = vec.match_replace(s2[:, j, :], top[:, j, 0:8], st[:, j, :], NEVER)
                    order.step(dve, ins)
                    for j in range(HP):
                        ins = vec.max(top[:, j, 8:16], s2[:, j, :])
                    order.step(dve, ins)
                    for j in range(HP):
                        ins = vec.max_index(idx[:, j, 8:16], top[:, j, 8:16], s2[:, j, :])
                    halves = top.rearrange("p (h w) k -> p h w k", w=2)
                    order.step(dve, vec.tensor_tensor(
                        cand.rearrange("p h (a b) -> p h a b", a=TOPK),
                        halves[:, :, 0, :].unsqueeze(3).to_broadcast([P, HEADS, TOPK, TOPK]),
                        halves[:, :, 1, :].unsqueeze(2).to_broadcast([P, HEADS, TOPK, TOPK]), ALU.add))
                    vec.tensor_copy(idxf, idx)
                    for h in range(HEADS):
                        ins = vec.max(ts[:, h, 0:8], cand[:, h, :])
                    order.step(dve, ins)
                    for h in range(HEADS):
                        vec.max_index(pos[:, h, 0:8], ts[:, h, 0:8], cand[:, h, :])
                        ins = vec.match_replace(cand2[:, h, :], ts[:, h, 0:8], cand[:, h, :], NEVER)
                    order.step(dve, ins)
                    for h in range(HEADS):
                        ins = vec.max(ts[:, h, 8:16], cand2[:, h, :])
                    order.step(dve, ins)
                    for h in range(HEADS):
                        vec.max_index(pos[:, h, 8:16], ts[:, h, 8:16], cand2[:, h, :])
                    base = found[:, t, :]
                    order.step(dve, vec.tensor_tensor(base[:, 2 * P:3 * P].rearrange("p (h k) -> p h k", h=HEADS), ts,
                                                      ts[:, :, 0:1].to_broadcast([P, HEADS, TOPK]), ALU.subtract))
                    flat = pos.rearrange("p h k -> p (h k)")
                    vec.tensor_scalar(part[:, 0, :], flat, 4, None, ALU.logical_shift_right)
                    order.step(dve, vec.tensor_scalar(part[:, 1, :], flat, TOPK - 1, None, ALU.bitwise_and))
                    order.step(dve, vec.tensor_copy(partf, part))
                    index = idxf.rearrange("p (h w) k -> p h w k", w=2)
                    hots = hot.rearrange("p (h k) a -> p h k a", h=HEADS)
                    for w in range(2):
                        order.step(dve, vec.tensor_tensor(
                            hot, partf[:, w, :].unsqueeze(2).to_broadcast([P, HEADS * TOPK, TOPK]),
                            count16.unsqueeze(1).to_broadcast([P, HEADS * TOPK, TOPK]), ALU.is_equal))
                        order.step(dve, vec.tensor_tensor(
                            hots, hots, index[:, :, w, :].unsqueeze(2).to_broadcast([P, HEADS, TOPK, TOPK]), ALU.mult))
                        order.step(dve, vec.tensor_reduce(base[:, w * P:(w + 1) * P], hot, AX, ALU.add))
    m.panels += HP + U
    m.fills += HP + U


def spread_gates(m, io, found):
    nc = m.nc
    first, turn0, fill0 = m.panels, m.panels // SLOTS, m.fills // SLOTS
    U0 = ROUTE_GROUPS * EXPERT_GROUP
    U = SPREAD_GROUPS * EXPERT_GROUP
    BATCH = 4
    BATCHES = 4
    assert U * BATCH * BATCHES == T and SPREAD_T == SLOTS * BATCH * BATCHES
    activated = m.sem("parked_activated")
    stored = [m.sem(f"parked_stored{s}") for s in range(SLOTS)]
    rows_ready = m.sem("spread_rows_ready")
    done = m.sem("spread_products")
    evac = m.sem("spread_evacuated")
    gate_stored = [m.sem(f"spread_stored{h}") for h in range(2)]
    expd = m.sem("spread_exp")
    gated = m.sem("spread_softmax")
    turned = m.sem("spread_turned")
    gt_ready = m.sem("spread_turned_read")
    count = m.const[:, COUNT:COUNT + P]
    G = io["gates"].rearrange("g p t n -> p g t n")
    with ExitStack() as ctx:
        space = Space(m, ctx, "spread", 2 * KEYS * SPREAD_T + 4 * BATCH * P + 3 * T + SLOTS * T + TT * HEADS)
        stage = [space.take(KEYS, SPREAD_T) for h in range(2)]
        rows2, rows1 = space.take(2, BATCH * P), space.take(2, BATCH * P)
        gt = space.take(3, T)
        buffers = space.take(SLOTS, T)
        total = space.take(TT, HEADS)
        with nc.Block() as block:
            @block.vector
            def _(dve):
                dve.wait_ge(expd, 1)
                e = found[:, :, 2 * P:3 * P].rearrange("p t (h k) -> p t h k", h=HEADS)
                m.vector_order.step(dve, nc.vector.tensor_reduce(total, e, AX, ALU.add))
                m.vector_order.step(dve, nc.vector.reciprocal(total, total))
                nc.vector.tensor_tensor(e, e, total.unsqueeze(3).to_broadcast([P, TT, HEADS, TOPK]), ALU.mult)\
                  .then_inc(gated, 1)
                dve.sem_inc(done, 2)
                dve.wait_ge(gt_ready, 1)
                with dve.Fori(0, T // BATCH // 2) as i:
                    for h in range(2):
                        dve.wait_ge(done, i * 2 + h + 1)
                        for u in range(BATCH):
                            t = i * (2 * BATCH) + (h * BATCH + u)
                            nc.vector.tensor_scalar(rows2[:, h, u * P:(u + 1) * P], count,
                                                    gt[:, 1, bass.ds(t, 1)], None, ALU.is_equal)
                            ins = nc.vector.tensor_scalar(rows1[:, h, u * P:(u + 1) * P], count,
                                                          gt[:, 0, bass.ds(t, 1)], gt[:, 2, bass.ds(t, 1)],
                                                          ALU.is_equal, ALU.mult)
                        ins.then_inc(rows_ready, 1)

            @block.gpsimd
            def _(pool):
                for h in range(2):
                    pool.sem_inc(gate_stored[h], 16)
                split_low(m, pool, U)

            @block.tensor
            def _(pe):
                pe.sem_inc(evac, BATCHES)
                pe.wait_ge(gated, 1)
                for t in range(TT):
                    for w in range(3):
                        ins = nc.tensor.transpose(m.bank[4 + w][:, t * P:(t + 1) * P],
                                                  found[:, t, w * P:(w + 1) * P], m.const[:, IDENT:IDENT + P])
                ins.then_inc(turned, 1)
                pe.wait_ge(gt_ready, 1)
                with pe.Fori(0, U // SLOTS) as i:
                    for s in range(SLOTS):
                        pe.wait_ge(m.low, i * SLOTS + low_count(first + s))
                        pe.wait_ge(m.bank_free[s], i + (fill0 + 1))
                        part_products(m, m.bank[s][:, :], s, DC, n_hi(m), n_lo(m), True, True).then_inc(m.used, 1)
                        for b in range(BATCHES):
                            k = s * BATCHES + b
                            pe.wait_ge(rows_ready, i * (SLOTS * BATCHES) + k + 1)
                            pe.wait_ge(evac, i * (SLOTS * BATCHES) + k + 1)
                            for u in range(BATCH):
                                ins = nc.tensor.matmul(m.bank[4 + b][:, u * P:(u + 1) * P],
                                                       rows2[:, b % 2, u * P:(u + 1) * P],
                                                       rows1[:, b % 2, u * P:(u + 1) * P], start=(u == 0),
                                                       stop=(u == BATCH - 1), skip_group_check=True)
                            ins.then_inc(done, 1)

            @block.scalar
            def _(act):
                e = found[:, :, 2 * P:3 * P]
                nc.scalar.activation(e, e, ACT.Exp).then_inc(expd, 1)
                act.wait_ge(turned, 1)
                for w in range(3):
                    ins = nc.scalar.activation(gt[:, w, :], m.bank[4 + w][:, :], ACT.Copy)
                ins.then_inc(gt_ready, 1)
                with act.Fori(0, U // SLOTS // 2) as i:
                    for r in range(2):
                        act.wait_ge(gate_stored[r], i * 16 + 16)
                        for s in range(SLOTS):
                            activate(m, act, buffers, i * 2 + (turn0 + r), s, turn0 - U0 // SLOTS, activated, stored)
                            for b in range(BATCHES):
                                k = s * BATCHES + b
                                act.wait_ge(done, i * (2 * SLOTS * BATCHES) + (r * SLOTS * BATCHES + k + 3))
                                out = stage[r][:, :, k * BATCH:(k + 1) * BATCH]
                                nc.scalar.activation(out.rearrange("p a t -> p t a"),
                                                     m.bank[4 + b][:, :].rearrange("p (t a) -> p t a", t=BATCH),
                                                     ACT.Copy).then_inc(evac, 1)

            @block.sync
            def _(sp):
                with sp.Fori(0, U // SLOTS // 2) as i:
                    for r in range(2):
                        for s in range(SLOTS):
                            k = r * SLOTS + s
                            load_panel(m, sp, i * (2 * SLOTS) + (first + SLOTS + k), s,
                                       panel(io["experts"], i * (2 * SLOTS) + (U0 + SLOTS + k)))
                            sp.wait_ge(activated, i * (2 * SLOTS) + (U0 + k + 1))
                            sp.dma_start(panel(io["parked"], i * (2 * SLOTS) + (U0 + k), T), buffers[:, s, :])\
                              .then_inc(stored[s], 16)
                        sp.wait_ge(evac, i * (2 * SLOTS * BATCHES) + (r + 1) * SLOTS * BATCHES + BATCHES)
                        sp.dma_start(G[:, :, bass.ds(i * 2 + r, 1), :].rearrange("p g o n -> p (g o) n"),
                                     stage[r].rearrange("p (g j) t -> p g (j t)", g=EXPERT_GROUPS))\
                          .then_inc(gate_stored[r], 16)
                for s in range(SLOTS):
                    sp.wait_ge(stored[s], 16 + 16 * (U0 + U) // SLOTS)
                for r in range(2):
                    sp.wait_ge(gate_stored[r], 16 + 16 * (U // SLOTS // 2))
    m.panels += U
    m.fills += U


def parked_experts(m, io):
    nc = m.nc
    E = EXPERT_GROUP
    U = LATE_GROUPS * E
    U0 = (PARKED - LATE_GROUPS) * E
    u_first, u_turn = m.panels, (m.panels - U0) // SLOTS
    first, turn0, fill0 = m.panels + U, (m.panels + U) // SLOTS, (m.fills + U) // SLOTS
    N = PARKED * E
    activated = m.sem("parked_activated")
    stored = [m.sem(f"parked_stored{s}") for s in range(SLOTS)]
    fetched = m.sem("parked_fetched")
    product = m.sem("parked_products")
    high = m.sem("parked_high")
    gated = m.sem("parked_gated")
    with ExitStack() as ctx:
        space = Space(m, ctx, "parked", 2 * E * T + (2 + SLOTS) * T)
        gates = space.take(T // SPREAD_T, E * SPREAD_T)
        value = space.take(E, T)
        tmp = space.take(2, T)
        buffers = space.take(SLOTS, T)
        hi = [m.tensor(f"parked_high{h}", E, T, dt=FR, ctx=ctx) for h in range(2)]
        lo = [m.tensor(f"parked_low{h}", E, T, dt=FR, ctx=ctx) for h in range(2)]
        by_token = gates.rearrange("p n (j t) -> p n j t", j=E)

        def gate(dve, g, h, c):
            nc.vector.tensor_tensor(tmp[:, c % 2, :].rearrange("p (n t) -> p n t", t=SPREAD_T),
                                    value[:, c, :].rearrange("p (n t) -> p n t", t=SPREAD_T),
                                    by_token[:, :, c, :], ALU.mult).then_inc(product, 1)
            dve.wait_ge(product, g * E + (c + 1))
            nc.vector.tensor_copy(hi[h][:, c, :], tmp[:, c % 2, :]).then_inc(high, 1)
            dve.wait_ge(high, g * E + (c + 1))
            nc.vector.tensor_tensor(lo[h][:, c, :], tmp[:, c % 2, :], hi[h][:, c, :].bitcast(FP), ALU.subtract)\
              .then_inc(gated, 1)

        with nc.Block() as block:
            @block.sync
            def _(sp):
                def fetch(g):
                    sp.wait_ge(gated, g * E + E)
                    sp.dma_start(gates, io["gates"][bass.ds(g, 1)].rearrange("o p n t -> p (o n) t")).then_inc(fetched, 16)
                    sp.dma_start(value, io["parked"][bass.ds(g * E, E)].rearrange("a p t -> p a t")).then_inc(fetched, 16)

                def load(g):
                    for c in range(E):
                        load_panel(m, sp, g * E + (first + SLOTS + c), c % SLOTS, panel(io["experts"], g * E + (N + SLOTS + c)))

                fetch(0)
                for k in range(U):
                    load_panel(m, sp, u_first + SLOTS + k, k % SLOTS, panel(io["experts"], U0 + SLOTS + k))
                    sp.wait_ge(activated, U0 + k + 1)
                    sp.dma_start(panel(io["parked"], U0 + k, T), buffers[:, k % SLOTS, :]).then_inc(stored[k % SLOTS], 16)
                for s in range(SLOTS):
                    sp.wait_ge(stored[s], 16 + 16 * (U0 + U) // SLOTS)
                with sp.Fori(0, PARKED - 1) as g:
                    fetch(g + 1)
                    load(g)
                load(PARKED - 1)

            @block.gpsimd
            def _(pool):
                split_low(m, pool, U + N)

            @block.scalar
            def _(act):
                for k in range(U):
                    activate(m, act, buffers, (u_first + k) // SLOTS, k % SLOTS, u_turn, activated, stored)
                with act.Fori(0, PARKED) as g:
                    for c in range(E):
                        split_next(m, act, g * 2 + (turn0 + c // SLOTS), c % SLOTS)

            @block.tensor
            def _(pe):
                panel_products(m, pe, U)

                def group(g, h):
                    pe.wait_ge(gated, g * E + 2 * E)
                    for c in range(E):
                        s = c % SLOTS
                        pe.wait_ge(m.low, g * E + low_count(first + c))
                        pe.wait_ge(m.bank_free[s], g * 2 + (fill0 + c // SLOTS + 1))
                        part_products(m, m.bank[s][:, :], s, E, lambda k: hi[h][:, k, :], lambda k: lo[h][:, k, :],
                                      True, True).then_inc(m.used, 1)
                with pe.Fori(0, PARKED // 2) as i:
                    for h in range(2):
                        group(i * 2 + h, h)

            @block.vector
            def _(dve):
                def add(g, c):
                    dve.wait_ge(m.used, g * E + used_count(first + c))
                    nc.vector.tensor_tensor(m.x[:, c, :], m.x[:, c, :], m.bank[c % SLOTS][:, :], ALU.add)\
                      .then_inc(m.bank_free[c % SLOTS], 1)

                dve.sem_inc(gated, E)
                dve.wait_ge(fetched, 32)
                for c in range(E):
                    gate(dve, 0, 0, c)

                def turn(g, h, fetches):
                    dve.wait_ge(fetched, fetches)
                    for c in range(E):
                        gate(dve, g + 1, 1 - h, c)
                        add(g, c)

                with dve.Fori(0, PARKED // 2 - 1) as i:
                    for h in range(2):
                        turn(i * 2 + h, h, i * 64 + 32 * (h + 2))
                turn(PARKED - 2, 0, 32 * PARKED)
                for c in range(E):
                    add(PARKED - 1, c)
    m.panels += U + N
    m.fills += U + N


def experts(m, io, ahead):
    nc = m.nc
    E = EXPERT_GROUP
    GROUPS = EXPERT_GROUPS - PARKED
    first, turn0, fill0 = m.panels, m.panels // SLOTS, m.fills // SLOTS
    START = 2 * PARKED * E
    ROUND = 2 * E // SLOTS
    fetched = m.sem("expert_gates_fetched")
    activated = m.sem("expert_activated")
    product = m.sem("expert_products")
    high = m.sem("expert_high")
    gated = m.sem("expert_gated")
    with ExitStack() as ctx:
        space = Space(m, ctx, "experts", E * T + (SLOTS + 2) * T)
        gates = space.take(T // SPREAD_T, E * SPREAD_T)
        buffers = space.take(SLOTS, T)
        tmp = space.take(2, T)
        hi = m.tensor("expert_high", E, T, dt=FR, ctx=ctx)
        lo = m.tensor("expert_low", E, T, dt=FR, ctx=ctx)
        by_token = gates.rearrange("p n (j t) -> p n j t", j=E)
        with nc.Block() as block:
            @block.sync
            def _(sp):
                def fetch(g):
                    sp.wait_ge(gated, g * E + E)
                    sp.dma_start(gates, io["gates"][bass.ds(g + PARKED, 1)].rearrange("o p n t -> p (o n) t"))\
                      .then_inc(fetched, 16)
                with sp.Fori(0, GROUPS - 1) as g:
                    fetch(g)
                    for k in range(2 * E):
                        load_panel(m, sp, g * (2 * E) + (first + SLOTS + k), k % SLOTS,
                                   panel(io["experts"], g * (2 * E) + (START + SLOTS + k)))
                fetch(GROUPS - 1)
                g = GROUPS - 1
                for k in range(2 * E):
                    p = g * 2 * E + SLOTS + k
                    if k < 2 * E - SLOTS:
                        load_panel(m, sp, first + p, k % SLOTS, panel(io["experts"], START + p))
                    else:
                        source, width = ahead[k - 2 * E + SLOTS]
                        load_panel(m, sp, first + p, k % SLOTS, source, width)

            @block.gpsimd
            def _(pool):
                split_low(m, pool, GROUPS * 2 * E)

            @block.tensor
            def _(pe):
                with pe.Fori(0, GROUPS) as g:
                    for k in range(2 * E):
                        s = k % SLOTS
                        pe.wait_ge(m.low, g * (2 * E) + low_count(first + k))
                        pe.wait_ge(m.bank_free[s], g * ROUND + (fill0 + k // SLOTS + 1))
                        if k < E:
                            ins = part_products(m, m.bank[s][:, :], s, DC, n_hi(m), n_lo(m), True, True)
                        else:
                            if k == E:
                                pe.wait_ge(gated, g * E + 2 * E)
                            ins = part_products(m, m.bank[s][:, :], s, E, lambda c: hi[:, c, :], lambda c: lo[:, c, :],
                                                True, True)
                        ins.then_inc(m.used, 1)

            @block.scalar
            def _(act):
                with act.Fori(0, GROUPS) as g:
                    for k in range(2 * E):
                        s = k % SLOTS
                        split_next(m, act, g * ROUND + (turn0 + k // SLOTS), s)
                        if k < E:
                            act.wait_ge(m.used, g * (2 * E) + used_count(first + k))
                            act.wait_ge(gated, g * E + (k + E + 1 - SLOTS))
                            nc.scalar.activation(buffers[:, s, :], m.bank[s][:, :], ACT.Gelu_apprx_tanh)\
                              .then_inc(activated, 1)
                            act.wait_ge(activated, g * E + (k + 1))
                            act.sem_inc(m.bank_free[s], 1)

            @block.vector
            def _(dve):
                def group(g, last):
                    dve.wait_ge(fetched, g * 16 + 16)
                    dve.wait_ge(m.used, g * (2 * E) + used_count(first - 1))
                    for c in range(E):
                        dve.wait_ge(activated, g * E + (c + 1))
                        nc.vector.tensor_tensor(tmp[:, c % 2, :].rearrange("p (n t) -> p n t", t=SPREAD_T),
                                                buffers[:, c % SLOTS, :].rearrange("p (n t) -> p n t", t=SPREAD_T),
                                                by_token[:, :, c, :], ALU.mult).then_inc(product, 1)
                        dve.wait_ge(product, g * E + (c + 1))
                        nc.vector.tensor_copy(hi[:, c, :], tmp[:, c % 2, :]).then_inc(high, 1)
                        dve.wait_ge(high, g * E + (c + 1))
                        nc.vector.tensor_tensor(lo[:, c, :], tmp[:, c % 2, :], hi[:, c, :].bitcast(FP), ALU.subtract)\
                          .then_inc(gated, 1)
                    for c in range(DC):
                        dve.wait_ge(m.used, g * (2 * E) + used_count(first + E + c))
                        ins = nc.vector.tensor_tensor(m.x[:, c, :], m.x[:, c, :], m.bank[c % SLOTS][:, :], ALU.add)
                        if last:
                            m.vector_order.step(dve, ins)
                            dve.sem_inc(m.bank_free[c % SLOTS], 1)
                            add_squares(m, dve, c)
                        else:
                            ins.then_inc(m.bank_free[c % SLOTS], 1)

                dve.sem_inc(gated, E)
                with dve.Fori(0, GROUPS - 1) as g:
                    group(g, False)
                group(GROUPS - 1, True)
    m.panels += 2 * E * GROUPS
    m.fills += 2 * E * GROUPS


DOWN_WIDTHS = (8 * P, 8 * P, (FC - 16) * P)


def turns(eng, n, unrolled):
    if unrolled:
        yield from range(n)
    else:
        with eng.Fori(0, n) as i:
            yield i


def swiglu(m, gate_w, up_w, down_w, ahead):
    nc = m.nc
    run = m.panels
    first, turn0, fill0 = m.panels, m.panels // SLOTS, m.fills // SLOTS
    down, down_fill0 = first + 2 * FC, fill0 + 2 * FC // SLOTS
    DOWN = 3 * DC
    product = Count(m, "hidden_product", FC)
    high = Count(m, "hidden_high", FC)
    ready = Count(m, "hidden_ready", FC)
    with ExitStack() as ctx:
        sg = m.square
        hi = m.tensor(f"hidden_high{run}", FC, T, dt=FR, ctx=ctx)
        lo = m.tensor(f"hidden_low{run}", FC, T, dt=FR, ctx=ctx)
        at = lambda t, f: t[:, bass.ds(f, 1), :].rearrange("p o t -> p (o t)")
        with nc.Block() as block:
            @block.sync
            def _(sp):
                with sp.Fori(1, FC // 2) as i:
                    for s in range(SLOTS):
                        load_panel(m, sp, i * SLOTS + (first + s), s, panel((gate_w, up_w)[s % 2], i * 2 + s // 2))
                for k in range(DOWN):
                    c, part = divmod(k, 3)
                    load_panel(m, sp, down + k, k % SLOTS, panel(down_w, c, DOWN_WIDTHS[part], part * PANEL),
                               DOWN_WIDTHS[part])
                for s, (source, width) in enumerate(ahead):
                    load_panel(m, sp, down + DOWN + s, s, source, width)

            @block.gpsimd
            def _(pool):
                split_low(m, pool, 2 * FC)
                m.panels += 2 * FC
                split_low(m, pool, DOWN, DOWN_WIDTHS)
                m.panels -= 2 * FC

            @block.tensor
            def _(pe):
                panel_products(m, pe, 2 * FC)
                pe.wait_ge(ready.sem, ready.base + FC + 2)
                with pe.Fori(0, 2) as i:
                    for k in range(DOWN // 2):
                        b, part = divmod(k, 3)
                        pe.wait_ge(m.low, i * (DOWN // 2) + low_count(down + k))
                        if part == 0:
                            pe.wait_ge(m.bank_free[b], i + (down_fill0 + 1))
                        part_products(m, m.bank[b][:, :], k % SLOTS, DOWN_WIDTHS[part] // P,
                                      lambda c: hi[:, part * 8 + c, :], lambda c: lo[:, part * 8 + c, :],
                                      part == 0, part == 2).then_inc(m.used, 1)

            @block.scalar
            def _(act):
                with act.Fori(0, FC // 2) as i:
                    for s in range(SLOTS):
                        split_next(m, act, i + turn0, s)
                        if s % 2 == 0:
                            v = s // 2
                            act.wait_ge(m.used, i * SLOTS + used_count(first + s))
                            act.wait_ge(ready.sem, i * 2 + (ready.base + v + 1))
                            nc.scalar.activation(sg[:, v, :], m.bank[s][:, :], ACT.Silu).then_inc(m.bank_free[s], 1)
                for i in turns(act, 2, not ahead):
                    for k in range(DOWN // 2):
                        if ahead or (i, k) != (1, DOWN // 2 - 1):
                            split_next(m, act, i * 3 + (down // SLOTS + k // SLOTS), k % SLOTS, DOWN_WIDTHS[(k + 1) % 3])

            @block.vector
            def _(dve):
                with dve.Fori(0, FC // 2) as i:
                    for v in range(2):
                        f = i * 2 + v
                        dve.wait_ge(m.bank_free[2 * v], i + (fill0 + 2))
                        dve.wait_ge(m.used, i * SLOTS + used_count(first + 2 * v + 1))
                        nc.vector.tensor_tensor(sg[:, v, :], sg[:, v, :], m.bank[2 * v + 1][:, :], ALU.mult)\
                          .then_inc(product.sem, 1)
                        dve.wait_ge(product.sem, f + (product.base + 1))
                        dve.sem_inc(m.bank_free[2 * v + 1], 1)
                        nc.vector.tensor_copy(at(hi, f), sg[:, v, :]).then_inc(high.sem, 1)
                        dve.wait_ge(high.sem, f + (high.base + 1))
                        nc.vector.tensor_tensor(at(lo, f), sg[:, v, :], at(hi, f).bitcast(FP), ALU.subtract)\
                          .then_inc(ready.sem, 1)
                for c in range(DC):
                    dve.wait_ge(m.used, used_count(down + 3 * c + 2))
                    x = m.x[:, c, :]
                    m.vector_order.step(dve, nc.vector.scalar_tensor_tensor(
                        out=x, in0=m.bank[c % 4][:, :], scalar=0.5, in1=x, op0=ALU.mult, op1=ALU.add))
                    dve.sem_inc(m.bank_free[c % 4], 1)
                    if ahead:
                        add_squares(m, dve, c)
    m.panels = down + DOWN
    m.fills += 2 * FC + DC


def head_rms(m, src, dst, gain, chunks, width, scratch):
    nc = m.nc
    sq = scratch.cut(0, 4, width)
    root = scratch.cut(4 * width, 4, width)
    squared = Count(m, "head_squared", chunks)
    summed = Count(m, "head_summed", chunks)
    rooted = Count(m, "head_rooted", chunks)
    scaled = Count(m, "head_scaled", chunks)
    with nc.Block() as block:
        @block.scalar
        def _(act):
            def roots(c):
                act.wait_ge(summed.sem, summed.base + c + 1)
                nc.scalar.activation(root[:, c % 4, :], m.bank[4 + c % 4][:, 0:width], ACT.Sqrt, bias=m.eps,
                                     scale=1.0 / HD).then_inc(rooted.sem, 1)
            for c in range(chunks):
                if c >= 4:
                    act.wait_ge(scaled.sem, scaled.base + c - 3)
                nc.scalar.activation(sq[:, c % 4, :], src(c), ACT.Square).then_inc(squared.sem, 1)
                if c >= 1:
                    roots(c - 1)
            roots(chunks - 1)

        @block.tensor
        def _(pe):
            for c in range(chunks):
                pe.wait_ge(squared.sem, squared.base + c + 1)
                if c >= 4:
                    pe.wait_ge(rooted.sem, rooted.base + c - 3)
                nc.tensor.matmul(m.bank[4 + c % 4][:, 0:width], m.const[:, BLOCK:BLOCK + P], sq[:, c % 4, :],
                                 start=True, stop=True).then_inc(summed.sem, 1)

        @block.vector
        def _(dve):
            for c in range(chunks):
                dve.wait_ge(rooted.sem, rooted.base + c + 1)
                m.vector_order.step(dve, nc.vector.reciprocal(root[:, c % 4, :], root[:, c % 4, :]))
                nc.vector.scalar_tensor_tensor(out=dst(c), in0=src(c), scalar=gain(c), in1=root[:, c % 4, :],
                                               op0=ALU.mult, op1=ALU.mult).then_inc(scaled.sem, 1)


def memory_keys_values(m, io, contexts):
    nc = m.nc
    kept = [Space(m, ctx, "memory", 4 * MEM_T) for ctx in reversed(contexts)][::-1]
    keys = [space.take(2, MEM_T) for space in kept]
    values = [space.take(2, MEM_T) for space in kept]
    mem_loaded = m.sem("memory_loaded")
    w_loaded = [m.sem(f"memory_weights_loaded{i}") for i in range(LAYERS)]
    again = m.sem("memory_scaled")
    done = m.sem("memory_products")
    read = m.sem("memory_read")
    with ExitStack() as own:
        scratch = Space(m, own, "memory_norm", 10 * MEM_T)
        space = Space(m, own, "memory_inputs", (1 + LAYERS) * DC * MEM_T + LAYERS * DC * 2 * MEM_HEADS * HD)
        mem = space.take(DC, MEM_T)
        normed = [space.take(DC, MEM_T) for _ in range(LAYERS)]
        w = [space.take(DC, 2 * MEM_HEADS * HD) for _ in range(LAYERS)]
        with nc.Block() as block:
            @block.sync
            def _(sp):
                sp.dma_start(mem, io["mem"]).then_inc(mem_loaded, 16)
                for i in range(LAYERS):
                    sp.dma_start(w[i], io["w_mem_kv"][i]).then_inc(w_loaded[i], 16)
                sp.wait_ge(mem_loaded, 16)
        rms(m, lambda c: mem[:, c, :], lambda c: normed[0][:, c, :], lambda c: m.v("mem_g", c), DC, MEM_T, scratch)
        inv = scratch.cut(9 * MEM_T, MEM_T)
        with nc.Block() as block:
            @block.vector
            def _(dve):
                for c in range(DC):
                    nc.vector.scalar_tensor_tensor(out=normed[1][:, c, :], in0=mem[:, c, :], scalar=m.v("mem_g", DC + c),
                                                   in1=inv, op0=ALU.mult, op1=ALU.mult).then_inc(again, 1)

            @block.tensor
            def _(pe):
                for i in range(LAYERS):
                    pe.wait_ge(w_loaded[i], 16)
                    if i:
                        pe.wait_ge(again, DC)
                    for j in range(4):
                        if i:
                            pe.wait_ge(read, j + 1)
                        for c in range(DC):
                            if j < 2:
                                lhs, rhs = w[i][:, c, j * P:(j + 1) * P], normed[i][:, c, :]
                            else:
                                lhs, rhs = normed[i][:, c, (j - 2) * P:(j - 1) * P], w[i][:, c, 2 * P:4 * P]
                            ins = nc.tensor.matmul(m.bank[4 + j][:, 0:MEM_T], lhs, rhs, start=(c == 0), stop=(c == DC - 1))
                        ins.then_inc(done, 1)

            @block.scalar
            def _(act):
                for k in range(4 * LAYERS):
                    i, j = divmod(k, 4)
                    act.wait_ge(done, k + 1)
                    dst = keys[i][:, j, :] if j < 2 else values[i][:, j - 2, :]
                    nc.scalar.activation(dst, m.bank[4 + j][:, 0:MEM_T], ACT.Copy).then_inc(read, 1)
        head_rms(m, lambda c: keys[c // 2][:, c % 2, :], lambda c: keys[c // 2][:, c % 2, :],
                 lambda c: m.v("mem_k", c // 2), 2 * LAYERS, MEM_T, scratch)
    return list(zip(keys, values))


class Head:

    def __init__(self, q, k, value, span, bias, group, chunk, off):
        self.q, self.k, self.value, self.span = q, k, value, span
        self.bias, self.group, self.chunk, self.off = bias, group, chunk, off


def memory_heads(q, memory, first_group, first_chunk):
    keys, values = memory
    heads = []
    for h in range(MEM_HEADS):
        c, off = h // 2, HD * (h % 2)
        heads.append(Head(q=lambda t, c=c, off=off: q[off:off + HD, c, t * P:(t + 1) * P],
                          k=lambda a, b, c=c, off=off: keys[off:off + HD, c, a * P:b * P],
                          value=lambda s, h=h: values[:, s, h * HD:(h + 1) * HD],
                          span=lambda t: (0, MEM_T // P), bias=None, group=first_group + h,
                          chunk=first_chunk + c, off=off))
    return heads


def attention(m, heads, groups, space):
    nc = m.nc
    H = len(heads)
    s = space.take(H, T)
    pt = space.take(4, T)
    top, negtop = space.take(H), space.take(groups)
    den, inv = space.take(H), space.take(groups)
    N = TT * H
    s_done = Count(m, "att_scores_done", N)
    s_read = Count(m, "att_scores_read", N)
    top_ready = Count(m, "att_top_ready", TT)
    exp_done = Count(m, "att_exp_done", TT)
    p_ready = Count(m, "att_weights_ready", N)
    turned = Count(m, "att_weights_turned", N)
    pt_ready = Count(m, "att_turned_read", N)
    v_done = Count(m, "att_values_done", N // 2)
    v_high = Count(m, "att_values_high", N // 2)
    v_read = Count(m, "att_values_read", N // 2)
    members = [[h for h in range(H) if heads[h].group == g] for g in range(groups)]
    shared = [g for g in range(groups) if len(members[g]) > 1]
    for g in shared:
        assert members[g] == [g + len(shared) * i for i in range(len(members[g]))]
    with nc.Block() as block:
        @block.tensor
        def _(pe):
            def product(t, h):
                head, g = heads[h], t * H + h
                lo, hi = head.span(t)
                pair = g // 2
                out = m.bank[6 + pair % 2][head.off:head.off + HD, 0:P]
                pe.wait_ge(pt_ready.sem, pt_ready.base + g + 1)
                if head.off == 0 and pair >= 2:
                    pe.wait_ge(v_read.sem, v_read.base + pair - 1)
                for j in range(lo, hi):
                    ins = nc.tensor.matmul(out, head.value(j), pt[:, g % 4, (j - lo) * P:(j - lo + 1) * P],
                                           start=(j == lo), stop=(j == hi - 1))
                if head.off:
                    ins.then_inc(v_done.sem, 1)

            for t in range(TT):
                for h in range(H):
                    head, g = heads[h], t * H + h
                    lo, hi = head.span(t)
                    if g >= 4:
                        pe.wait_ge(s_read.sem, s_read.base + g - 3)
                    nc.tensor.matmul(m.bank[g % 4][:, 0:(hi - lo) * P], head.q(t), head.k(lo, hi),
                                     start=True, stop=True).then_inc(s_done.sem, 1)
                for h in range(H):
                    head, g = heads[h], t * H + h
                    lo, hi = head.span(t)
                    pe.wait_ge(p_ready.sem, p_ready.base + g + 1)
                    if g >= 2:
                        pe.wait_ge(pt_ready.sem, pt_ready.base + g - 1)
                    for j in range(hi - lo):
                        ins = nc.tensor.transpose(m.bank[4 + g % 2][:, j * P:(j + 1) * P],
                                                  s[:, h, j * P:(j + 1) * P], m.const[:, IDENT:IDENT + P])
                    ins.then_inc(turned.sem, 1)
                    if h:
                        product(t, h - 1)
                product(t, H - 1)

        @block.vector
        def _(dve):
            order = m.vector_order
            for t in range(TT):
                for h in range(H):
                    head, g = heads[h], t * H + h
                    lo, hi = head.span(t)
                    dst, src = s[:, h, 0:(hi - lo) * P], m.bank[g % 4][:, 0:(hi - lo) * P]
                    dve.wait_ge(s_done.sem, s_done.base + g + 1)
                    if t:
                        dve.wait_ge(turned.sem, turned.base + g - H + 1)
                    if head.bias is None:
                        ins = nc.vector.tensor_scalar(dst, src, ATT_SCALE, None, ALU.mult)
                    else:
                        ins = nc.vector.scalar_tensor_tensor(out=dst, in0=src, scalar=ATT_SCALE, in1=head.bias(t),
                                                             op0=ALU.mult, op1=ALU.add)
                    ins.then_inc(s_read.sem, 1)
                dve.wait_ge(s_read.sem, s_read.base + (t + 1) * H)
                for h in range(H):
                    lo, hi = heads[h].span(t)
                    ins = nc.vector.reduce_max(top[:, h:h + 1], s[:, h, 0:(hi - lo) * P], AX)
                order.step(dve, ins)
                G, S = len(shared), len(members[0])
                if G:
                    for i in range(1, S):
                        order.step(dve, nc.vector.tensor_tensor(top[:, 0:G], top[:, 0:G], top[:, i * G:(i + 1) * G], ALU.max))
                    nc.vector.tensor_scalar(negtop[:, 0:G], top[:, 0:G], -1.0, None, ALU.mult)
                order.step(dve, nc.vector.tensor_scalar(negtop[:, G:groups], top[:, H - groups + G:H], -1.0, None, ALU.mult))
                dve.sem_inc(top_ready.sem, 1)
                dve.wait_ge(exp_done.sem, exp_done.base + t + 1)
                if G:
                    for i in range(1, S):
                        order.step(dve, nc.vector.tensor_tensor(den[:, 0:G], den[:, 0:G], den[:, i * G:(i + 1) * G], ALU.add))
                    nc.vector.reciprocal(inv[:, 0:G], den[:, 0:G])
                order.step(dve, nc.vector.reciprocal(inv[:, G:groups], den[:, H - groups + G:H]))
                for h in range(H):
                    lo, hi = heads[h].span(t)
                    w = s[:, h, 0:(hi - lo) * P]
                    nc.vector.tensor_scalar(w, w, inv[:, heads[h].group:heads[h].group + 1], None, ALU.mult)\
                      .then_inc(p_ready.sem, 1)
                for h in range(1, H, 2):
                    pair = (t * H + h) // 2
                    place = slice(t * P, (t + 1) * P)
                    dve.wait_ge(v_high.sem, v_high.base + pair + 1)
                    nc.vector.tensor_tensor(m.n_lo[:, heads[h].chunk, place], m.bank[6 + pair % 2][:, 0:P],
                                            m.n_hi[:, heads[h].chunk, place].bitcast(FP), ALU.subtract)\
                      .then_inc(v_read.sem, 1)

        @block.scalar
        def _(act):
            def values(act, t, h):
                pair = (t * H + h) // 2
                act.wait_ge(v_done.sem, v_done.base + pair + 1)
                nc.scalar.activation(m.n_hi[:, heads[h].chunk, t * P:(t + 1) * P], m.bank[6 + pair % 2][:, 0:P],
                                     ACT.Copy).then_inc(v_high.sem, 1)

            for t in range(TT):
                act.wait_ge(top_ready.sem, top_ready.base + t + 1)
                for h in range(H):
                    lo, hi = heads[h].span(t)
                    w = s[:, h, 0:(hi - lo) * P]
                    ins = nc.scalar.activation(w, w, ACT.Exp, bias=negtop[:, heads[h].group:heads[h].group + 1],
                                               accum_out=den[:, h:h + 1])
                ins.then_inc(exp_done.sem, 1)
                for h in range(H):
                    head, g = heads[h], t * H + h
                    lo, hi = head.span(t)
                    act.wait_ge(turned.sem, turned.base + g + 1)
                    nc.scalar.activation(pt[:, g % 4, 0:(hi - lo) * P], m.bank[4 + g % 2][:, 0:(hi - lo) * P], ACT.Copy)\
                      .then_inc(pt_ready.sem, 1)
                    if h % 2 and h > 1:
                        values(act, t, h - 2)
                values(act, t, H - 1)



SECOND_SEL, SECOND_MASK = 0, ML_HEADS * P
SECOND_HOT = SECOND_MASK + P
SECOND_COLUMNS = SECOND_HOT + TOEP


def turn_values(m, pe, act, values_t, values, chunks, turned, read):
    for j in range(chunks):
        bank = m.bank[4 + j % 4]
        if pe:
            if j >= 4:
                pe.wait_ge(read, j - 3)
            for t in range(TT):
                ins = m.nc.tensor.transpose(bank[:, t * P:(t + 1) * P], values_t[:, j, t * P:(t + 1) * P],
                                            m.const[:, IDENT:IDENT + P])
            ins.then_inc(turned, 1)
        else:
            act.wait_ge(turned, j + 1)
            m.nc.scalar.activation(values[:, :, j * P:(j + 1) * P], bank[:, :].rearrange("p (t a) -> p t a", t=TT),
                                   ACT.Copy).then_inc(read, 1)


def mlstm_layer(m, io, memory, ahead):
    with ExitStack() as ctx:
        norm_x(m, "mix2_g", 0)
        mlstm_cell(m, io, memory, Space(m, ctx, "mlstm", 27888), panels_ahead(io["a_w_out"]))
    linear_add(m, io["a_w_out"], ahead)


def mlstm_cell(m, io, memory, space, ahead):
    nc = m.nc
    take = space.take
    PAD = T + 4
    QK = 2 * ML_CHUNKS
    C = ML_CHUNKS
    IN = QK + 2 * C + 4
    pq = take(QK, PAD)
    out_gate = take(C, T)
    qm = take(2, T)
    values_at = space.at
    values = take(TT, ML_W)
    qk_at = space.at
    qk = take(QK, T)
    rows = take(8, T)
    second = take(SECOND_HOT)
    values_t = take(C, T)
    w = space.cut(space.at - C * T, TT, T)
    neg_m = space.cut(space.at - 2 * T, T)
    diag = space.cut(space.at - T, TT, P)
    dn = take(T)
    ccol = take(TT, ML_HEADS)
    cell = space.cut(0, C, T)
    first = m.panels
    side = m.sem("ml_side_loaded")
    evac = m.sem("ml_evacuated")
    convolved = m.sem("ml_convolved")
    v_turned = m.sem("ml_values_turned")
    v_read = m.sem("ml_values_read")
    lnf = m.sem("ml_ln_ready")
    sums = m.sem("ml_sums_ready")
    R = ML_HEADS
    i_row, f_row, l_row, one_row, b_row, c_row, m_row, g_row = (rows[0:R, j, :] for j in range(8))
    with nc.Block() as block:
        @block.sync
        def _(sp):
            sp.dma_start(second, io["second"][:, 0:SECOND_HOT]).then_inc(side, 16)
            weight_panels(m, sp, io["a_w_in"], IN, ahead)
            sp.wait_ge(side, 16)

        @block.gpsimd
        def _(pool):
            split_low(m, pool, IN)

        @block.tensor
        def _(pe):
            panel_products(m, pe, IN)
            pe.wait_ge(evac, QK + C)
            turn_values(m, pe, None, values_t, values, C, v_turned, v_read)

        @block.scalar
        def _(act):
            order = m.scalar_order
            for j in range(IN):
                out = None
                if j < QK:
                    out, func = pq[:, j, 3:3 + T], ACT.Copy
                elif j < QK + C:
                    out, func = values_t[:, j - QK, :], ACT.Copy
                elif j < QK + 2 * C:
                    out, func = out_gate[:, j - QK - C, :], ACT.Sigmoid
                elif j < IN - 2:
                    out, func = qm[:, j - QK - 2 * C, :], ACT.Copy
                split_next(m, act, first // SLOTS + j // SLOTS, j % SLOTS)
                act.wait_ge(m.used, used_count(first + j))
                if out is not None:
                    ins = nc.scalar.activation(out, m.bank[j % 4][:, :], func)
                else:
                    at_v = VEC["gate_i" if j == IN - 2 else "gate_f"]
                    ins = nc.scalar.activation(i_row if j == IN - 2 else f_row, m.bank[j % 4][0:R, :], ACT.Identity,
                                               bias=m.vec[0:R, at_v:at_v + 1])
                order.step(act, ins)
                act.sem_inc(m.bank_free[j % 4], 1)
                act.sem_inc(evac, 1)
            order.step(act, nc.scalar.activation(l_row, f_row, ACT.Abs))
            order.step(act, nc.scalar.activation(l_row, l_row, ACT.Exp, scale=-1.0))
            nc.scalar.activation(l_row, l_row, ACT.Ln, bias=1.0).then_inc(lnf, 1)
            act.wait_ge(sums, 1)
            nc.scalar.activation(g_row, g_row, ACT.Exp, scale=-1.0)
            turn_values(m, None, act, values_t, values, C, v_turned, v_read)
            for j in range(QK):
                act.wait_ge(convolved, j // 4 + 1)
                nc.scalar.activation(qk[:, j, :], qk[:, j, :], ACT.Silu)

        @block.vector
        def _(dve):
            order, vec = m.vector_order, nc.vector
            vec.memset(one_row, 1.0)
            order.step(dve, vec.memset(pq[:, :, 0:3], 0.0))
            for b in range(QK // 4):
                dve.wait_ge(evac, 4 * b + 4)
                for tap in range(ML_TAPS):
                    for j in range(4 * b, 4 * b + 4):
                        src, tapw = pq[:, j, tap:tap + T], m.v("a_conv", tap * QK + j)
                        if tap == 0:
                            ins = vec.tensor_scalar(qk[:, j, :], src, tapw, None, ALU.mult)
                        else:
                            ins = vec.scalar_tensor_tensor(out=qk[:, j, :], in0=src, scalar=tapw, in1=qk[:, j, :],
                                                           op0=ALU.mult, op1=ALU.add)
                    if tap < ML_TAPS - 1:
                        order.step(dve, ins)
                ins.then_inc(convolved, 1)
            dve.wait_ge(lnf, 1)
            order.step(dve, vec.tensor_scalar(f_row, f_row, 0.0, None, ALU.min))
            order.step(dve, vec.tensor_tensor(l_row, f_row, l_row, ALU.subtract))
            order.step(dve, vec.tensor_tensor_scan(b_row, one_row, l_row, 0.0, ALU.mult, ALU.add))
            order.step(dve, vec.tensor_tensor(c_row, i_row, b_row, ALU.subtract))
            order.step(dve, vec.tensor_tensor_scan(m_row, one_row, c_row, 0.0, ALU.mult, ALU.max))
            vec.tensor_tensor(g_row, b_row, m_row, ALU.add).then_inc(sums, 1)
    m.panels += IN
    m.fills += IN

    spread = m.sem("ml_rows_spread")
    cols = m.sem("ml_columns_ready")
    scores = m.sem("ml_scores_done")
    negated = m.sem("ml_negated")
    exps = m.sem("ml_exp_done")
    weights = m.sem("ml_weights_ready")
    summed = m.sem("ml_cell_sums")
    absd = m.sem("ml_abs_ready")
    celled = m.sem("ml_cell_ready")
    sel = lambda h: second[0:R, h * P:(h + 1) * P]
    mask = second[:, SECOND_MASK:SECOND_MASK + P]
    COLS, GUARD, DEN = m.bank[7], m.bank[5], m.bank[4]
    NUM = (m.bank[6], m.bank[7])
    with nc.Block() as block:
        @block.tensor
        def _(pe):
            for sb in range(TT):
                ins = nc.tensor.transpose(COLS[:, sb * R:(sb + 1) * R], c_row[:, sb * P:(sb + 1) * P],
                                          m.const[0:R, IDENT:IDENT + R])
            ins.then_inc(cols, 1)
            for h in range(ML_HEADS):
                if h:
                    pe.wait_ge(celled, h)
                nc.tensor.matmul(NUM[0][:, :], sel(h), m_row, start=True, stop=True).then_inc(spread, 1)
                nc.tensor.matmul(GUARD[:, :], sel(h), g_row, start=True, stop=True)
                for sb in range(TT):
                    for i, (c, p0, n) in enumerate(ML_PIECES[h]):
                        ins = nc.tensor.matmul(m.bank[sb][:, 0:T - sb * P],
                                               qk[p0:p0 + n, ML_CHUNKS + c, sb * P:(sb + 1) * P],
                                               qk[p0:p0 + n, c, sb * P:T], start=(i == 0), stop=(i == 1))
                    ins.then_inc(scores, 1)
                pe.wait_ge(negated, h + 1)
                pe.wait_ge(cols, 2)
                for sb in range(TT):
                    pe.wait_ge(weights, h * TT + sb + 1)
                    for i, (c, p0, n) in enumerate(ML_PIECES[h]):
                        f0 = c * P + p0
                        nc.tensor.matmul(NUM[i][p0:p0 + n, sb * P:T], values[:, sb, f0:f0 + n], w[:, sb, 0:T - sb * P],
                                         start=(sb == 0), stop=(sb == TT - 1))
                    ins = nc.tensor.matmul(DEN[:, sb * P:T], m.const[:, ONES:ONES + P], w[:, sb, 0:T - sb * P],
                                           start=(sb == 0), stop=(sb == TT - 1))
                ins.then_inc(summed, 1)

        @block.scalar
        def _(act):
            act.wait_ge(cols, 1)
            m.scalar_order.step(act, nc.scalar.activation(ccol.rearrange("p s h -> p (s h)"), COLS[:, 0:TT * R], ACT.Copy))
            act.sem_inc(cols, 1)
            for h in range(ML_HEADS):
                act.wait_ge(negated, h + 1)
                for sb in range(TT):
                    bias = ccol[:, sb, h:h + 1]
                    ins = nc.scalar.activation(w[:, sb, 0:P], diag[:, sb, :], ACT.Exp, bias=bias)
                    if sb < TT - 1:
                        ins = nc.scalar.activation(w[:, sb, P:T - sb * P], neg_m[:, (sb + 1) * P:T], ACT.Exp, bias=bias)
                    ins.then_inc(exps, 1)
                act.wait_ge(summed, h + 1)
                nc.scalar.activation(dn, DEN[:, :], ACT.Abs).then_inc(absd, 1)

        @block.vector
        def _(dve):
            order, vec = m.vector_order, nc.vector
            for h in range(ML_HEADS):
                dve.wait_ge(spread, h + 1)
                order.step(dve, vec.tensor_scalar(neg_m, NUM[0][:, :], -1.0, None, ALU.mult))
                vec.tensor_tensor(diag, neg_m.rearrange("p (s t) -> p s t", s=TT),
                                  mask.unsqueeze(1).to_broadcast([P, TT, P]), ALU.add).then_inc(negated, 1)
                for sb in range(TT):
                    n = T - sb * P
                    dve.wait_ge(exps, h * TT + sb + 1)
                    dve.wait_ge(scores, h * TT + sb + 1)
                    vec.scalar_tensor_tensor(out=w[:, sb, 0:n], in0=m.bank[sb][:, 0:n], scalar=ML_HD ** -0.5,
                                             in1=w[:, sb, 0:n], op0=ALU.mult, op1=ALU.mult).then_inc(weights, 1)
                dve.wait_ge(absd, h + 1)
                order.step(dve, vec.tensor_tensor(dn, dn, GUARD[:, :], ALU.max))
                order.step(dve, vec.reciprocal(dn, dn))
                for i, (c, p0, n) in enumerate(ML_PIECES[h]):
                    ins = vec.tensor_tensor(cell[p0:p0 + n, c, :], NUM[i][p0:p0 + n, :], dn[p0:p0 + n, :], ALU.mult)
                ins.then_inc(celled, 1)

    sq = space.cut(C * T, C, T)
    squared = m.sem("ml_squared")
    total = m.sem("ml_norm_sums")
    rooted = m.sem("ml_norm_rooted")
    gated, high = Count(m, "ml_gated", C), Count(m, "ml_high", C)
    root = space.cut(qk_at, TT, T)
    tmp = space.cut(qk_at + TT * T, C, T)
    with nc.Block() as block:
        @block.scalar
        def _(act):
            for c in range(ML_CHUNKS):
                nc.scalar.activation(sq[:, c, :], cell[:, c, :], ACT.Square).then_inc(squared, 1)
            for h in range(ML_HEADS):
                act.wait_ge(total, h + 1)
                nc.scalar.activation(root[:, h, :], m.bank[h][:, :], ACT.Sqrt, bias=m.eps, scale=1.0 / ML_HD)\
                  .then_inc(rooted, 1)
            input_high(m, act, C, lambda c: tmp[:, c, :], 0, gated, high)

        @block.tensor
        def _(pe):
            for h in range(ML_HEADS):
                pe.wait_ge(squared, max(c for c, _, _ in ML_PIECES[h]) + 1)
                for i, (c, p0, n) in enumerate(ML_PIECES[h]):
                    ins = nc.tensor.matmul(m.bank[h][:, :], m.const[p0:p0 + n, ONES:ONES + P], sq[p0:p0 + n, c, :],
                                           start=(i == 0), stop=(i == 1))
                ins.then_inc(total, 1)

        @block.vector
        def _(dve):
            order, vec = m.vector_order, nc.vector
            for h in range(ML_HEADS):
                dve.wait_ge(rooted, h + 1)
                order.step(dve, vec.reciprocal(root[:, h, :], root[:, h, :]))
                for c, p0, n in ML_PIECES[h]:
                    g0 = VEC["a_h"] + c
                    ins = vec.scalar_tensor_tensor(out=cell[p0:p0 + n, c, :], in0=cell[p0:p0 + n, c, :],
                                                   scalar=m.vec[p0:p0 + n, g0:g0 + 1], in1=root[p0:p0 + n, h, :],
                                                   op0=ALU.mult, op1=ALU.mult)
            order.step(dve, ins)
            for c in range(C):
                vec.tensor_tensor(tmp[:, c, :], cell[:, c, :], out_gate[:, c, :], ALU.mult).then_inc(gated.sem, 1)
            input_low(m, dve, vec, range(1, C, 2), lambda c: tmp[:, c, :], 0, high)

        @block.gpsimd
        def _(pool):
            input_low(m, pool, nc.gpsimd, range(0, C, 2), lambda c: tmp[:, c, :], 0, high)

    head_rms(m, lambda c: qm[:, c, :], lambda c: qm[:, c, :], lambda c: m.v("mem_q", 0), 2, T, space)
    space.at = values_at
    attention(m, memory_heads(qm, memory, 0, C), MEM_HEADS, space)


def shared_keys_values(m, io, ahead, ctx):
    nc = m.nc
    K6 = DIL_W // P
    N = 2 * K6
    first = m.panels
    kept = Space(m, ctx, "shared", K6 * T + TT * DIL_W)
    keys, values = kept.take(K6, T), kept.take(TT, DIL_W)
    evac = m.sem("kv_evacuated")
    v_turned = m.sem("kv_values_turned")
    v_read = m.sem("kv_values_read")
    with ExitStack() as own:
        space = Space(m, own, "kv", 8 * T)
        values_t = space.cut(0, K6, T)
        with nc.Block() as block:
            @block.sync
            def _(sp):
                weight_panels(m, sp, io["w_kv"], N, ahead)

            @block.gpsimd
            def _(pool):
                split_low(m, pool, N)

            @block.tensor
            def _(pe):
                panel_products(m, pe, N)
                pe.wait_ge(evac, N)
                turn_values(m, pe, None, values_t, values, K6, v_turned, v_read)

            @block.scalar
            def _(act):
                for j in range(N):
                    out = keys[:, j, :] if j < K6 else values_t[:, j - K6, :]
                    split_next(m, act, first // SLOTS + j // SLOTS, j % SLOTS)
                    act.wait_ge(m.used, used_count(first + j))
                    m.scalar_order.step(act, nc.scalar.activation(out, m.bank[j % 4][:, :], ACT.Copy))
                    act.sem_inc(m.bank_free[j % 4], 1)
                    act.sem_inc(evac, 1)
                turn_values(m, None, act, values_t, values, K6, v_turned, v_read)
        m.panels += N
        m.fills += N
        head_rms(m, lambda c: keys[:, c, :], lambda c: keys[:, c, :], lambda c: m.v("kv_k"), K6, T, space)
    return keys, values


def dilated_layer(m, io, shared, memory, ahead):
    with ExitStack() as ctx:
        norm_x(m, "mix2_g", DC)
        space = Space(m, ctx, "dilated", (DC + DIL_HEADS) * T + (DIL_HEADS + MEM_HEADS) * T + 4 * T + 64)
        dilated_attention(m, io, shared, memory, space, panels_ahead(io["b_w_out"]))
    linear_add(m, io["b_w_out"], ahead)


def dilated_attention(m, io, shared, memory, space, ahead):
    nc = m.nc
    K6 = DIL_W // P
    keys, values = shared
    q = space.take(DC, T)
    bias = space.take(DIL_HEADS, T)
    hot = space.cut(space.at, TOEP)
    line = space.cut(space.at + TOEP, TOEP)
    table = space.cut(space.at + 2 * TOEP, DIL_HEADS)
    K = BUCKETS + len(DILATIONS)
    first = m.panels
    side = m.sem("dil_side_loaded")
    line_done = m.sem("dil_line_products")
    line_read = m.sem("dil_line_read")
    line_stored = m.sem("dil_line_stored")
    spread = m.sem("dil_bias_spread")
    scratch = io["bias_lines"]
    with nc.Block() as block:
        @block.sync
        def _(sp):
            sp.dma_start(hot[0:K, :], io["second"][0:K, SECOND_HOT:SECOND_COLUMNS]).then_inc(side, 16)
            sp.dma_start(table[0:K, :], io["rel_bias"]).then_inc(side, 16)
            weight_panels(m, sp, io["b_w_q"], DC, ahead)

        @block.tensor
        def _(pe):
            pe.wait_ge(side, 32)
            for j in range(2):
                nc.tensor.matmul(m.bank[4 + j][0:DIL_HEADS, 0:TOEP // 2], table[0:K, :],
                                 hot[0:K, j * TOEP // 2:(j + 1) * TOEP // 2], start=True, stop=True)\
                  .then_inc(line_done, 1)
            panel_products(m, pe, DC)

        @block.scalar
        def _(act):
            for j in range(2):
                act.wait_ge(line_done, j + 1)
                nc.scalar.activation(line[0:DIL_HEADS, j * TOEP // 2:(j + 1) * TOEP // 2],
                                     m.bank[4 + j][0:DIL_HEADS, 0:TOEP // 2], ACT.Copy).then_inc(line_read, 1)
            for j in range(DC):
                split_next(m, act, first // SLOTS + j // SLOTS, j % SLOTS)
                act.wait_ge(m.used, used_count(first + j))
                nc.scalar.activation(q[:, j, :], m.bank[j % 4][:, :], ACT.Copy).then_inc(m.bank_free[j % 4], 1)

        @block.gpsimd
        def _(pool):
            pool.wait_ge(line_read, 2)
            pool.dma_start(scratch, line[0:DIL_HEADS, :].unsqueeze(1).to_broadcast([DIL_HEADS, P, TOEP]))\
                .then_inc(line_stored, 16)
            split_low(m, pool, DC)
            pool.wait_ge(line_stored, 16)
            for h in range(DIL_HEADS):
                pool.dma_start(bias[:, h, :], bass.AP(scratch.tensor, h * P * TOEP + P - 1, [[TOEP - 1, P], [1, T]]))\
                    .then_inc(spread, 16)
            pool.wait_ge(spread, 16 * DIL_HEADS)
    m.panels += DC
    m.fills += DC
    gain = lambda c: m.v("b_q") if c < K6 else m.v("mem_q", 1)
    head_rms(m, lambda c: q[:, c, :], lambda c: q[:, c, :], gain, DC, T, Scratch(space, space.at))
    heads = []
    for h in range(DIL_HEADS):
        c, off, g = h // 2, HD * (h % 2), h // DIL_PER_GROUP
        span = (lambda t: (max(t - 1, 0), t + 1)) if g == 0 else (lambda t: (0, t + 1))
        heads.append(Head(
            q=lambda t, c=c, off=off: q[off:off + HD, c, t * P:(t + 1) * P],
            k=lambda a, b, c=c, off=off: keys[off:off + HD, c, a * P:b * P],
            value=lambda s, h=h: values[:, s, h * HD:(h + 1) * HD], span=span,
            bias=lambda t, h=h, span=span: bias[:, h, (TT - 1 - t + span(t)[0]) * P:T],
            group=h % DIL_PER_GROUP, chunk=c, off=off))
    heads += memory_heads(q[:, K6:DC, :], memory, DIL_PER_GROUP, K6)
    attention(m, heads, DIL_PER_GROUP + MEM_HEADS, space)


def store(m, io):
    stored = m.sem("result_stored")
    with m.nc.Block() as block:
        @block.sync
        def _(sp):
            sp.dma_start(io["out"], m.x[:, :, :]).then_inc(stored, 16)
            sp.wait_ge(stored, 16)


def swiglu_ahead(io, which, layer):
    return [(panel(io[f"ffn{which}_{('gate', 'up')[s % 2]}"], layer * FC + s // 2), PANEL) for s in range(SLOTS)]


def first_block(m, io, ahead):
    norm_x(m, "mix_g")
    hybrid_mixer(m, io, panels_ahead(io["w_q"]))
    norm_x(m, "ffn_g")
    product_key_experts(m, io, ahead)
    norm_x(m, "final_g", dst=lambda c: m.x[:, c, :])


def product_key_experts(m, io, ahead):
    with ExitStack() as ctx:
        found = m.tensor("found_experts", TT, 3 * HEADS * TOPK, ctx=ctx)
        route(m, io, found)
        spread_gates(m, io, found)
    parked_experts(m, io)
    experts(m, io, ahead)


def feed_forward(m, io, which, layer, ahead):
    norm_x(m, f"ffn{which}_g", layer * DC)
    swiglu(m, io[f"ffn{which}_gate"][layer * FC:(layer + 1) * FC], io[f"ffn{which}_up"][layer * FC:(layer + 1) * FC],
           io[f"ffn{which}_down"][layer * DC:(layer + 1) * DC], ahead)


def second_block(m, io):
    feed_forward(m, io, 1, 0, panels_ahead(io["a_w_in"]))
    with ExitStack() as both:
        with ExitStack() as first:
            memory = memory_keys_values(m, io, (first, both))
            mlstm_layer(m, io, memory[0], swiglu_ahead(io, 2, 0))
        feed_forward(m, io, 2, 0, panels_ahead(io["w_kv"]))
        dilated_half(m, io, memory[1])
    feed_forward(m, io, 2, 1, ())


def dilated_half(m, io, memory):
    with ExitStack() as ctx:
        norm_x(m, "kv_g")
        shared = shared_keys_values(m, io, swiglu_ahead(io, 1, 1), ctx)
        feed_forward(m, io, 1, 1, panels_ahead(io["b_w_q"]))
        dilated_layer(m, io, shared, memory, swiglu_ahead(io, 2, 1))


def program(nc, io):
    with ExitStack() as ctx:
        m = Machine(nc, ctx)
        start(m, io, panels_ahead(io["w_in"]))
        first_block(m, io, swiglu_ahead(io, 1, 0))
        second_block(m, io)
        store(m, io)



def panels(w):
    k, n = w.shape
    return w.reshape(k // P, P, n // P, P).transpose(2, 1, 0, 3).reshape(n // P, P, k)


def by_chunk(w):
    k, n = w.shape
    return w.reshape(k // P, P, n).transpose(1, 0, 2)


def columns(v):
    return np.asarray(v, np.float32).reshape(-1, P).T


def constants():
    c = np.zeros((P, CONST_COLUMNS), np.float32)
    c[:, IDENT:IDENT + P] = np.eye(P)
    c[:, ONES:ONES + P] = 1
    for b in range(P // HD):
        c[b * HD:(b + 1) * HD, BLOCK + b * HD:BLOCK + (b + 1) * HD] = 1
    c[:, COUNT:COUNT + P] = np.arange(P)
    return c


def second_constants():
    c = np.zeros((P, SECOND_COLUMNS), np.float32)
    for h in range(ML_HEADS):
        c[h, SECOND_SEL + h * P:SECOND_SEL + (h + 1) * P] = 1
    s, t = np.arange(P)[:, None], np.arange(P)[None, :]
    c[:, SECOND_MASK:SECOND_MASK + P] = np.where(t >= s, 0, NEG)
    exact = BUCKETS // 2
    for y in range(TOEP):
        d = T - 1 - y
        if d < 0:
            c[BUCKETS:BUCKETS + len(DILATIONS), SECOND_HOT + y] = NEG
            continue
        f = np.float32(max(d, 1))
        large = exact + int(np.log(f / np.float32(exact)) / np.float32(np.log(MAX_DISTANCE / exact)) * np.float32(BUCKETS - exact))
        c[d if d < exact else min(large, BUCKETS - 1), SECOND_HOT + y] = 1
        for g, (window, dilation) in enumerate(DILATIONS):
            if d % dilation or d > window:
                c[BUCKETS + g, SECOND_HOT + y] = NEG
    return c


def layouts(a):
    f = {k: np.asarray(v) for k, v in a.items()}
    io = {"constants": constants(), "second": second_constants()}
    vec = np.zeros((P, VEC_COLUMNS), np.float32)

    def put(name, cols):
        vec[:cols.shape[0], VEC[name]:VEC[name] + cols.shape[1]] = cols

    for name, key in (("mix_g", "mix_norm_g"), ("ffn_g", "ffn_norm_g"), ("final_g", "final_norm_g"),
                      ("ffn1_g", "ffn1_norm_2"), ("ffn2_g", "ffn2_norm_2"), ("mix2_g", "mix_norm_2"),
                      ("mem_g", "mem_norm_2"), ("kv_g", "kv_norm_2"), ("lru_w", "lru_conv_w"),
                      ("lru_b", "lru_conv_b"), ("b_rg", "lru_b_rg"), ("b_ig", "lru_b_ig"),
                      ("lam", "lru_lambda"), ("conf_b", "conf_conv_b"), ("conf_g", "conf_norm_g"),
                      ("conf_nb", "conf_norm_b"), ("beta_lru", "beta_lru"), ("beta_conv", "beta_conv"),
                      ("a_conv", "a_conv_2"), ("a_h", "a_h_norm_2")):
        put(name, columns(f[key]))
    put("conf_w", f["conf_conv_w"][0].reshape(CONF_TAPS, LRU_C4, P).transpose(2, 1, 0).reshape(P, -1))
    for name, key in (("mem_q", "mem_q_norm_2"), ("mem_k", "mem_k_norm_2"), ("b_q", "b_q_norm_2"),
                      ("kv_k", "kv_k_norm_2")):
        g = f[key].reshape(-1, HD)
        put(name, np.concatenate([g, g], axis=1).T)
    put("gate_i", f["a_gate_bias_2"][0, :ML_HEADS].reshape(-1, 1))
    put("gate_f", f["a_gate_bias_2"][0, ML_HEADS:].reshape(-1, 1))
    io["vectors"] = vec
    io["x"] = f["x"][0].T.reshape(DC, P, T).transpose(1, 0, 2)
    io["w_in"] = panels(f["w_in"][0])
    io["w_out"] = panels(f["w_out"][0])
    gates = np.zeros((P, 4 * LRU_C4, P), np.float32)
    for way in range(2):
        for gate, key in enumerate(("lru_w_rg", "lru_w_ig")):
            for h in range(8):
                o = h % 2 * HD
                gates[o:o + HD, (way * 2 + gate) * LRU_C4 + h // 2, o:o + HD] = f[key][0, way, h]
    io["lru_gates"] = gates
    io["w_q"] = panels(f["peer_w_q"][0])
    io["keys"] = f["peer_sub_keys"][0].reshape(HP, KEYS, P).transpose(2, 0, 1)
    u = f["peer_u"][0].reshape(EXPERT_GROUPS, EXPERT_GROUP, P, DC, P).transpose(0, 1, 4, 3, 2)\
        .reshape(EXPERT_GROUPS, EXPERT_GROUP, P, PANEL)
    v = f["peer_v"][0].reshape(EXPERT_GROUPS, EXPERT_GROUP, P, DC, P).transpose(0, 3, 2, 1, 4)\
        .reshape(EXPERT_GROUPS, EXPERT_GROUP, P, PANEL)
    io["experts"] = np.concatenate([u[:PARKED].reshape(-1, P, PANEL), v[:PARKED].reshape(-1, P, PANEL),
                                    np.concatenate([u[PARKED:], v[PARKED:]], axis=1).reshape(-1, P, PANEL)])
    for which in (1, 2):
        for name in ("gate", "up", "down"):
            w = f[f"ffn{which}_w_{name}_2"]
            io[f"ffn{which}_{name}"] = np.concatenate([panels(w[0]), panels(w[1])])
    io["mem"] = f["mem_2"][0].T.reshape(DC, P, MEM_T).transpose(1, 0, 2)
    io["w_mem_kv"] = np.stack([by_chunk(w) for w in f["w_mem_kv_2"]])
    w = f["a_w_in_2"][0]
    g0 = 4 * ML_W
    m0 = g0 + 2 * ML_HEADS
    lone = np.zeros((D, P - ML_HEADS), np.float32)
    io["a_w_in"] = panels(np.concatenate([w[:, :g0], w[:, m0:], w[:, g0:g0 + ML_HEADS], lone,
                                          w[:, g0 + ML_HEADS:m0], lone], axis=1))
    io["a_w_out"] = panels(f["a_w_out_2"][0])
    io["w_kv"] = panels(f["w_kv_2"])
    io["b_w_q"] = panels(f["b_w_q_2"][0])
    io["b_w_out"] = panels(f["b_w_out_2"][0])
    pick = np.zeros((len(DILATIONS), DIL_HEADS), np.float32)
    for h in range(DIL_HEADS):
        pick[h // DIL_PER_GROUP, h] = 1
    io["rel_bias"] = np.concatenate([f["rel_bias_2"], pick])
    return {k: np.ascontiguousarray(v) for k, v in io.items()}


def build(nc, shapes):
    io = {}
    for name, (shape, dtype) in shapes.items():
        io[name] = nc.dram_tensor(f"in_{name}", shape, mybir.dt.from_np(dtype), kind="ExternalInput").ap()
    io["out"] = nc.dram_tensor("out", (P, DC, T), FP, kind="ExternalOutput").ap()
    io["gates"] = nc.dram_tensor("expert_gates", (EXPERT_GROUPS, P, T // SPREAD_T, EXPERT_GROUP * SPREAD_T), FP).ap()
    io["parked"] = nc.dram_tensor("parked_activations", (PARKED * EXPERT_GROUP, P, T), FP).ap()
    io["bias_lines"] = nc.dram_tensor("dilated_bias_lines", (DIL_HEADS, P, TOEP), FP).ap()
    program(nc, io)


def kernel(**inputs):
    import concourse.bacc as bacc
    from concourse.bass_utils import run_bass_kernel_spmd

    nc = bacc.Bacc("TRN2", target_bir_lowering=False, num_devices=1)
    arrays = layouts(inputs)
    build(nc, {k: (v.shape, v.dtype) for k, v in arrays.items()})
    r = run_bass_kernel_spmd(nc, [{f"in_{k}": v for k, v in arrays.items()}], core_ids=[0])
    out = r.results[0]["out"]
    return out.transpose(1, 0, 2).reshape(D, T).T.reshape(1, T, D)
```
